# Optimizing a Trainium2 kernel written in Bass

```python
import math
import jax, jax.numpy as jnp
from jax import lax
import numpy as np

D_MODEL = 1024
BATCH = 1
SEQ = 1024
DEPTH = 1
DEC_BATCH = 8
DEC_SEQ = 8
PAST_LEN = 2048
PAGE_SIZE = 128

H_ATT = 8
HEAD_DIM = 64
ATT_W = H_ATT * HEAD_DIM
IDX_HEADS = 4
IDX_DIM = 64
TOPK_MAX = 256
Q_BLOCK = 128
H_RET = 8
RET_DK = 64
RET_DV = 64
RET_W = H_RET * RET_DV
RET_CHUNK = 128
ROPE_BASE = 10000.0
NUM_BUCKETS = 32
MAX_DISTANCE = 1024
N_GROUPS = 4
EXPERTS_PER_GROUP = 8
N_EXPERTS = N_GROUPS * EXPERTS_PER_GROUP
TOP_EXPERTS = 2
D_EXPERT = 256
NORM_EPS = 1e-6
GN_EPS = 1e-5
IN_SIZES = (ATT_W, ATT_W, ATT_W, IDX_HEADS * IDX_DIM, IDX_DIM, IDX_HEADS,
            H_RET * RET_DK, H_RET * RET_DK, RET_W, RET_W)
N_IN = sum(IN_SIZES)

kernel_name = "hybrid_dsa_retention_hmoe_step"

def _rmsnorm(x, g):
    xf = x.astype(jnp.float32)
    y = xf * lax.rsqrt(jnp.mean(xf * xf, axis=-1, keepdims=True) + NORM_EPS)
    return (y * g.astype(jnp.float32)).astype(x.dtype)

def _rotary(x, pos):
    half = x.shape[-1] // 2
    inv = ROPE_BASE ** (-jnp.arange(half, dtype=jnp.float32) / half)
    ang = pos.astype(jnp.float32)[:, None] * inv[None, :]
    cos = jnp.cos(ang)[None, :, None, :]
    sin = jnp.sin(ang)[None, :, None, :]
    xf = x.astype(jnp.float32)
    x1, x2 = xf[..., :half], xf[..., half:]
    return jnp.concatenate([x1 * cos - x2 * sin, x1 * sin + x2 * cos], axis=-1)

def _rel_bucket(dist):
    n = jnp.maximum(dist, 0)
    max_exact = NUM_BUCKETS // 2
    nf = jnp.maximum(n, max_exact).astype(jnp.float32)
    large = max_exact + (jnp.log(nf / max_exact) / math.log(MAX_DISTANCE / max_exact)
                         * (NUM_BUCKETS - max_exact)).astype(jnp.int32)
    large = jnp.minimum(large, NUM_BUCKETS - 1)
    return jnp.where(n < max_exact, n, large)

def _take_rows(rows, idx):
    return jax.vmap(lambda r, i: r[i])(rows, idx)

def _project(u, w_in, q_g, k_g, pos):
    b, t, _ = u.shape
    z = u @ w_in
    splits = np.cumsum(IN_SIZES)[:-1].tolist()
    qa, ka, va, qi, ki, wi, qr, kr, vr, gr = jnp.split(z, splits, axis=-1)
    qa = _rmsnorm(qa.reshape(b, t, H_ATT, HEAD_DIM), q_g)
    ka = _rmsnorm(ka.reshape(b, t, H_ATT, HEAD_DIM), k_g)
    va = va.reshape(b, t, H_ATT, HEAD_DIM)
    qi = qi.reshape(b, t, IDX_HEADS, IDX_DIM)
    wi = wi * (IDX_HEADS ** -0.5)
    qr = _rotary(qr.reshape(b, t, H_RET, RET_DK), pos)
    kr = _rotary(kr.reshape(b, t, H_RET, RET_DK), pos) * (RET_DK ** -0.5)
    vr = vr.reshape(b, t, H_RET, RET_DV).astype(jnp.float32)
    return qa, ka, va, qi, ki, wi, qr, kr, vr, gr

def _index_topk(qi, wi, kidx, q_pos, k_top):
    s = jnp.einsum("bthd,bsd->bths", qi.astype(jnp.float32),
                   kidx.astype(jnp.float32)) * (IDX_DIM ** -0.5)
    score = jnp.einsum("bths,bth->bts", jax.nn.relu(s), wi.astype(jnp.float32))
    key_pos = jnp.arange(kidx.shape[1], dtype=jnp.int32)
    score = jnp.where(key_pos[None, None, :] <= q_pos[None, :, None], score, -jnp.inf)
    _, idx = lax.top_k(score, k_top)
    return idx.astype(jnp.int32)

def _attend_selected(q, kg, vg, idx, q_pos, rel_bias):
    logits = jnp.einsum("bthd,btkhd->bthk", q.astype(jnp.float32),
                        kg.astype(jnp.float32)) * (HEAD_DIM ** -0.5)
    bias = rel_bias[_rel_bucket(q_pos[None, :, None] - idx)]
    logits = logits + jnp.swapaxes(bias, -1, -2).astype(jnp.float32)
    valid = (idx <= q_pos[None, :, None])[:, :, None, :]
    p = jax.nn.softmax(jnp.where(valid, logits, -1e30), axis=-1)
    return jnp.einsum("bthk,btkhd->bthd", p, vg.astype(jnp.float32))

def _dsa_prompt(qa, ka, va, qi, ki, wi, pos, rel_bias, k_top):
    b, t = qa.shape[:2]
    nb = t // Q_BLOCK

    def to_blocks(a):
        return a.reshape((b, nb, Q_BLOCK) + a.shape[2:]).swapaxes(0, 1)

    def one_block(args):
        q_blk, qi_blk, wi_blk, pos_blk = args
        idx = _index_topk(qi_blk, wi_blk, ki, pos_blk, k_top)
        kg = _take_rows(ka, idx)
        vg = _take_rows(va, idx)
        return _attend_selected(q_blk, kg, vg, idx, pos_blk, rel_bias)

    out = lax.map(one_block, (to_blocks(qa), to_blocks(qi), to_blocks(wi),
                              pos.reshape(nb, Q_BLOCK)))
    return out.swapaxes(0, 1).reshape(b, t, H_ATT, HEAD_DIM)

def _dsa_sample(qa, ka, va, qi, ki, wi, pos, rel_bias, ck, cv, cki, page_table, k_top):
    db, t_new = qa.shape[:2]
    past = page_table.shape[1] * PAGE_SIZE
    kidx_past = cki[page_table].reshape(db, past, IDX_DIM)
    kidx_all = jnp.concatenate([kidx_past.astype(ki.dtype), ki], axis=1)
    idx = _index_topk(qi, wi, kidx_all, pos, k_top)
    is_past = (idx < past)[..., None, None]
    ip = jnp.minimum(idx, past - 1)
    phys = _take_rows(page_table, ip // PAGE_SIZE)
    off = ip % PAGE_SIZE
    inew = jnp.clip(idx - past, 0, t_new - 1)
    kg = jnp.where(is_past, ck[phys, off].astype(ka.dtype), _take_rows(ka, inew))
    vg = jnp.where(is_past, cv[phys, off].astype(va.dtype), _take_rows(va, inew))
    return _attend_selected(qa, kg, vg, idx, pos, rel_bias)

def _log_gamma():
    return jnp.log1p(-jnp.exp2(-5.0 - jnp.arange(H_RET, dtype=jnp.float32)))

def _retention_chunk(s0, q, k, v, lg):
    c = q.shape[1]
    j = jnp.arange(c, dtype=jnp.float32)
    decay_in = jnp.exp((j[:, None] + 1.0) * lg[None, :])
    rel = j[:, None] - j[None, :]
    dmat = jnp.where(rel[:, :, None] >= 0,
                     jnp.exp(jnp.maximum(rel, 0.0)[:, :, None] * lg), 0.0)
    dmat = jnp.transpose(dmat, (2, 0, 1))
    intra = jnp.einsum("bchd,bmhd->bhcm", q, k) * dmat[None]
    o = (jnp.einsum("bhcm,bmhe->bche", intra, v)
         + jnp.einsum("bchd,bhde->bche", q * decay_in[None, :, :, None], s0))
    decay_out = jnp.exp((c - 1.0 - j)[:, None] * lg[None, :])
    s_new = (s0 * jnp.exp(c * lg)[None, :, None, None]
             + jnp.einsum("bchd,bche->bhde", k * decay_out[None, :, :, None], v))
    return s_new, o

def _retention_prompt(qr, kr, vr):
    b, t = qr.shape[:2]
    nc = t // RET_CHUNK
    lg = _log_gamma()

    def to_chunks(a):
        return a.reshape((b, nc, RET_CHUNK) + a.shape[2:]).swapaxes(0, 1)

    s0 = jnp.zeros((b, H_RET, RET_DK, RET_DV), jnp.float32)
    s_fin, o = lax.scan(lambda s, xs: _retention_chunk(s, xs[0], xs[1], xs[2], lg),
                        s0, (to_chunks(qr), to_chunks(kr), to_chunks(vr)))
    return o.swapaxes(0, 1).reshape(b, t, H_RET, RET_DV), s_fin

def _merge(att, ret_o, gr, gn_g, gn_b, w_out, out_dtype):
    b, t = att.shape[:2]
    mu = jnp.mean(ret_o, axis=-1, keepdims=True)
    var = jnp.mean(jnp.square(ret_o - mu), axis=-1, keepdims=True)
    on = ((ret_o - mu) * lax.rsqrt(var + GN_EPS)).reshape(b, t, RET_W)
    on = on * gn_g.astype(jnp.float32) + gn_b.astype(jnp.float32)
    ret = jax.nn.silu(gr.astype(jnp.float32)) * on
    mix = jnp.concatenate([att.reshape(b, t, ATT_W), ret], axis=-1).astype(out_dtype)
    return mix @ w_out

def _hmoe(u, w_group, w_expert, w_gate, w_up, w_down):
    shape = u.shape
    uf = u.reshape(-1, D_MODEL)
    gp = jax.nn.softmax((uf @ w_group).astype(jnp.float32), axis=-1)
    p_top, g_top = lax.top_k(gp, 1)
    el = (uf @ w_expert).astype(jnp.float32).reshape(-1, N_GROUPS, EXPERTS_PER_GROUP)
    el_g = jnp.take_along_axis(el, g_top[:, :, None], axis=1)[:, 0, :]
    ep = jax.nn.softmax(el_g, axis=-1)
    e_val, e_idx = lax.top_k(ep, TOP_EXPERTS)
    e_val = e_val / jnp.sum(e_val, axis=-1, keepdims=True)
    within = jnp.sum(jax.nn.one_hot(e_idx, EXPERTS_PER_GROUP, dtype=jnp.float32)
                     * e_val[..., None], axis=1)
    combine = (jax.nn.one_hot(g_top[:, 0], N_GROUPS, dtype=jnp.float32)[:, :, None]
               * within[:, None, :] * p_top[:, :, None]).reshape(-1, N_EXPERTS)
    h = (jax.nn.silu(jnp.einsum("nd,edf->nef", uf, w_gate))
         * jnp.einsum("nd,edf->nef", uf, w_up))
    h = h * combine.astype(h.dtype)[:, :, None]
    y = jnp.einsum("nef,efd->nd", h, w_down)
    return y.reshape(shape).astype(u.dtype)

def setup_inputs(seed: int = 0) -> dict:
    key = jax.random.key(seed)
    ks = jax.random.split(key, 24)
    n_pages = PAST_LEN // PAGE_SIZE
    n_phys = (DEC_BATCH * n_pages * 5) // 4

    def nrm(k, shape, s=1.0):
        return s * jax.random.normal(k, shape, jnp.float32)

    perm = jax.random.permutation(ks[6], n_phys)
    page_table = perm[: DEC_BATCH * n_pages].reshape(DEC_BATCH, n_pages).astype(jnp.int32)
    return {
        "x_prompt": nrm(ks[0], (BATCH, SEQ, D_MODEL)),
        "x_sample": nrm(ks[1], (DEC_BATCH, DEC_SEQ, D_MODEL)),
        "cache_k": nrm(ks[2], (DEPTH, n_phys, PAGE_SIZE, H_ATT, HEAD_DIM)),
        "cache_v": nrm(ks[3], (DEPTH, n_phys, PAGE_SIZE, H_ATT, HEAD_DIM)),
        "cache_kidx": nrm(ks[4], (DEPTH, n_phys, PAGE_SIZE, IDX_DIM)),
        "state_ret": nrm(ks[5], (DEPTH, DEC_BATCH, H_RET, RET_DK, RET_DV), 0.5),
        "page_table": page_table,
        "rel_bias": nrm(ks[7], (NUM_BUCKETS, H_ATT), 0.5),
        "ln1_g": 1.0 + nrm(ks[8], (DEPTH, D_MODEL), 0.02),
        "w_in": nrm(ks[9], (DEPTH, D_MODEL, N_IN), D_MODEL ** -0.5),
        "q_norm_g": 1.0 + nrm(ks[10], (DEPTH, HEAD_DIM), 0.02),
        "k_norm_g": 1.0 + nrm(ks[11], (DEPTH, HEAD_DIM), 0.02),
        "ret_gn_g": 1.0 + nrm(ks[12], (DEPTH, RET_W), 0.02),
        "ret_gn_b": nrm(ks[13], (DEPTH, RET_W), 0.02),
        "w_out": nrm(ks[14], (DEPTH, ATT_W + RET_W, D_MODEL), (ATT_W + RET_W) ** -0.5),
        "ln2_g": 1.0 + nrm(ks[15], (DEPTH, D_MODEL), 0.02),
        "w_group": nrm(ks[16], (DEPTH, D_MODEL, N_GROUPS), D_MODEL ** -0.5),
        "w_expert": nrm(ks[17], (DEPTH, D_MODEL, N_EXPERTS), D_MODEL ** -0.5),
        "w_gate": nrm(ks[18], (DEPTH, N_EXPERTS, D_MODEL, D_EXPERT), D_MODEL ** -0.5),
        "w_up": nrm(ks[19], (DEPTH, N_EXPERTS, D_MODEL, D_EXPERT), D_MODEL ** -0.5),
        "w_down": nrm(ks[20], (DEPTH, N_EXPERTS, D_EXPERT, D_MODEL), D_EXPERT ** -0.5),
    }

def reference(x_prompt, x_sample, cache_k, cache_v, cache_kidx, state_ret, page_table,
              rel_bias, ln1_g, w_in, q_norm_g, k_norm_g, ret_gn_g, ret_gn_b, w_out,
              ln2_g, w_group, w_expert, w_gate, w_up, w_down):
    k_top_prompt = min(TOPK_MAX, SEQ // 4)
    k_top_sample = min(TOPK_MAX, (PAST_LEN + DEC_SEQ) // 4)
    pos_p = jnp.arange(SEQ, dtype=jnp.int32)
    pos_s = PAST_LEN + jnp.arange(DEC_SEQ, dtype=jnp.int32)
    lg = _log_gamma()
    hp, hs = x_prompt, x_sample
    kp_l, vp_l, ip_l, sp_l = [], [], [], []
    ks_l, vs_l, is_l, ss_l = [], [], [], []
    for l in range(DEPTH):
        u = _rmsnorm(hp, ln1_g[l])
        qa, ka, va, qi, ki, wi, qr, kr, vr, gr = _project(u, w_in[l], q_norm_g[l],
                                                          k_norm_g[l], pos_p)
        att = _dsa_prompt(qa, ka, va, qi, ki, wi, pos_p, rel_bias, k_top_prompt)
        ret_o, s_fin = _retention_prompt(qr, kr, vr)
        hp = hp + _merge(att, ret_o, gr, ret_gn_g[l], ret_gn_b[l], w_out[l], hp.dtype)
        hp = hp + _hmoe(_rmsnorm(hp, ln2_g[l]), w_group[l], w_expert[l],
                        w_gate[l], w_up[l], w_down[l])
        kp_l.append(ka)
        vp_l.append(va)
        ip_l.append(ki)
        sp_l.append(s_fin.astype(x_prompt.dtype))

        u = _rmsnorm(hs, ln1_g[l])
        qa, ka, va, qi, ki, wi, qr, kr, vr, gr = _project(u, w_in[l], q_norm_g[l],
                                                          k_norm_g[l], pos_s)
        att = _dsa_sample(qa, ka, va, qi, ki, wi, pos_s, rel_bias, cache_k[l], cache_v[l],
                          cache_kidx[l], page_table, k_top_sample)
        s_new, ret_o = _retention_chunk(state_ret[l].astype(jnp.float32), qr, kr, vr, lg)
        hs = hs + _merge(att, ret_o, gr, ret_gn_g[l], ret_gn_b[l], w_out[l], hs.dtype)
        hs = hs + _hmoe(_rmsnorm(hs, ln2_g[l]), w_group[l], w_expert[l],
                        w_gate[l], w_up[l], w_down[l])
        ks_l.append(ka)
        vs_l.append(va)
        is_l.append(ki)
        ss_l.append(s_new.astype(state_ret.dtype))

    return (hp, hs, jnp.stack(kp_l), jnp.stack(vp_l), jnp.stack(ip_l), jnp.stack(sp_l),
            jnp.stack(ks_l), jnp.stack(vs_l), jnp.stack(is_l), jnp.stack(ss_l))


_drawn_inputs = setup_inputs


def setup_inputs(seed=0):
    import zlib

    import numpy as np

    out = dict(_drawn_inputs(seed))
    spreads = {}
    factors = {'q_norm_g': 7.645, 'k_norm_g': 2.755, 'ret_gn_g': 3.246, 'ret_gn_b': 2.744, 'ln2_g': 2.864}
    for name, (base, spread) in spreads.items():
        noise = np.random.default_rng([zlib.crc32(name.encode()), seed]).standard_normal(out[name].shape)
        drawn = base * np.exp(spread * noise) if base else spread * noise
        out[name] = __import__('jax').numpy.asarray(drawn.astype(out[name].dtype))
    for name, factor in factors.items():
        out[name] = (out[name] * factor).astype(out[name].dtype)
    return out
```

```python
from contextlib import ExitStack

import numpy as np
import concourse.bass as bass
from concourse import mybir

ALU = mybir.AluOpType
ACT = mybir.ActivationFunctionType
F32 = mybir.dt.float32
BF16 = mybir.dt.bfloat16
U32 = mybir.dt.uint32
I32 = mybir.dt.int32
AX_X = mybir.AxisListType.X

P = 128
D = 1024
KD = D // P
SEQ = 1024
DB, DS = 8, 8
NS = DB * DS
TOK = SEQ + NS
NT = SEQ // P
TILES = NT + 1
H, HD = 8, 64
W = H * HD
PAIRS = H // 2
IH = 4
PAST, PAGE = 2048, 128
PAGES = PAST // PAGE
NPHYS = DB * PAGES * 5 // 4
NK = PAST + NS
TOPK = 256
NE, NG, EPG, DE = 32, 4, 8, 256
EPS, GN_EPS = 1e-6, 1e-5
NEG = -1e30
CAP = 96
PAGE_RING = 12
OVER = 2 * TOK // CAP
SLOTS = NE + OVER
MULTIPLES = TOK // CAP + 1
BISECT = 32

QA, KA, VA, QI, QR, KR, VR, GR = 0, 512, 1024, 1536, 1860, 2372, 2884, 3396
N_IN = 3908
N_QI = IH * 64 + 64 + IH


def rows_of(i):
    return P if i < NT else NS


def cols_of(i):
    return slice(i * P, i * P + rows_of(i))


def stage_semaphores(nc, ctx, prefix):
    taken = []

    def release():
        nc.clear_and_free_semaphores(taken)
        nc.all_engine_barrier()

    def take(name):
        taken.append(nc.alloc_semaphore(prefix + name))
        return taken[-1]

    ctx.callback(release)
    return take


class Chain:

    def __init__(self, engine, semaphore):
        self.engine, self.semaphore, self.n = engine, semaphore, 0

    def __call__(self, instruction):
        self.n += 1
        instruction.then_inc(self.semaphore, 1)
        self.engine.wait_ge(self.semaphore, self.n)


def norm_and_transpose(nc, name, tile_rows, g_dram, identity, uT, xn_dram=None):
    with ExitStack() as ctx:
        sb = lambda n, s, d=F32: ctx.enter_context(nc.sbuf_tensor(name + n, s, d))
        sem = stage_semaphores(nc, ctx, name)
        x = sb("x", [P, 3, D])
        sq = sb("sq", [P, D])
        xn = sb("xn", [P, 2, D])
        ms = sb("ms", [P, TILES])
        rms = sb("rms", [P, TILES])
        rstd = sb("rstd", [P, TILES])
        g = sb("g", [P, KD])
        psT = ctx.enter_context(nc.psum_tensor(name + "psT", [P, 2, KD, P], F32))
        x_loaded = [sem(f"x_loaded{j}") for j in range(3)]
        xn_stored = [sem(f"xn_stored{j}") for j in range(2)]
        g_loaded, squared, rooted = sem("g_loaded"), sem("squared"), sem("rooted")
        mean_ready, xn_ready = sem("mean_ready"), sem("xn_ready")
        turned, taken, dve_done = sem("turned"), sem("taken"), sem("dve_done")
        block = ctx.enter_context(nc.Block())

        @block.sync
        def _(sp):
            with nc.allow_non_contiguous_dma(reason="one gain per partition"):
                sp.dma_start(g[:, :], g_dram.rearrange("o (k p) -> p (o k)", p=P)).then_inc(g_loaded, 16)
            for i in range(TILES):
                if i >= 3:
                    sp.wait_ge(xn_ready, i - 2)
                sp.dma_start(x[:rows_of(i), i % 3, :], tile_rows(i)).then_inc(x_loaded[i % 3], 16)

        @block.scalar
        def _(act):
            for i in range(TILES):
                n = rows_of(i)
                act.wait_ge(x_loaded[i % 3], 16 * (i // 3 + 1))
                if i:
                    act.wait_ge(squared, i)
                nc.scalar.activation(sq[:n, :], x[:n, i % 3, :], ACT.Square,
                                     accum_out=ms[:n, i:i + 1]).then_inc(squared, 1)
                act.wait_ge(mean_ready, i + 1)
                nc.scalar.activation(rms[:n, i:i + 1], rstd[:n, i:i + 1], ACT.Sqrt).then_inc(rooted, 1)

        @block.vector
        def _(dve):
            link = Chain(dve, dve_done)
            dve.wait_ge(g_loaded, 16)
            for i in range(TILES + 1):
                if i < TILES:
                    n = rows_of(i)
                    dve.wait_ge(squared, i + 1)
                    nc.vector.tensor_scalar(rstd[:n, i:i + 1], ms[:n, i:i + 1], 1.0 / D, EPS,
                                            ALU.mult, ALU.add).then_inc(mean_ready, 1)
                    dve.wait_ge(rooted, i + 1)
                    link(nc.vector.reciprocal(rstd[:n, i:i + 1], rms[:n, i:i + 1]))
                    if i >= 2:
                        dve.wait_ge(turned, i - 1)
                        if xn_dram is not None:
                            dve.wait_ge(xn_stored[i % 2], 16 * (i // 2))
                    nc.vector.tensor_scalar(xn[:n, i % 2, :], x[:n, i % 3, :], rstd[:n, i:i + 1], None,
                                            ALU.mult).then_inc(xn_ready, 1)
                if i:
                    n = rows_of(i - 1)
                    dve.wait_ge(turned, i)
                    nc.vector.tensor_tensor(uT[:, :, cols_of(i - 1)], psT[:, (i - 1) % 2, :, :n],
                                            g[:, :].unsqueeze(2).to_broadcast([P, KD, n]),
                                            ALU.mult).then_inc(taken, 1)

        @block.tensor
        def _(pe):
            for i in range(TILES):
                n = rows_of(i)
                pe.wait_ge(xn_ready, i + 1)
                if i >= 2:
                    pe.wait_ge(taken, i - 1)
                for k in range(KD):
                    mm = nc.tensor.transpose(psT[:, i % 2, k, :n], xn[:n, i % 2, k * P:(k + 1) * P],
                                             identity[:n, :n])
                mm.then_inc(turned, 1)

        @block.gpsimd
        def _(pool):
            if xn_dram is not None:
                for i in range(TILES):
                    pool.wait_ge(xn_ready, i + 1)
                    pool.dma_start(xn_dram[cols_of(i), :], xn[:rows_of(i), i % 2, :]).then_inc(xn_stored[i % 2], 16)
                pool.wait_ge(xn_stored[0], 16 * ((TILES + 1) // 2))
                pool.wait_ge(xn_stored[1], 16 * (TILES // 2))


def project(nc, name, chunks, S, A, rotary=None, gains=None):
    units = [(c, i) for c in range(len(chunks)) for i in range(TILES)]
    worked = [u for u, (c, i) in enumerate(units) if chunks[c]["kind"] in ("rotary", "norm", "index")]
    stored = [u for u, (c, i) in enumerate(units) if "out" in chunks[c]]
    with ExitStack() as ctx:
        sb = lambda n, s, d=F32: ctx.enter_context(nc.sbuf_tensor(name + n, s, d))
        sem = stage_semaphores(nc, ctx, name)
        w = sb("w", [P, 2, KD, W])
        z = sb("z", [P, 3, W])
        nat = sb("nat", [P, 2, W])
        t = sb("t", [P, 4, W // 2])
        ssq = sb("ssq", [P, H])
        rms = sb("rms", [P, H])
        rstd = sb("rstd", [P, H])
        psZ = [ctx.enter_context(nc.psum_tensor(f"{name}psZ{j}", [P, W], F32)) for j in range(3)]
        psT = [ctx.enter_context(nc.psum_tensor(f"{name}psT{j}", [P, 4, P], F32)) for j in range(2)]
        w_loaded = [sem(f"w_loaded{j}") for j in range(2)]
        z_ready, z_taken, z_kept = sem("z_ready"), sem("z_taken"), sem("z_kept")
        mean_ready, rooted, nat_ready = sem("mean_ready"), sem("rooted"), sem("nat_ready")
        turned, t_taken, dve_done = sem("turned"), sem("t_taken"), sem("dve_done")
        out_stored = [sem(f"out_stored{j}") for j in range(2)]
        block = ctx.enter_context(nc.Block())

        def store_count(u, j):
            return sum(1 for q, s in enumerate(stored) if s < u and q % 2 == j)

        @block.sync
        def _(sp):
            for c, ch in enumerate(chunks):
                if c >= 2:
                    sp.wait_ge(z_ready, TILES * (c - 1))
                sp.dma_start(w[:, c % 2, :, :ch["n"]],
                             S["w_in"][:, ch["col"]:ch["col"] + ch["n"]].rearrange("(k p) n -> p k n", p=P)
                             ).then_inc(w_loaded[c % 2], 16)

        @block.tensor
        def _(pe):
            def turn(q):
                c, i = units[worked[q]]
                ch, n = chunks[c], rows_of(i)
                pe.wait_ge(nat_ready, q + 1)
                if q >= 2:
                    pe.wait_ge(t_taken, q - 1)
                src = ch["nat"][:, i, :] if "nat" in ch else nat[:, q % 2, :]
                for b in range(ch["blocks"]):
                    mm = nc.tensor.transpose(psT[q % 2][:, b, :n], src[:n, b * P:(b + 1) * P], A["identity"][:n, :n])
                mm.then_inc(turned, 1)

            done = 0
            for u, (c, i) in enumerate(units):
                n, ch = rows_of(i), chunks[c]
                if i == 0:
                    pe.wait_ge(w_loaded[c % 2], 16 * (c // 2 + 1))
                if u >= 3:
                    pe.wait_ge(z_taken, u - 2)
                for k in range(KD):
                    mm = nc.tensor.matmul(psZ[u % 3][:n, :ch["n"]], A["uT"][:, k, cols_of(i)],
                                          w[:, c % 2, k, :ch["n"]], start=(k == 0), stop=(k == KD - 1))
                mm.then_inc(z_ready, 1)
                while done < len(worked) and worked[done] < u:
                    turn(done)
                    done += 1
            while done < len(worked):
                turn(done)
                done += 1

        @block.scalar
        def _(act):
            def take_turned(q):
                c, i = units[worked[q]]
                ch = chunks[c]
                act.wait_ge(turned, q + 1)
                for dst, b0, b1 in ch["to"]:
                    ins = nc.scalar.activation(dst[:, :, cols_of(i)], psT[q % 2][:, b0:b1, :rows_of(i)], ACT.Copy)
                ins.then_inc(t_taken, 1)

            done, roots = 0, 0
            for u, (c, i) in enumerate(units):
                ch, n = chunks[c], rows_of(i)
                act.wait_ge(z_ready, u + 1)
                if u in worked:
                    q = worked.index(u)
                    if q >= 3:
                        act.wait_ge(nat_ready, q - 2)
                    if ch["kind"] == "index" and "out" in ch:
                        q2 = stored.index(u)
                        if q2 >= 3:
                            act.wait_ge(out_stored[(q2 - 3) % 2], 16 * ((q2 - 3) // 2 + 1))
                    nc.scalar.activation(z[:n, q % 3, :ch["n"]], psZ[u % 3][:n, :ch["n"]], ACT.Copy).then_inc(z_taken, 1)
                    if ch["kind"] == "norm":
                        roots += 1
                        act.wait_ge(mean_ready, roots)
                        nc.scalar.activation(rms[:n, :], ssq[:n, :], ACT.Sqrt).then_inc(rooted, 1)
                elif ch["kind"] == "silu":
                    nc.scalar.activation(ch["keep"][:n, i, :], psZ[u % 3][:n, :], ACT.Silu).then_inc(z_taken, 1)
                else:
                    nc.scalar.activation(ch["keep"][:n, i, :], psZ[u % 3][:n, :], ACT.Copy).then_inc(z_taken, 1)
                while done < len(worked) and worked[done] < u:
                    take_turned(done)
                    done += 1
            while done < len(worked):
                take_turned(done)
                done += 1

        @block.vector
        def _(dve):
            link = Chain(dve, dve_done)
            roots = 0
            for q, u in enumerate(worked):
                c, i = units[u]
                ch, n = chunks[c], rows_of(i)
                dve.wait_ge(z_taken, u + 1)
                zz = z[:n, q % 3, :]
                out = (ch["nat"][:n, i, :] if "nat" in ch else nat[:n, q % 2, :])
                if q >= 2:
                    dve.wait_ge(turned, q - 1)
                    for j in range(2):
                        if "nat" not in ch and store_count(u - 1, j):
                            dve.wait_ge(out_stored[j], 16 * store_count(u - 1, j))
                if ch["kind"] == "rotary":
                    z4 = zz.rearrange("p (h s r) -> p h s r", h=H, s=2)
                    o4 = out.rearrange("p (h s r) -> p h s r", h=H, s=2)
                    r = HD // 2
                    cos = A["cos"][:n, i, :].unsqueeze(1).to_broadcast([n, H, r])
                    sin = A["sin"][:n, i, :].unsqueeze(1).to_broadcast([n, H, r])
                    tv = [t[:n, j, :].rearrange("p (h r) -> p h r", h=H) for j in range(4)]
                    nc.vector.tensor_tensor(tv[0], z4[:, :, 0, :], cos, ALU.mult)
                    nc.vector.tensor_tensor(tv[1], z4[:, :, 1, :], sin, ALU.mult)
                    nc.vector.tensor_tensor(tv[2], z4[:, :, 0, :], sin, ALU.mult)
                    link(nc.vector.tensor_tensor(tv[3], z4[:, :, 1, :], cos, ALU.mult))
                    nc.vector.tensor_tensor(o4[:, :, 0, :], tv[0], tv[1], ALU.subtract)
                    link(nc.vector.tensor_tensor(o4[:, :, 1, :], tv[2], tv[3], ALU.add))
                    o3 = out.rearrange("p (h e) -> p h e", h=H)
                    dec = ch["decay"][:n, 1 if i == NT else 0, :].unsqueeze(2).to_broadcast([n, H, HD])
                    nc.vector.tensor_tensor(o3, o3, dec, ALU.mult).then_inc(nat_ready, 1)
                elif ch["kind"] == "norm":
                    roots += 1
                    z3 = zz.rearrange("p (h e) -> p h e", h=H)
                    o3 = out.rearrange("p (h e) -> p h e", h=H)
                    link(nc.vector.tensor_tensor(out, zz, zz, ALU.mult))
                    link(nc.vector.tensor_reduce(rstd[:n, :], o3, AX_X, ALU.add))
                    nc.vector.tensor_scalar(ssq[:n, :], rstd[:n, :], 1.0 / HD, EPS, ALU.mult, ALU.add).then_inc(mean_ready, 1)
                    dve.wait_ge(rooted, roots)
                    link(nc.vector.reciprocal(rstd[:n, :], rms[:n, :]))
                    link(nc.vector.tensor_tensor(o3, z3, rstd[:n, :].unsqueeze(2).to_broadcast([n, H, HD]), ALU.mult))
                    nc.vector.tensor_tensor(o3, o3, ch["gain"][:n, :].unsqueeze(1).to_broadcast([n, H, HD]),
                                            ALU.mult).then_inc(nat_ready, 1)
                else:
                    nc.vector.tensor_copy(out[:, 0:320], zz[:, 0:320])
                    nc.vector.tensor_copy(out[:, 320:384], zz[:, 256:320])
                    nc.vector.tensor_scalar(A["wi"][:n, i, :], zz[:, 320:324], IH ** -0.5 * 0.125, None,
                                            ALU.mult).then_inc(nat_ready, 1)

        @block.gpsimd
        def _(pool):
            for q, u in enumerate(stored):
                c, i = units[u]
                ch, n = chunks[c], rows_of(i)
                if u in worked:
                    pool.wait_ge(nat_ready, worked.index(u) + 1)
                    src = nat[:n, worked.index(u) % 2, ch["out_cols"]]
                else:
                    pool.wait_ge(z_taken, u + 1)
                    src = ch["keep"][:n, i, :]
                pool.dma_start(ch["out"](i), src).then_inc(out_stored[q % 2], 16)
            for j in range(2):
                if store_count(len(units), j):
                    pool.wait_ge(out_stored[j], 16 * store_count(len(units), j))


def retention(nc, S, A):
    with ExitStack() as ctx:
        sb = lambda n, s, d=F32: ctx.enter_context(nc.sbuf_tensor("r_" + n, s, d))
        sem = stage_semaphores(nc, ctx, "r_")
        ps = lambda n, s: ctx.enter_context(nc.psum_tensor("r_" + n, s, F32))
        intra = sb("intra", [P, H, P])
        state = sb("state", [P, PAIRS, HD])
        s0 = sb("s0", [P, DB, PAIRS, HD])
        vexp = sb("vexp", [NS, 2, DB, HD])
        oT = sb("oT", [HD, W])
        o = sb("o", [P, W])
        o2 = sb("o2", [P, W])
        on = sb("on", [P, 2, W])
        st = sb("st", [P, 4, H])
        gg = sb("gg", [P, W])
        gb = sb("gb", [P, W])
        blank = sb("blank", [CAP, D])
        blank_ready = sem("blank_ready")
        psI = ps("psI", [P, 2, 4, P])
        psO = ps("psO", [P, 2, PAIRS, P])
        psU = ps("psU", [P, PAIRS, P])
        psN = ps("psN", [P, W])
        psT = ps("psT", [P, PAIRS, P])
        loaded, intra_used = sem("loaded"), sem("intra_used")
        scores_ready, intra_ready, o_ready, o_taken = sem("scores_ready"), sem("intra_ready"), sem("o_ready"), sem("o_taken")
        update_ready, state_ready, on_ready = sem("update_ready"), sem("state_ready"), sem("on_ready")
        turned, t_taken, dve_done, var_ready, rooted = sem("turned"), sem("t_taken"), sem("dve_done"), sem("var_ready"), sem("rooted")
        oT_ready, v_spread, su_ready, su_taken, stored = sem("oT_ready"), sem("v_spread"), sem("su_ready"), sem("su_taken"), sem("stored")
        block = ctx.enter_context(nc.Block())
        qpT, kpT, kp, vr = A["qpT"], A["kpT"], A["kp"], A["vr"]

        @block.sync
        def _(sp):
            sp.dma_start(gg[:, :], S["ret_gn_g"].to_broadcast([P, W])).then_inc(loaded, 16)
            sp.dma_start(gb[:, :], S["ret_gn_b"].to_broadcast([P, W])).then_inc(loaded, 16)
            for half in range(2):
                for b in range(DB):
                    sp.dma_start(s0[half * HD:(half + 1) * HD, b, :, :],
                                 S["state_ret"][b].rearrange("(pr hh) d e -> hh d pr e", hh=2)[half]).then_inc(loaded, 16)
            sp.wait_ge(blank_ready, 1)
            for v in range(NE, SLOTS):
                sp.dma_start(S["y"][v * CAP:(v + 1) * CAP, :], blank[:, :]).then_inc(stored, 16)
            sp.wait_ge(state_ready, NT)
            for half in range(2):
                sp.dma_start(S["ret_prompt"].rearrange("(pr hh) d e -> hh d pr e", hh=2)[half],
                             state[half * HD:(half + 1) * HD, :, :]).then_inc(stored, 16)
            sp.wait_ge(su_taken, PAIRS)
            for half in range(2):
                for b in range(DB):
                    sp.dma_start(S["ret_sample"][b].rearrange("(pr hh) d e -> hh d pr e", hh=2)[half],
                                 s0[half * HD:(half + 1) * HD, b, :, :]).then_inc(stored, 16)
            sp.wait_ge(stored, 16 * (2 + 2 * DB + OVER))

        @block.tensor
        def _(pe):
            def scores(i):
                n = rows_of(i)
                if i:
                    pe.wait_ge(intra_ready, i)
                for h in range(H):
                    half = slice(h % 2 * HD, h % 2 * HD + HD)
                    mm = nc.tensor.matmul(psI[:n, h % 2, h // 2, :n], kpT[half, h // 2, cols_of(i)],
                                          qpT[half, h // 2, cols_of(i)], start=True, stop=True)
                mm.then_inc(scores_ready, 1)

            def turn(i):
                n = rows_of(i)
                pe.wait_ge(on_ready, i + 1)
                if i:
                    pe.wait_ge(t_taken, i)
                for b in range(PAIRS):
                    mm = nc.tensor.transpose(psT[:, b, :n], on[:n, i % 2, b * P:(b + 1) * P], A["identity"][:n, :n])
                mm.then_inc(turned, 1)

            scores(0)
            for i in range(NT):
                scores_next = i + 1
                pe.wait_ge(intra_ready, i + 1)
                if i:
                    pe.wait_ge(state_ready, i)
                    pe.wait_ge(o_taken, i)
                for h in range(H):
                    half = slice(h % 2 * HD, h % 2 * HD + HD)
                    out = psO[:, h % 2, h // 2, :HD]
                    mm = nc.tensor.matmul(out, intra[:, h, :], vr[:, i, h * HD:(h + 1) * HD],
                                          start=True, stop=(i == 0))
                    if i:
                        mm = nc.tensor.matmul(out, qpT[half, h // 2, cols_of(i)], state[half, h // 2, :],
                                              start=False, stop=True)
                mm.then_inc(o_ready, 1)
                for pr in range(PAIRS):
                    mm = nc.tensor.matmul(psU[:, pr, :], kp[:, i, pr * P:(pr + 1) * P], vr[:, i, pr * P:(pr + 1) * P],
                                          start=True, stop=True)
                mm.then_inc(update_ready, 1)
                scores(scores_next)
                if i:
                    turn(i - 1)
            i = NT
            pe.wait_ge(intra_ready, i + 1)
            pe.wait_ge(o_taken, i)
            pe.wait_ge(loaded, 16 * (2 + 2 * DB))
            for h in range(H):
                mm = nc.tensor.matmul(psO[:HD, h % 2, h // 2, :HD], vr[:NS, i, h * HD:(h + 1) * HD], intra[:NS, h, :NS],
                                      start=(h < 2), stop=False, skip_group_check=True)
            mm.then_inc(intra_used, 1)
            pe.wait_ge(intra_used, 1)
            for h in range(H):
                half = slice(h % 2 * HD, h % 2 * HD + HD)
                for b in range(DB):
                    mm = nc.tensor.matmul(psO[:HD, h % 2, h // 2, b * DS:(b + 1) * DS], s0[half, b, h // 2, :],
                                          qpT[half, h // 2, SEQ + b * DS:SEQ + (b + 1) * DS],
                                          start=False, stop=(b == DB - 1), skip_group_check=True)
            mm.then_inc(o_ready, 1)
            turn(NT - 1)
            pe.wait_ge(oT_ready, 1)
            for h in range(H):
                mm = nc.tensor.transpose(psN[:NS, h * HD:(h + 1) * HD], oT[:, h * HD:(h + 1) * HD], A["identity"][:HD, :HD])
            mm.then_inc(o_ready, 1)
            for pr in range(PAIRS):
                pe.wait_ge(v_spread, 2 * (pr + 1))
                pe.wait_ge(state_ready, NT)
                if pr:
                    pe.wait_ge(su_taken, pr)
                for hh in range(2):
                    mm = nc.tensor.matmul(psU[hh * HD:(hh + 1) * HD, :, :].rearrange("p a b -> p (a b)"),
                                          kp[:NS, i, (2 * pr + hh) * HD:(2 * pr + hh + 1) * HD],
                                          vexp[:, hh, :, :].rearrange("p b e -> p (b e)"), start=True, stop=True)
                mm.then_inc(su_ready, 1)
            turn(NT)

        @block.scalar
        def _(act):
            for i in range(TILES):
                n = rows_of(i)
                if i == NT:
                    act.wait_ge(o_ready, NT + 1)
                    nc.scalar.activation(oT[:, :].rearrange("p (pr hh e) -> p hh pr e", hh=2, e=HD), psO[:HD, :, :, :HD], ACT.Copy).then_inc(oT_ready, 1)
                    act.wait_ge(o_ready, NT + 2)
                    act.wait_ge(on_ready, i)
                    nc.scalar.activation(o[:n, :], psN[:n, :], ACT.Copy).then_inc(o_taken, 1)
                else:
                    act.wait_ge(o_ready, i + 1)
                    if i:
                        act.wait_ge(on_ready, i)
                    nc.scalar.activation(o[:n, :].rearrange("p (pr hh e) -> p hh pr e", hh=2, e=HD), psO[:n, :, :, :HD], ACT.Copy).then_inc(o_taken, 1)
                act.wait_ge(var_ready, i + 1)
                nc.scalar.activation(st[:n, 2, :], st[:n, 1, :], ACT.Sqrt).then_inc(rooted, 1)
                act.wait_ge(turned, i + 1)
                nc.scalar.activation(A["retT"][:, :, cols_of(i)], psT[:, :, :n], ACT.Copy).then_inc(t_taken, 1)

        @block.vector
        def _(dve):
            link = Chain(dve, dve_done)
            link(nc.vector.memset(state[:, :, :], 0.0))
            nc.vector.memset(blank[:, :], 0.0).then_inc(blank_ready, 1)
            dve.wait_ge(loaded, 16 * (2 + 2 * DB))

            def mask(i):
                n = rows_of(i)
                dve.wait_ge(scores_ready, i + 1)
                if i:
                    dve.wait_ge(o_ready, i)
                m = A["ret_mask"][:n, 1 if i == NT else 0, :n].unsqueeze(1).to_broadcast([n, 4, n])
                link(nc.vector.tensor_tensor(intra[:n, 0:H:2, :n], psI[:n, 0, :, :n], m, ALU.mult))
                nc.vector.tensor_tensor(intra[:n, 1:H:2, :n], psI[:n, 1, :, :n], m, ALU.mult).then_inc(intra_ready, 1)

            mask(0)
            for i in range(TILES):
                n = rows_of(i)
                if i < NT:
                    dve.wait_ge(update_ready, i + 1)
                    for hh in range(2):
                        half = slice(hh * HD, (hh + 1) * HD)
                        link(nc.vector.tensor_tensor(state[half, :, :], psU[half, :, hh * HD:(hh + 1) * HD],
                                                     state[half, :, :], ALU.add))
                    nc.vector.tensor_tensor(state[:, :, :], state[:, :, :],
                                            A["gamma_chunk"][:, 0, :].unsqueeze(2).to_broadcast([P, PAIRS, HD]),
                                            ALU.mult).then_inc(state_ready, 1)
                    mask(i + 1)
                else:
                    for pr in range(PAIRS):
                        if pr:
                            dve.wait_ge(su_ready, pr)
                        for hh in range(2):
                            h = 2 * pr + hh
                            nc.vector.tensor_tensor(
                                vexp[:, hh, :, :], A["own_seq"][:NS, :].unsqueeze(2).to_broadcast([NS, DB, HD]),
                                vr[:NS, i, h * HD:(h + 1) * HD].unsqueeze(1).to_broadcast([NS, DB, HD]),
                                ALU.mult).then_inc(v_spread, 1)
                        dve.wait_ge(su_ready, pr + 1)
                        link(nc.vector.tensor_tensor(s0[:, :, pr, :], psU[:, :, :].rearrange("p a (b e) -> p (a b) e", e=HD),
                                                     s0[:, :, pr, :], ALU.add))
                        nc.vector.tensor_scalar(s0[:, :, pr, :], s0[:, :, pr, :], A["gamma_chunk"][:, 1, pr:pr + 1], None,
                                                ALU.mult).then_inc(su_taken, 1)
                dve.wait_ge(o_taken, i + 1)
                o3 = o[:n, :].rearrange("p (h e) -> p h e", h=H)
                q3 = o2[:n, :].rearrange("p (h e) -> p h e", h=H)
                bc = lambda a: a.unsqueeze(2).to_broadcast([n, H, HD])
                link(nc.vector.tensor_reduce(st[:n, 0, :], o3, AX_X, ALU.add))
                link(nc.vector.tensor_scalar(st[:n, 0, :], st[:n, 0, :], 1.0 / HD, None, ALU.mult))
                link(nc.vector.tensor_tensor(o3, o3, bc(st[:n, 0, :]), ALU.subtract))
                link(nc.vector.tensor_tensor(q3, o3, o3, ALU.mult))
                link(nc.vector.tensor_reduce(st[:n, 3, :], q3, AX_X, ALU.add))
                nc.vector.tensor_scalar(st[:n, 1, :], st[:n, 3, :], 1.0 / HD, GN_EPS, ALU.mult, ALU.add).then_inc(var_ready, 1)
                dve.wait_ge(rooted, i + 1)
                link(nc.vector.reciprocal(st[:n, 3, :], st[:n, 2, :]))
                link(nc.vector.tensor_tensor(q3, o3, bc(st[:n, 3, :]), ALU.mult))
                link(nc.vector.tensor_tensor(o2[:n, :], o2[:n, :], gg[:n, :], ALU.mult))
                link(nc.vector.tensor_tensor(o2[:n, :], o2[:n, :], gb[:n, :], ALU.add))
                if i >= 2:
                    dve.wait_ge(turned, i - 1)
                nc.vector.tensor_tensor(on[:n, i % 2, :], o2[:n, :], A["sg"][:n, i, :], ALU.mult).then_inc(on_ready, 1)


def index_scores(nc, S, A, X):
    blocks = list(range(TOPK // P, NT))
    chunks = [(i, k0, min(512, (i + 1) * P - k0)) for i in blocks for k0 in range(0, (i + 1) * P, 512)]
    units = [(i, k0, n, h) for i, k0, n in chunks for h in range(IH)]
    U = len(units)
    with ExitStack() as ctx:
        sb = lambda n, s, d=F32: ctx.enter_context(nc.sbuf_tensor("x_" + n, s, d))
        sem = stage_semaphores(nc, ctx, "x_")
        r = sb("r", [P, 3, 512])
        qs = sb("qs", [P, DB, IH, DS])
        ws = sb("ws", [P, 2])
        kx = sb("kx", [P, 2, 16, 64])
        kxT = sb("kxT", [P, 4, 8, P])
        wsum = sb("wsum", [P, 2, 512])
        psS = ctx.enter_context(nc.psum_tensor("x_psS", [P, 3, 512], F32))
        psK = ctx.enter_context(nc.psum_tensor("x_psK", [P, 2, 4, P], F32))
        psQ = ctx.enter_context(nc.psum_tensor("x_psQ", [P, 512], F32))
        psR = ctx.enter_context(nc.psum_tensor("x_psR", [NS, 512], F32))
        s_ready, s_taken, r_used, dve_done = sem("s_ready"), sem("s_taken"), sem("r_used"), sem("dve_done")
        q_loaded, w_loaded = sem("q_loaded"), sem("w_loaded")
        kx_loaded = [sem(f"kx_loaded{j}") for j in range(2)]
        kx_turned, kxT_ready = sem("kx_turned"), sem("kxT_ready")
        heads_ready, heads_weighed, row_ready, row_taken = sem("heads_ready"), sem("heads_weighed"), sem("row_ready"), sem("row_taken")
        block = ctx.enter_context(nc.Block())
        parts = [(half, rr) for half in range(2) for rr in (0, 4)] + [None]

        @block.sync
        def _(sp):
            with nc.allow_non_contiguous_dma(reason="small pieces of the sample queries"):
                for half in range(2):
                    for h in range(IH):
                        sp.dma_start(qs[half * 64:half * 64 + 64, :, h, :],
                                     A["qiT"][h % 2 * 64:h % 2 * 64 + 64, h // 2, SEQ:].rearrange("p (b t) -> p b t", b=DB)
                                     ).then_inc(q_loaded, 16)
                for b in range(DB):
                    for h in range(IH):
                        row = b % 4 * 32 + h * DS
                        sp.dma_start(ws[row:row + DS, b // 4:b // 4 + 1], A["wi"][b * DS:(b + 1) * DS, NT, h:h + 1]
                                     ).then_inc(w_loaded, 16)

        @block.gpsimd
        def _(pool):
            for b in range(DB):
                if b >= 2:
                    pool.wait_ge(kx_turned, 2 * (b - 1))
                pool.indirect_dma_start(kx[:, b % 2, :, :].rearrange("p r e -> p (r e)"), None, S["cache_kidx"],
                                        bass.IndirectOffsetOnAxis(ap=A["row_id"][:, b:b + 1], axis=0)
                                        ).then_inc(kx_loaded[b % 2], 16)

        @block.tensor
        def _(pe):
            for u, (i, k0, n, h) in enumerate(units):
                if u >= 3:
                    pe.wait_ge(s_taken, u - 2)
                half = slice(h % 2 * 64, h % 2 * 64 + 64)
                nc.tensor.matmul(psS[:, u % 3, :n], A["qiT"][half, h // 2, cols_of(i)],
                                 A["kiT"][half, k0:k0 + n], start=True, stop=True).then_inc(s_ready, 1)
            pe.wait_ge(q_loaded, 16 * 2 * IH)
            m = 0
            for g in range(2):
                for bb in range(4):
                    b = 4 * g + bb
                    pe.wait_ge(kx_loaded[b % 2], 16 * (b // 2 + 1))
                    for j in range(2):
                        q = 2 * b + j
                        if q >= 2:
                            pe.wait_ge(kxT_ready, q - 1)
                        for rr in range(4):
                            e0 = (4 * j + rr) * 2
                            mm = nc.tensor.transpose(psK[:, j, rr, :], kx[:, b % 2, e0:e0 + 2, :].rearrange("p r e -> p (r e)"),
                                                     A["identity"][:, :])
                        mm.then_inc(kx_turned, 1)
                pe.wait_ge(kxT_ready, 8 * (g + 1))
                for part in parts:
                    if m:
                        pe.wait_ge(heads_weighed, m)
                    for bb in range(4):
                        half = slice((part[0] if part else 0) * 64, (part[0] if part else 0) * 64 + 64)
                        rhs = (kxT[half, bb, part[1]:part[1] + 4, :].rearrange("p r k -> p (r k)") if part
                               else A["kiT"][half, SEQ:])
                        mm = nc.tensor.matmul(psQ[bb * 32:bb * 32 + 32, :rhs.shape[1]],
                                              qs[half, 4 * g + bb, :, :].rearrange("p h t -> p (h t)"), rhs,
                                              start=True, stop=True)
                    mm.then_inc(heads_ready, 1)
                    pe.wait_ge(heads_weighed, m + 1)
                    if m:
                        pe.wait_ge(row_taken, m)
                    n = 512 if part else NS
                    nc.tensor.matmul(psR[32 * g:32 * g + 32, :n], A["sum_heads"][:, :], wsum[:, m % 2, :n],
                                     start=True, stop=True).then_inc(row_ready, 1)
                    m += 1

        @block.scalar
        def _(act):
            for u, (i, k0, n, h) in enumerate(units):
                act.wait_ge(s_ready, u + 1)
                if u >= 3:
                    act.wait_ge(r_used, u - 2)
                nc.scalar.activation(r[:, u % 3, :n], psS[:, u % 3, :n], ACT.Relu).then_inc(s_taken, 1)
            m = 0
            for g in range(2):
                for q in range(8 * g, 8 * g + 8):
                    act.wait_ge(kx_turned, q + 1)
                    if g:
                        act.wait_ge(heads_ready, 5)
                    nc.scalar.activation(kxT[:, (q // 2) % 4, 4 * (q % 2):4 * (q % 2) + 4, :], psK[:, q % 2, :, :],
                                         ACT.Copy).then_inc(kxT_ready, 1)
                for part in parts:
                    act.wait_ge(row_ready, m + 1)
                    rows = slice(32 * g, 32 * g + 32)
                    if part:
                        dst = X["sc_s"][rows, :PAST].rearrange("q (k rr hf) -> q hf rr k", hf=2, rr=8)[:, part[0], part[1]:part[1] + 4, :]
                        src = psR[rows, :].rearrange("q (rr k) -> q rr k", rr=4)
                    else:
                        dst, src = X["sc_s"][rows, PAST:], psR[rows, :NS]
                    nc.scalar.activation(dst, src, ACT.Copy).then_inc(row_taken, 1)
                    m += 1

        @block.vector
        def _(dve):
            link = Chain(dve, dve_done)
            link(nc.vector.memset(X["lo"][:, :], 0.0))
            link(nc.vector.memset(X["hi"][:, :], 0.0))
            for u, (i, k0, n, h) in enumerate(units):
                dve.wait_ge(s_taken, u + 1)
                acc = X["sc"](i)[:, k0:k0 + n]
                if h == 0:
                    ins = nc.vector.tensor_scalar(acc, r[:, u % 3, :n], A["wi"][:, i, h:h + 1], None, ALU.mult)
                else:
                    ins = nc.vector.scalar_tensor_tensor(acc, r[:, u % 3, :n], A["wi"][:, i, h:h + 1], acc, ALU.mult, ALU.add)
                ins.then_inc(r_used, 1)
                dve.wait_ge(r_used, u + 1)
            for i in blocks:
                sc = X["sc"](i)
                nc.vector.tensor_reduce(X["lo"][:, i:i + 1], sc, AX_X, ALU.min)
                link(nc.vector.tensor_reduce(X["hi"][:, i:i + 1], sc, AX_X, ALU.max))
                d = sc[:, i * P:]
                link(nc.vector.tensor_tensor(d, d, A["causal"][:, :], ALU.add))
            dve.wait_ge(w_loaded, 16 * DB * IH)
            m = 0
            for g in range(2):
                for part in parts:
                    n = 512 if part else NS
                    dve.wait_ge(heads_ready, m + 1)
                    nc.vector.tensor_scalar(wsum[:, m % 2, :n], psQ[:, :n], 0.0, ws[:, g:g + 1], ALU.max, ALU.mult
                                            ).then_inc(heads_weighed, 1)
                    m += 1
            dve.wait_ge(row_taken, m)
            link(nc.vector.tensor_reduce(X["lo"][:NS, NT:NT + 1], X["sc_s"][:, :], AX_X, ALU.min))
            link(nc.vector.tensor_reduce(X["hi"][:NS, NT:NT + 1], X["sc_s"][:, :], AX_X, ALU.max))
            d = X["sc_s"][:, PAST:]
            link(nc.vector.tensor_tensor(d, d, A["causal_s"][:NS, :], ALU.add))


def select_keys(nc, A, X):
    blocks = list(range(TOPK // P, NT))
    on_act = [NT, NT - 1]
    on_dve = [i for i in blocks if i not in on_act]
    c0 = blocks[0]

    def view(i):
        return X["sc"](i) if i < NT else X["sc_s"][:, :]

    with ExitStack() as ctx:
        sb = lambda n, s, d=F32: ctx.enter_context(nc.sbuf_tensor("t_" + n, s, d))
        sem = stage_semaphores(nc, ctx, "t_")
        two = sb("two", [P, TILES])
        mid = sb("mid", [P, TILES])
        nmid = sb("nmid", [P, TILES])
        count = sb("count", [P, TILES])
        want = sb("want", [P, TILES])
        up = sb("up", [P, TILES])
        down = sb("down", [P, TILES])
        junk = sb("junk", [P, SEQ], BF16)
        junk_act = sb("junk_act", [P, NK], BF16)
        above = sb("above", [P, NK])
        band = sb("band", [P, NK])
        before = sb("before", [P, NK])
        mid_ready, act_counted, dve_step, dve_done = sem("mid_ready"), sem("act_counted"), sem("dve_step"), sem("dve_done")
        block = ctx.enter_context(nc.Block())
        lo, hi = X["lo"], X["hi"]
        STEPS = 2 + len(on_dve) + 6

        @block.scalar
        def _(act):
            with act.Fori(0, BISECT) as it:
                act.wait_ge(mid_ready, it + 1)
                for i in on_act:
                    n = rows_of(i)
                    nc.scalar.activation(junk_act[:n, :view(i).shape[1]], view(i), ACT.Sign, bias=nmid[:n, i:i + 1],
                                         accum_out=count[:n, i:i + 1]).then_inc(act_counted, 1)
                    act.wait_ge(act_counted, it * len(on_act) + (on_act.index(i) + 1))

        @block.vector
        def _(dve):
            link = Chain(dve, dve_done)
            for i in blocks + [NT]:
                n = view(i).shape[1]
                link(nc.vector.memset(want[:, i:i + 1], float(2 * TOPK - n if i in on_act else TOPK)))
            link(nc.vector.memset(count[:, :], 0.0))
            with dve.Fori(0, BISECT) as it:
                base = it * STEPS
                nc.vector.tensor_tensor(two[:, c0:], lo[:, c0:], hi[:, c0:], ALU.add).then_inc(dve_step, 1)
                dve.wait_ge(dve_step, base + 1)
                nc.vector.tensor_scalar(nmid[:, c0:], two[:, c0:], -0.5, None, ALU.mult).then_inc(mid_ready, 1)
                nc.vector.tensor_scalar(mid[:, c0:], two[:, c0:], 0.5, None, ALU.mult).then_inc(dve_step, 1)
                dve.wait_ge(dve_step, base + 2)
                for j, i in enumerate(on_dve):
                    nc.vector.tensor_scalar(junk[:, :view(i).shape[1]], view(i), mid[:, i:i + 1], None, ALU.is_ge, ALU.add,
                                            accum_out=count[:, i:i + 1]).then_inc(dve_step, 1)
                    dve.wait_ge(dve_step, base + (3 + j))
                dve.wait_ge(act_counted, it * len(on_act) + len(on_act))
                nc.vector.tensor_tensor(up[:, c0:], count[:, c0:], want[:, c0:], ALU.is_ge).then_inc(dve_step, 1)
                nc.vector.tensor_tensor(down[:, c0:], count[:, c0:], want[:, c0:], ALU.is_lt).then_inc(dve_step, 1)
                dve.wait_ge(dve_step, base + (4 + len(on_dve)))
                nc.vector.scalar_tensor_tensor(down[:, c0:], down[:, c0:], NEG, mid[:, c0:], ALU.mult, ALU.add).then_inc(dve_step, 1)
                nc.vector.scalar_tensor_tensor(up[:, c0:], up[:, c0:], -NEG, mid[:, c0:], ALU.mult, ALU.add).then_inc(dve_step, 1)
                dve.wait_ge(dve_step, base + (6 + len(on_dve)))
                nc.vector.tensor_tensor(lo[:, c0:], lo[:, c0:], down[:, c0:], ALU.max).then_inc(dve_step, 1)
                nc.vector.tensor_tensor(hi[:, c0:], hi[:, c0:], up[:, c0:], ALU.min).then_inc(dve_step, 1)
                dve.wait_ge(dve_step, base + STEPS)
            for i in blocks + [NT]:
                s = view(i)
                r, n = s.shape[0], s.shape[1]
                a, bd, be = above[:r, :n], band[:r, :n], before[:r, :n]
                link(nc.vector.tensor_scalar(a, s, hi[:r, i:i + 1], None, ALU.is_gt, ALU.add, accum_out=count[:r, i:i + 1]))
                link(nc.vector.scalar_tensor_tensor(bd, s, lo[:r, i:i + 1], a, ALU.is_ge, ALU.subtract))
                link(nc.vector.tensor_tensor_scan(be, bd, bd, 0.0, ALU.add, ALU.max))
                link(nc.vector.tensor_scalar(want[:r, i:i + 1], count[:r, i:i + 1], -1.0, float(TOPK), ALU.mult, ALU.add))
                link(nc.vector.scalar_tensor_tensor(bd, be, want[:r, i:i + 1], bd, ALU.is_le, ALU.mult))
                link(nc.vector.tensor_tensor(a, a, bd, ALU.add))
                if i < NT:
                    link(nc.vector.tensor_scalar(X["mask"](i), a, -1.0, -NEG, ALU.add, ALU.mult))
                else:
                    link(nc.vector.tensor_scalar(X["mask_s"][:, :PAST].rearrange("q (r k) -> q k r", r=16),
                                                 a[:, :PAST].rearrange("q (k r) -> q k r", r=16), -1.0, -NEG, ALU.add, ALU.mult))
                    link(nc.vector.tensor_scalar(X["mask_s"][:, PAST:], a[:, PAST:], -1.0, -NEG, ALU.add, ALU.mult))


def make_bias(nc, S, T):
    LP, LS = SEQ + P, PAST + 2 * DS
    HOT = PAST + DS + P
    with ExitStack() as ctx:
        sb = lambda n, s, d=F32: ctx.enter_context(nc.sbuf_tensor("b_" + n, s, d))
        sem = stage_semaphores(nc, ctx, "b_")
        rb = sb("rb", [32, H])
        rep = sb("rep", [32, H, P])
        rep_s = sb("rep_s", [32, H, DS])
        hot = sb("hot", [32, HOT])
        row = sb("row", [P, 2, LP])
        row_s = sb("row_s", [NS, LS])
        ps = ctx.enter_context(nc.psum_tensor("b_ps", [P, 2, 512], F32))
        loaded, spread, ready, taken = sem("loaded"), sem("spread"), sem("ready"), sem("taken")
        wrote = [sem(f"wrote{j}") for j in range(2)]
        read, wrote_s = sem("read"), sem("wrote_s")
        block = ctx.enter_context(nc.Block())
        first = PAST + DS - SEQ
        jobs = [(h, a, min(512, LP - a)) for h in range(H) for a in range(0, LP, 512)]
        jobs_s = [(a, min(512, LS - a)) for a in range(0, LS, 512)]

        @block.sync
        def _(sp):
            sp.dma_start(rb[:, :], S["rel_bias"]).then_inc(loaded, 16)
            sp.dma_start(hot[:, :], S["c_onehot"]).then_inc(loaded, 16)
            per = len(jobs) // H
            for h in range(H):
                sp.wait_ge(taken, per * (h + 1))
                sp.dma_start(S["skew"][h], row[:, h % 2, :]).then_inc(wrote[h % 2], 16)
            sp.wait_ge(taken, len(jobs) + len(jobs_s))
            sp.dma_start(S["skew_s"], row_s[:, :]).then_inc(wrote_s, 16)
            for j in range(2):
                sp.wait_ge(wrote[j], 16 * (H // 2))
            for h in range(H):
                src = S["skew"][h].rearrange("p l -> (p l)")
                src = src[P - 1:P - 1 + P * (LP - 1)].rearrange("(p l) -> p l", l=LP - 1)[:, :SEQ]
                sp.dma_start(T["bias"][:, h, :], src).then_inc(read, 16)
            sp.wait_ge(wrote_s, 16)
            sp.wait_ge(read, 16 * H)

        @block.tensor
        def _(pe):
            pe.wait_ge(spread, 2)
            for j, (h, a, n) in enumerate(jobs):
                if j >= 2:
                    pe.wait_ge(taken, j - 1)
                nc.tensor.matmul(ps[:, j % 2, :n], rep[:, h, :], hot[:, first + a:first + a + n],
                                 start=True, stop=True).then_inc(ready, 1)
            for q, (a, n) in enumerate(jobs_s):
                j = len(jobs) + q
                pe.wait_ge(taken, j - 1)
                nc.tensor.matmul(ps[:NS, j % 2, :n], rep_s[:, :, :].rearrange("k h t -> k (h t)"), hot[:, a:a + n],
                                 start=True, stop=True).then_inc(ready, 1)

        @block.scalar
        def _(act):
            for j, (h, a, n) in enumerate(jobs):
                act.wait_ge(ready, j + 1)
                if a == 0 and h >= 2:
                    act.wait_ge(wrote[h % 2], 16 * (h // 2))
                nc.scalar.activation(row[:, h % 2, a:a + n], ps[:, j % 2, :n], ACT.Copy).then_inc(taken, 1)
            for q, (a, n) in enumerate(jobs_s):
                j = len(jobs) + q
                act.wait_ge(ready, j + 1)
                nc.scalar.activation(row_s[:, a:a + n], ps[:NS, j % 2, :n], ACT.Copy).then_inc(taken, 1)

        @block.vector
        def _(dve):
            dve.wait_ge(loaded, 32)
            nc.vector.tensor_copy(rep[:, :, :], rb[:, :].unsqueeze(2).to_broadcast([32, H, P])).then_inc(spread, 1)
            nc.vector.tensor_copy(rep_s[:, :, :], rb[:, :].unsqueeze(2).to_broadcast([32, H, DS])).then_inc(spread, 1)


def prompt_attention(nc, A, X, T):
    units = [(i, h) for i in range(NT) for h in range(H)]
    turns = [(u, b0, min(4, units[u][0] + 1 - b0)) for u in range(len(units)) for b0 in range(0, units[u][0] + 1, 4)]
    turns_before = [sum(1 for t in turns if t[0] < u) for u in range(len(units) + 1)]
    with ExitStack() as ctx:
        sb = lambda n, s, d=F32: ctx.enter_context(nc.sbuf_tensor("a_" + n, s, d))
        sem = stage_semaphores(nc, ctx, "a_")
        logit = sb("logit", [P, 2, SEQ])
        prob = sb("prob", [P, 2, SEQ])
        probT = sb("probT", [P, 2, NT, P])
        peak = sb("peak", [P, 2])
        neg = sb("neg", [P, 2])
        total = sb("total", [P, 2, H])
        inv = sb("inv", [P, H])
        o = sb("o", [P, 2, W])
        psS = [ctx.enter_context(nc.psum_tensor(f"a_psS{j}", [P, SEQ], F32)) for j in range(2)]
        psT = ctx.enter_context(nc.psum_tensor("a_psT", [P, 2, 4, P], F32))
        psO = ctx.enter_context(nc.psum_tensor("a_psO", [P, W], F32))
        psA = ctx.enter_context(nc.psum_tensor("a_psA", [P, PAIRS, P], F32))
        s_ready, l_ready, neg_ready, p_ready = sem("s_ready"), sem("l_ready"), sem("neg_ready"), sem("p_ready")
        turned, t_taken, o_ready, o_scaled = sem("turned"), sem("t_taken"), sem("o_ready"), sem("o_scaled")
        a_ready, a_taken, dve_done = sem("a_ready"), sem("a_taken"), sem("dve_done")
        block = ctx.enter_context(nc.Block())

        @block.tensor
        def _(pe):
            def scores(u):
                i, h = units[u]
                half = slice(h % 2 * HD, h % 2 * HD + HD)
                if u >= 2:
                    pe.wait_ge(l_ready, u - 1)
                for k0 in range(0, (i + 1) * P, 512):
                    n = min(512, (i + 1) * P - k0)
                    diagonal = i < TOPK // P and k0 + n == (i + 1) * P
                    masked = i >= TOPK // P or diagonal
                    mm = nc.tensor.matmul(psS[u % 2][:, k0:k0 + n], A["qaT"][half, h // 2, cols_of(i)],
                                          A["kaT"][half, h // 2, k0:k0 + n], start=True, stop=not masked,
                                          skip_group_check=True)
                    if diagonal:
                        mm = nc.tensor.matmul(psS[u % 2][:, i * P:(i + 1) * P], A["identity_b"][:, :], A["causal_b"][:, :],
                                              start=False, stop=True, skip_group_check=True)
                    elif masked:
                        mm = nc.tensor.matmul(psS[u % 2][:, k0:k0 + n], A["identity_b"][:, :], X["mask"](i)[:, k0:k0 + n],
                                              start=False, stop=True, skip_group_check=True)
                mm.then_inc(s_ready, 1)

            def turn(u):
                pe.wait_ge(p_ready, u + 1)
                for t in range(turns_before[u], turns_before[u + 1]):
                    _, b0, nb = turns[t]
                    if t >= 2:
                        pe.wait_ge(t_taken, t - 1)
                    for b in range(nb):
                        mm = nc.tensor.transpose(psT[:, t % 2, b, :], prob[:, u % 2, (b0 + b) * P:(b0 + b + 1) * P],
                                                 A["identity"][:, :])
                    mm.then_inc(turned, 1)

            def values(u):
                i, h = units[u]
                pe.wait_ge(t_taken, turns_before[u + 1])
                if h == 0 and i:
                    pe.wait_ge(o_scaled, i)
                for b in range(i + 1):
                    mm = nc.tensor.matmul(psO[:, h * HD:(h + 1) * HD], probT[:, u % 2, b, :], A["va"][:, b, h * HD:(h + 1) * HD],
                                          start=(b == 0), stop=(b == i))
                if h == H - 1:
                    mm.then_inc(o_ready, 1)

            def turn_out(i):
                pe.wait_ge(o_scaled, i + 1)
                if i:
                    pe.wait_ge(a_taken, i)
                for b in range(PAIRS):
                    mm = nc.tensor.transpose(psA[:, b, :], o[:, i % 2, b * P:(b + 1) * P], A["identity"][:, :])
                mm.then_inc(a_ready, 1)

            scores(0)
            for u in range(len(units)):
                if u + 1 < len(units):
                    scores(u + 1)
                turn(u)
                if u:
                    values(u - 1)
                if units[u][1] == 2 and units[u][0]:
                    turn_out(units[u][0] - 1)
            values(len(units) - 1)
            turn_out(NT - 1)

        def take(act, u):
            for t in range(turns_before[u], turns_before[u + 1]):
                _, b0, nb = turns[t]
                act.wait_ge(turned, t + 1)
                nc.scalar.activation(probT[:, u % 2, b0:b0 + nb, :], psT[:, t % 2, :nb, :], ACT.Copy).then_inc(t_taken, 1)

        def take_out(act, i):
            act.wait_ge(a_ready, i + 1)
            nc.scalar.activation(A["attT"][:, :, cols_of(i)], psA[:, :, :], ACT.Copy).then_inc(a_taken, 1)

        @block.scalar
        def _(act):
            for u, (i, h) in enumerate(units):
                n = (i + 1) * P
                act.wait_ge(neg_ready, u + 1)
                if u >= 2:
                    act.wait_ge(turned, turns_before[u - 1])
                if h == 0 and i >= 2:
                    act.wait_ge(o_scaled, i - 1)
                nc.scalar.activation(prob[:, u % 2, :n], logit[:, u % 2, :n], ACT.Exp, bias=neg[:, u % 2:u % 2 + 1],
                                     accum_out=total[:, i % 2, h:h + 1]).then_inc(p_ready, 1)
                if u:
                    take(act, u - 1)
                if h == 3 and i:
                    take_out(act, i - 1)
            take(act, len(units) - 1)
            take_out(act, NT - 1)

        @block.vector
        def _(dve):
            link = Chain(dve, dve_done)

            def scale_out(i):
                dve.wait_ge(o_ready, i + 1)
                link(nc.vector.reciprocal(inv[:, :], total[:, i % 2, :]))
                if i >= 2:
                    dve.wait_ge(a_ready, i - 1)
                nc.vector.tensor_tensor(o[:, i % 2, :].rearrange("p (h e) -> p h e", h=H),
                                        psO[:, :].rearrange("p (h e) -> p h e", h=H),
                                        inv[:, :].unsqueeze(2).to_broadcast([P, H, HD]), ALU.mult).then_inc(o_scaled, 1)

            for u, (i, h) in enumerate(units):
                n, off = (i + 1) * P, SEQ - (i + 1) * P
                dve.wait_ge(s_ready, u + 1)
                if u >= 2:
                    dve.wait_ge(p_ready, u - 1)
                nc.vector.tensor_tensor_reduce(logit[:, u % 2, :n], psS[u % 2][:, :n], T["bias"][:, h, off:off + n],
                                               1.0, NEG, ALU.add, ALU.max, peak[:, u % 2:u % 2 + 1]).then_inc(l_ready, 1)
                dve.wait_ge(l_ready, u + 1)
                nc.vector.tensor_scalar(neg[:, u % 2:u % 2 + 1], peak[:, u % 2:u % 2 + 1], -1.0, None, ALU.mult).then_inc(neg_ready, 1)
                if h == 1 and i:
                    scale_out(i - 1)
            scale_out(NT - 1)


def sample_attention(nc, S, A, X):
    R = 16
    loads = [(kind, b - (kind == "v"), c) for b in range(DB + 1) for kind in "kv" for c in range(4)]
    loads = [(kind, b, c) for kind, b, c in loads if 0 <= b < DB]
    index = {load: n for n, load in enumerate(loads)}
    strip = lambda pr: slice(32 * pr, 32 * pr + 32)
    pair = lambda pr: slice(pr * P, (pr + 1) * P)
    with ExitStack() as ctx:
        sb = lambda n, s, d=F32: ctx.enter_context(nc.sbuf_tensor("s_" + n, s, d))
        sem = stage_semaphores(nc, ctx, "s_")
        ring = sb("ring", [P, PAGE_RING, 4, W])
        kcT = sb("kcT", [P, 2, PAIRS, 512])
        logit = sb("logit", [P, NK])
        probT = sb("probT", [P, R + 1, P])
        qd = sb("qd", [P, 2, PAIRS, 32])
        st = sb("st", [P, 2, 4])
        bias = sb("bias", [P, NK])
        o_rows = sb("o_rows", [P, P])
        psK = ctx.enter_context(nc.psum_tensor("s_psK", [P, 2, 512], F32))
        psS = ctx.enter_context(nc.psum_tensor("s_psS", [P, 5 * 512], F32))
        psV = ctx.enter_context(nc.psum_tensor("s_psV", [P, 512], F32))
        slot_loaded = [sem(f"slot{j}_loaded") for j in range(PAGE_RING)]
        zeroed, q_spread = sem("zeroed"), sem("q_spread")
        k_turned, k_scored, s_ready, l_ready = sem("k_turned"), sem("k_scored"), sem("s_ready"), sem("l_ready")
        k_taken = [sem("k_taken_by_act"), sem("k_taken_by_dve")]
        neg_ready, e_ready, p_turned, p_taken = sem("neg_ready"), sem("e_ready"), sem("p_turned"), sem("p_taken")
        o_ready, o_normed, o_turned, o_taken = sem("o_ready"), sem("o_normed"), sem("o_turned"), sem("o_taken")
        dve_done, bias_loaded = sem("dve_done"), sem("bias_loaded")
        block = ctx.enter_context(nc.Block())

        @block.sync
        def _(sp):
            L = PAST + 2 * DS
            sp.wait_ge(zeroed, 3)
            for h in range(H):
                src = S["skew_s"][h * DS:(h + 1) * DS, :].rearrange("p l -> (p l)")
                src = src[DS - 1:DS - 1 + DS * (L - 1)].rearrange("(p l) -> p l", l=L - 1)
                row = 32 * (h // 2) + DS * (h % 2)
                sp.dma_start(logit[row:row + DS, :PAST + DS], src[:, :PAST + DS]).then_inc(bias_loaded, 16)

        @block.gpsimd
        def _(pool):
            for n, (kind, b, c) in enumerate(loads):
                if n >= PAGE_RING:
                    was, wb, wc = loads[n - PAGE_RING]
                    if was == "k":
                        pool.wait_ge(k_turned, 16 * wb + 4 * wc + 4)
                    else:
                        pool.wait_ge(o_ready, wb + 1)
                pool.indirect_dma_start(ring[:, n % PAGE_RING, :, :].rearrange("p r e -> p (r e)"), None, S["cache_" + kind],
                                        bass.IndirectOffsetOnAxis(ap=A["quarter_id"][:, c, b:b + 1], axis=0)
                                        ).then_inc(slot_loaded[n % PAGE_RING], 16)

        @block.tensor
        def _(pe):
            def slot_of(kind, b, c):
                n = index[kind, b, c]
                pe.wait_ge(slot_loaded[n % PAGE_RING], 16 * (n // PAGE_RING + 1))
                return n % PAGE_RING

            def turn_keys(b, c):
                slot = slot_of("k", b, c)
                for pr in range(PAIRS):
                    q = 16 * b + 4 * c + pr
                    if q >= 2:
                        pe.wait_ge(k_taken[q % 2], q // 2)
                    for r in range(4):
                        mm = nc.tensor.transpose(psK[:, q % 2, r * P:(r + 1) * P], ring[:, slot, r, pair(pr)], A["identity"][:, :])
                    mm.then_inc(k_turned, 1)

            def score(b, c):
                cols = slice(c * 512, (c + 1) * 512) if c < 4 else slice(PAST, NK)
                if c == 0 and b:
                    pe.wait_ge(l_ready, b)
                if c < 4:
                    for j in range(2):
                        pe.wait_ge(k_taken[j], 2 * (4 * b + c) + 2)
                nc.tensor.matmul(psS[:, cols], A["own_rows"][:, b, :], X["mask_s"][:, cols],
                                 start=True, stop=False, skip_group_check=True)
                for pr in range(PAIRS):
                    keys = kcT[:, c % 2, pr, :] if c < 4 else A["kaT_s"][:, pr, :]
                    mm = nc.tensor.matmul(psS[strip(pr), cols], qd[:, b % 2, pr, :], keys, start=False, stop=(pr == PAIRS - 1),
                                          tile_position=(0, 32 * pr), skip_group_check=True)
                mm.then_inc(k_scored if c < 4 else s_ready, 1)

            def turn_probs(b, t):
                pe.wait_ge(e_ready, b + 1)
                if b or t:
                    pe.wait_ge(p_taken, 5 * b + t)
                if t == 0 and b:
                    pe.wait_ge(o_taken, b)
                for r in range(4 if t < 4 else 1):
                    k = 4 * t + r
                    rows = P if k < R else NS
                    mm = nc.tensor.transpose(psV[:rows, r * P:(r + 1) * P], logit[:, k * P:k * P + rows], A["identity"][:, :])
                mm.then_inc(p_turned, 1)

            def sum_values(b):
                slot = [slot_of("v", b, c) for c in range(4)]
                pe.wait_ge(p_taken, 5 * b + 5)
                for r in range(R + 1):
                    for pr in range(PAIRS):
                        rows = P if r < R else NS
                        value = ring[:, slot[r // 4], r % 4, pair(pr)] if r < R else A["va_s"][:NS, pair(pr)]
                        mm = nc.tensor.matmul(psV[strip(pr), :P], probT[:rows, r, strip(pr)], value,
                                              start=(r == 0), stop=(r == R), tile_position=(0, 32 * pr), skip_group_check=True)
                mm.then_inc(o_ready, 1)

            def turn_output(b):
                pe.wait_ge(o_normed, b + 1)
                nc.tensor.transpose(psV[:, P:2 * P], o_rows[:, :], A["identity"][:, :]).then_inc(o_turned, 1)

            for b in range(DB + 1):
                if b < DB:
                    turn_keys(b, 0)
                if b >= 2:
                    turn_output(b - 2)
                if b < DB:
                    pe.wait_ge(q_spread, b + 1)
                for c in range(4):
                    if b < DB and c < 3:
                        turn_keys(b, c + 1)
                    if b:
                        turn_probs(b - 1, c)
                    if b < DB:
                        score(b, c)
                if b:
                    turn_probs(b - 1, 4)
                if b < DB:
                    score(b, 4)
                if b:
                    sum_values(b - 1)
            turn_output(DB - 1)

        @block.scalar
        def _(act):
            for b in range(DB):
                for c in range(4):
                    n = 4 * b + c
                    for pr in (0, 2):
                        act.wait_ge(k_turned, 16 * b + 4 * c + pr + 1)
                        if n >= 2:
                            act.wait_ge(k_scored, n - 1)
                        nc.scalar.activation(kcT[:, c % 2, pr, :], psK[:, 0, :], ACT.Copy).then_inc(k_taken[0], 1)
                act.wait_ge(neg_ready, b + 1)
                nc.scalar.activation(logit[:, :], logit[:, :], ACT.Exp, bias=st[:, b % 2, 1:2], accum_out=st[:, b % 2, 2:3]
                                     ).then_inc(e_ready, 1)

        @block.vector
        def _(dve):
            link = Chain(dve, dve_done)
            for j in range(2):
                nc.vector.memset(qd[:, j, :, :], 0.0).then_inc(zeroed, 1)
            nc.vector.memset(logit[:, :], 0.0).then_inc(zeroed, 1)
            dve.wait_ge(zeroed, 3)

            def spread_q(b):
                for hh in range(2):
                    half = slice(hh * HD, (hh + 1) * HD)
                    ins = nc.vector.tensor_copy(qd[half, b % 2, :, hh * DS:(hh + 1) * DS],
                                                A["qaT_s"][half, :, b * DS:(b + 1) * DS])
                ins.then_inc(q_spread, 1)

            def take_keys(b, c):
                n = 4 * b + c
                for pr in (1, 3):
                    dve.wait_ge(k_turned, 16 * b + 4 * c + pr + 1)
                    if n >= 2:
                        dve.wait_ge(k_scored, n - 1)
                    nc.vector.tensor_copy(kcT[:, c % 2, pr, :], psK[:, 1, :]).then_inc(k_taken[1], 1)

            def take_probs(b, t):
                n, rows = (4, P) if t < 4 else (1, NS)
                dve.wait_ge(p_turned, 5 * b + t + 1)
                if t == 0 and b:
                    dve.wait_ge(o_ready, b)
                nc.vector.tensor_copy(probT[:rows, 4 * t:4 * t + n, :],
                                      psV[:rows, :n * P].rearrange("p (r q) -> p r q", r=n)).then_inc(p_taken, 1)

            def norm_output(b):
                dve.wait_ge(o_ready, b + 1)
                if b:
                    dve.wait_ge(o_turned, b)
                nc.vector.tensor_scalar(o_rows[:, :], psV[:, :P], st[:, b % 2, 3:4], None, ALU.mult).then_inc(o_normed, 1)

            def take_output(b):
                dve.wait_ge(o_turned, b + 1)
                for hh in range(2):
                    half = slice(hh * HD, (hh + 1) * HD)
                    ins = nc.vector.tensor_copy(
                        A["attT"][half, :, SEQ + b * DS:SEQ + (b + 1) * DS],
                        psV[half, P:2 * P].rearrange("p (pr x) -> p pr x", pr=PAIRS)[:, :, hh * DS:(hh + 1) * DS])
                ins.then_inc(o_taken, 1)

            spread_q(0)
            for b in range(DB + 1):
                if b >= 2:
                    norm_output(b - 2)
                if b < DB:
                    take_keys(b, 0)
                if b == 0:
                    dve.wait_ge(bias_loaded, 16 * H)
                    link(nc.vector.tensor_copy(bias[:, :PAST].rearrange("q (r k) -> q k r", r=R),
                                               logit[:, :PAST].rearrange("q (k r) -> q k r", r=R)))
                    link(nc.vector.tensor_copy(bias[:, PAST:].rearrange("q (b t) -> q b t", b=DB),
                                               logit[:, PAST:PAST + DS].unsqueeze(1).to_broadcast([P, DB, DS])))
                if b >= 2:
                    take_output(b - 2)
                for c in range(4):
                    if b < DB and c < 3:
                        take_keys(b, c + 1)
                    if b and c == 0:
                        dve.wait_ge(e_ready, b)
                        link(nc.vector.reciprocal(st[:, (b - 1) % 2, 3:4], st[:, (b - 1) % 2, 2:3]))
                    if b:
                        take_probs(b - 1, c)
                if b:
                    take_probs(b - 1, 4)
                if b + 1 < DB:
                    if b:
                        dve.wait_ge(s_ready, b)
                    spread_q(b + 1)
                if b < DB:
                    dve.wait_ge(s_ready, b + 1)
                    nc.vector.tensor_tensor_reduce(logit[:, :], psS[:, :NK], bias[:, :], 1.0, NEG, ALU.add, ALU.max,
                                                   st[:, b % 2, 0:1]).then_inc(l_ready, 1)
                    dve.wait_ge(l_ready, b + 1)
                    nc.vector.tensor_scalar(st[:, b % 2, 1:2], st[:, b % 2, 0:1], -1.0, None, ALU.mult).then_inc(neg_ready, 1)
            norm_output(DB - 1)
            take_output(DB - 1)


def output_projection(nc, S, A):
    with ExitStack() as ctx:
        sb = lambda n, s, d=F32: ctx.enter_context(nc.sbuf_tensor("o_" + n, s, d))
        sem = stage_semaphores(nc, ctx, "o_")
        w = sb("w", [P, KD, D])
        x = sb("x", [P, 3, D])
        h = sb("h", [P, 2, D])
        ps = ctx.enter_context(nc.psum_tensor("o_ps", [P, 2, D], F32))
        w_loaded, y_ready, h_ready = sem("w_loaded"), sem("y_ready"), sem("h_ready")
        x_loaded = [sem(f"x_loaded{j}") for j in range(3)]
        h_stored = [sem(f"h_stored{j}") for j in range(2)]
        block = ctx.enter_context(nc.Block())

        @block.sync
        def _(sp):
            sp.dma_start(w[:, :, :], S["w_out"].rearrange("(k p) n -> p k n", p=P)).then_inc(w_loaded, 16)
            for i in range(TILES):
                if i >= 3:
                    sp.wait_ge(h_ready, i - 2)
                sp.dma_start(x[:rows_of(i), i % 3, :], S["x_rows"](i)).then_inc(x_loaded[i % 3], 16)

        @block.tensor
        def _(pe):
            pe.wait_ge(w_loaded, 16)
            for i in range(TILES):
                n = rows_of(i)
                if i >= 2:
                    pe.wait_ge(h_ready, i - 1)
                for half in range(2):
                    for k in range(KD):
                        src = A["attT"][:, k, cols_of(i)] if k < PAIRS else A["retT"][:, k - PAIRS, cols_of(i)]
                        mm = nc.tensor.matmul(ps[:n, i % 2, half * 512:(half + 1) * 512], src, w[:, k, half * 512:(half + 1) * 512],
                                              start=(k == 0), stop=(k == KD - 1))
                mm.then_inc(y_ready, 1)

        @block.vector
        def _(dve):
            for i in range(TILES):
                n = rows_of(i)
                dve.wait_ge(y_ready, i + 1)
                dve.wait_ge(x_loaded[i % 3], 16 * (i // 3 + 1))
                if i >= 2:
                    dve.wait_ge(h_stored[i % 2], 16 * (i // 2))
                nc.vector.tensor_tensor(h[:n, i % 2, :], ps[:n, i % 2, :], x[:n, i % 3, :], ALU.add).then_inc(h_ready, 1)

        @block.gpsimd
        def _(pool):
            for i in range(TILES):
                pool.wait_ge(h_ready, i + 1)
                pool.dma_start(S["h"][cols_of(i), :], h[:rows_of(i), i % 2, :]).then_inc(h_stored[i % 2], 16)
            pool.wait_ge(h_stored[0], 16 * ((TILES + 1) // 2))
            pool.wait_ge(h_stored[1], 16 * (TILES // 2))


def route(nc, S, A, M):
    NR = NG + NE
    with ExitStack() as ctx:
        sb = lambda n, s, d=F32: ctx.enter_context(nc.sbuf_tensor("g_" + n, s, d))
        sem = stage_semaphores(nc, ctx, "g_")
        wr = sb("wr", [P, KD, NR])
        lg = sb("lg", [P, TILES, NR])
        a4 = sb("a4", [P, TILES, NG])
        g_hot = sb("g_hot", [P, TILES, NG])
        prod = sb("prod", [P, TILES, NE])
        el = sb("el", [P, TILES, EPG])
        a8 = sb("a8", [P, TILES, EPG])
        hot = sb("hot", [P, 2, TILES, EPG])
        s9 = sb("s9", [P, 12, TILES])
        pick = sb("pick", [P, 2, TILES, NE])
        both = sb("both", [P, TILES, NE], BF16)
        rank = sb("rank", [P, TILES + 1, NE])
        over = sb("over", [P, 4, NE])
        cmp_t = sb("cmp_t", [P, NE, MULTIPLES])
        ovx = sb("ovx", [P, OVER])
        zeros = sb("zeros", [P, -(-SLOTS * CAP // P)], U32)
        tok = sb("tok", [P, TILES], U32)
        ps = ctx.enter_context(nc.psum_tensor("g_ps", [P, TILES * NR], F32))
        psR = ctx.enter_context(nc.psum_tensor("g_psR", [P, (TILES + 1) * NE], F32))
        loaded, lg_ready, both_ready, rank_ready = sem("loaded"), sem("lg_ready"), sem("both_ready"), sem("rank_ready")
        dve_done, act_in, act_out, pos_ready = sem("dve_done"), sem("act_in"), sem("act_out"), sem("pos_ready")
        zeroed, tok_ready, cleared, read = sem("zeroed"), sem("tok_ready"), sem("cleared"), sem("read")
        listed = [sem(f"listed{j}") for j in range(6)]
        block = ctx.enter_context(nc.Block())

        @block.sync
        def _(sp):
            with nc.allow_non_contiguous_dma(reason="narrow router weights"):
                sp.dma_start(wr[:, :, :NG], S["w_group"].rearrange("(k p) n -> p k n", p=P)).then_inc(loaded, 16)
                sp.dma_start(wr[:, :, NG:], S["w_expert"].rearrange("(k p) n -> p k n", p=P)).then_inc(loaded, 16)
            sp.wait_ge(cleared, 16)
            for j in range(6):
                sp.wait_ge(listed[j], 16 * (2 * TILES // 6))
            with nc.allow_non_contiguous_dma(reason="one token id per partition"):
                sp.dma_start(M["token"][:, :], S["token_list"][:SLOTS * CAP, :].rearrange("(s c) o -> c (s o)", c=CAP)
                             ).then_inc(read, 16)
            sp.wait_ge(read, 16)

        @block.tensor
        def _(pe):
            pe.wait_ge(loaded, 32)
            for i in range(TILES):
                n = rows_of(i)
                for k in range(KD):
                    mm = nc.tensor.matmul(ps[:n, i * NR:(i + 1) * NR], A["uT"][:, k, cols_of(i)], wr[:, k, :],
                                          start=(k == 0), stop=(k == KD - 1), skip_group_check=True)
            mm.then_inc(lg_ready, 1)
            pe.wait_ge(both_ready, 1)
            for i in range(TILES + 1):
                n = rows_of(i) if i < TILES else P
                out = psR[:n, i * NE:(i + 1) * NE]
                last = i == TILES
                for j in range(i):
                    m = rows_of(j)
                    mm = nc.tensor.matmul(out, A["ones_b"][:m, :n], both[:m, j, :], start=(j == 0), stop=(last and j == i - 1),
                                          skip_group_check=True)
                if not last:
                    mm = nc.tensor.matmul(out, A["above_b"][:n, :n], both[:n, i, :], start=(i == 0), stop=True,
                                          skip_group_check=True)
            mm.then_inc(rank_ready, 1)

        @block.scalar
        def _(act):
            act.wait_ge(act_in, 1)
            nc.scalar.activation(a4[:, :, :], a4[:, :, :], ACT.Exp).then_inc(act_out, 1)
            act.wait_ge(act_in, 2)
            nc.scalar.activation(s9[:, 4, :], s9[:, 3, :], ACT.Exp).then_inc(act_out, 1)

        @block.gpsimd
        def _(pool):
            nc.gpsimd.memset(zeros[:, :], 0).then_inc(zeroed, 1)
            nc.gpsimd.iota(tok[:, :], [[P, TILES]], base=0, channel_multiplier=1).then_inc(tok_ready, 1)
            pool.wait_ge(zeroed, 1)
            pool.dma_start(S["token_list"].rearrange("(p n) o -> p (n o)", p=P), zeros[:, :]).then_inc(cleared, 16)
            pool.wait_ge(cleared, 16)
            pool.wait_ge(tok_ready, 1)
            pool.wait_ge(pos_ready, 1)
            for i in range(TILES):
                for c in range(2):
                    n, q = rows_of(i), 2 * i + c
                    if q >= 6:
                        pool.wait_ge(listed[q % 6], 16 * (q // 6))
                    pool.indirect_dma_start(S["token_list"], bass.IndirectOffsetOnAxis(ap=M["pos"][:n, c, i:i + 1], axis=0),
                                            tok[:n, i:i + 1], None).then_inc(listed[q % 6], 16)
            for j in range(6):
                pool.wait_ge(listed[j], 16 * (2 * TILES // 6))

        @block.vector
        def _(dve):
            link = Chain(dve, dve_done)
            V = nc.vector
            link(V.memset(lg[:, :, :], 0.0))
            link(V.memset(rank[:, :, :], 0.0))
            dve.wait_ge(lg_ready, 1)
            lp = ps[:, :].rearrange("p (i n) -> p i n", i=TILES)
            link(V.tensor_copy(lg[:, :NT, :], lp[:, :NT, :]))
            link(V.tensor_copy(lg[:NS, NT, :], lp[:NS, NT, :]))
            wide = lambda a, n: a.unsqueeze(2).to_broadcast([P, TILES, n])
            tiles = lambda a, n: a.unsqueeze(1).to_broadcast([P, TILES, n])

            def first_of_max(hot_out, values, peak, scratch, n):
                link(V.tensor_reduce(peak, values, AX_X, ALU.max))
                link(V.tensor_tensor(scratch, values, wide(peak, n), ALU.is_ge))
                link(V.tensor_tensor(scratch, scratch, tiles(A["countdown"][:, EPG - n:], n), ALU.mult))
                link(V.tensor_reduce(s9[:, 11, :], scratch, AX_X, ALU.max))
                link(V.tensor_tensor(hot_out, tiles(A["countdown"][:, EPG - n:], n), wide(s9[:, 11, :], n), ALU.is_equal))

            first_of_max(g_hot[:, :, :], lg[:, :, :NG], s9[:, 0, :], a4[:, :, :], NG)
            V.tensor_tensor(a4[:, :, :], lg[:, :, :NG], wide(s9[:, 0, :], NG), ALU.subtract).then_inc(act_in, 1)
            g3 = g_hot[:, :, :].unsqueeze(3).to_broadcast([P, TILES, NG, EPG])
            link(V.tensor_tensor(prod[:, :, :].rearrange("p i (g e) -> p i g e", g=NG),
                                 lg[:, :, NG:].rearrange("p i (g e) -> p i g e", g=NG), g3, ALU.mult))
            link(V.tensor_reduce(el[:, :, :], prod[:, :, :].rearrange("p i (g e) -> p i e g", g=NG), AX_X, ALU.add))
            first_of_max(hot[:, 0, :, :], el[:, :, :], s9[:, 1, :], a8[:, :, :], EPG)
            link(V.tensor_scalar(a8[:, :, :], hot[:, 0, :, :], NEG, None, ALU.mult))
            link(V.tensor_tensor(el[:, :, :], el[:, :, :], a8[:, :, :], ALU.add))
            first_of_max(hot[:, 1, :, :], el[:, :, :], s9[:, 2, :], a8[:, :, :], EPG)
            V.tensor_tensor(s9[:, 3, :], s9[:, 2, :], s9[:, 1, :], ALU.subtract).then_inc(act_in, 1)
            for c in range(2):
                link(V.tensor_tensor(pick[:, c, :, :].rearrange("p i (g e) -> p i g e", g=NG), g3,
                                     hot[:, c, :, :].unsqueeze(2).to_broadcast([P, TILES, NG, EPG]), ALU.mult))
            V.tensor_tensor(both[:, :, :], pick[:, 0, :, :], pick[:, 1, :, :], ALU.add).then_inc(both_ready, 1)
            dve.wait_ge(act_out, 2)
            link(V.tensor_reduce(s9[:, 5, :], a4[:, :, :], AX_X, ALU.add))
            link(V.tensor_scalar(s9[:, 6, :], s9[:, 4, :], 1.0, None, ALU.add))
            link(V.tensor_tensor(s9[:, 5, :], s9[:, 5, :], s9[:, 6, :], ALU.mult))
            link(V.reciprocal(M["weight"][:, 0, :], s9[:, 5, :]))
            link(V.tensor_tensor(M["weight"][:, 1, :], M["weight"][:, 0, :], s9[:, 4, :], ALU.mult))
            dve.wait_ge(rank_ready, 1)
            rp = psR[:, :].rearrange("p (i e) -> p i e", e=NE)
            link(V.tensor_copy(rank[:, :NT, :], rp[:, :NT, :]))
            link(V.tensor_copy(rank[:NS, NT, :], rp[:NS, NT, :]))
            link(V.tensor_copy(rank[:, TILES, :], rp[:, TILES, :]))
            link(V.tensor_tensor(cmp_t[:, :, :], rank[:, TILES, :].unsqueeze(2).to_broadcast([P, NE, MULTIPLES]),
                                 A["cap_multiples"][:, :].unsqueeze(1).to_broadcast([P, NE, MULTIPLES]), ALU.is_gt))
            link(V.tensor_reduce(over[:, 0, :], cmp_t[:, :, :], AX_X, ALU.add))
            link(V.tensor_tensor_scan(over[:, 1, :], over[:, 0, :], over[:, 0, :], 0.0, ALU.add, ALU.max))
            link(V.tensor_tensor(over[:, 2, :], over[:, 1, :], over[:, 0, :], ALU.subtract))
            link(V.tensor_scalar(over[:, 3, :], over[:, 2, :], float(NE - 1), None, ALU.add))
            link(V.tensor_tensor(over[:, 3, :], over[:, 3, :], A["expert_id"][:, :], ALU.subtract))
            for c in range(2):
                def chosen(out, table):
                    link(V.tensor_tensor(prod[:, :, :], pick[:, c, :, :], table, ALU.mult))
                    link(V.tensor_reduce(out, prod[:, :, :], AX_X, ALU.add))
                chosen(s9[:, 7, :], rank[:, :TILES, :])
                chosen(s9[:, 8, :], A["expert_id"][:, :].unsqueeze(1).to_broadcast([P, TILES, NE]))
                chosen(s9[:, 9, :], over[:, 3, :].unsqueeze(1).to_broadcast([P, TILES, NE]))
                link(V.tensor_scalar(s9[:, 10, :], s9[:, 7, :], float(CAP), None, ALU.is_ge))
                link(V.tensor_tensor(s9[:, 9, :], s9[:, 9, :], s9[:, 10, :], ALU.mult))
                link(V.tensor_tensor(s9[:, 8, :], s9[:, 8, :], s9[:, 9, :], ALU.add))
                link(V.tensor_scalar(s9[:, 8, :], s9[:, 8, :], float(CAP), None, ALU.mult))
                link(V.tensor_tensor(s9[:, 8, :], s9[:, 8, :], s9[:, 7, :], ALU.add))
                link(V.tensor_copy(M["pos"][:, c, :], s9[:, 8, :]))
            link(V.tensor_copy(M["over_count"][:, :], over[:, 1, NE - 1:NE]))
            for v in range(OVER):
                link(V.tensor_scalar(prod[:, 0, :], over[:, 1, :], float(v), None, ALU.is_le, ALU.add, accum_out=ovx[:, v:v + 1]))
            link(V.tensor_scalar(ovx[:, :], ovx[:, :], float(NE - 1), None, ALU.min))
            V.tensor_copy(M["over_expert"][:, :], ovx[:, :]).then_inc(pos_ready, 1)


def experts(nc, S, A, M):
    RING = 4
    K2 = DE // P
    with ExitStack() as ctx:
        sb = lambda n, s, d=F32: ctx.enter_context(nc.sbuf_tensor("e_" + n, s, d))
        sem = stage_semaphores(nc, ctx, "e_")
        wg = sb("wg", [P, RING, KD, DE])
        wu = sb("wu", [P, RING, KD, DE])
        wd = sb("wd", [P, RING, K2, D])
        xg = sb("xg", [CAP, RING, D])
        ids = sb("ids", [CAP, RING], U32)
        xT = sb("xT", [P, 2, KD, CAP])
        gate = sb("gate", [P, 2, K2, CAP])
        hT = sb("hT", [P, 2, K2, CAP])
        y = sb("y", [CAP, 2, D])
        psX = ctx.enter_context(nc.psum_tensor("e_psX", [P, 2, 512], F32))
        psG = ctx.enter_context(nc.psum_tensor("e_psG", [P, 2, 512], F32))
        psY = ctx.enter_context(nc.psum_tensor("e_psY", [CAP, 2, D], F32))
        w_loaded = [sem(f"w_loaded{j}") for j in range(RING)]
        x_loaded = [sem(f"x_loaded{j}") for j in range(RING)]
        gathers = sem("gathers")
        ids_ready, x_half, x_turned, xT_ready = sem("ids_ready"), sem("x_half"), sem("x_turned"), sem("xT_ready")
        g_ready, gate_ready, h_ready, y_ready, y_taken = sem("g_ready"), sem("gate_ready"), sem("h_ready"), sem("y_ready"), sem("y_taken")
        y_stored = [sem(f"y_stored{j}") for j in range(2)]
        block = ctx.enter_context(nc.Block())

        def rounds(engine, body):
            for j in range(RING):
                body(0, j)
            with engine.Fori(1, NE // RING) as it:
                for j in range(RING):
                    body(it, j)

        @block.sync
        def _(sp):
            def body(it, j):
                e = it * RING + j
                if not isinstance(it, int):
                    sp.wait_ge(y_ready, e - (RING - 1))
                sp.dma_start(wg[:, j, :, :], S["w_gate"][bass.ds(e, 1)].rearrange("o (k p) f -> p (o k) f", p=P)).then_inc(w_loaded[j], 16)
                sp.dma_start(wu[:, j, :, :], S["w_up"][bass.ds(e, 1)].rearrange("o (k p) f -> p (o k) f", p=P)).then_inc(w_loaded[j], 16)
                sp.dma_start(wd[:, j, :, :], S["w_down"][bass.ds(e, 1)].rearrange("o (k p) n -> p (o k) n", p=P)).then_inc(w_loaded[j], 16)
            rounds(sp, body)

        @block.gpsimd
        def _(pool):
            def body(it, j):
                e = it * RING + j
                if not isinstance(it, int):
                    pool.wait_ge(x_turned, e - (RING - 1))
                    pool.wait_ge(x_loaded[j], it * 16)
                nc.gpsimd.tensor_copy(ids[:, j:j + 1], M["token"][:, bass.ds(e, 1)]).then_inc(ids_ready, 1)
                pool.wait_ge(ids_ready, e + 1)
                pool.sem_inc(gathers, 1)
                pool.indirect_dma_start(xg[:, j, :], None, S["xn"], bass.IndirectOffsetOnAxis(ap=ids[:, j:j + 1], axis=0)
                                        ).then_inc(x_loaded[j], 16)
            rounds(pool, body)

        @block.tensor
        def _(pe):
            def body(it, j):
                e = it * RING + j
                first = isinstance(it, int)
                b = j % 2
                pe.wait_ge(x_loaded[j], it * 16 + 16)
                for half in range(2):
                    if not (first and j == 0):
                        pe.wait_ge(xT_ready, e * 2 + half - 1)
                    for k in range(4):
                        mm = nc.tensor.transpose(psX[:, half, k * CAP:(k + 1) * CAP],
                                                 xg[:, j, (4 * half + k) * P:(4 * half + k + 1) * P], A["identity"][:CAP, :CAP])
                    mm.then_inc(x_turned if half else x_half, 1)
                pe.wait_ge(w_loaded[j], it * 48 + 48)
                pe.wait_ge(xT_ready, e * 2 + 2)
                if not (first and j < 2):
                    pe.wait_ge(h_ready, e - 1)
                for m in range(2 * K2):
                    w = wg if m < K2 else wu
                    f = m % K2
                    for k in range(KD):
                        mm = nc.tensor.matmul(psG[:, b, m * CAP:(m + 1) * CAP], w[:, j, k, f * P:(f + 1) * P], xT[:, b, k, :],
                                              start=(k == 0), stop=(k == KD - 1), skip_group_check=True)
                mm.then_inc(g_ready, 1)
                pe.wait_ge(h_ready, e + 1)
                if not (first and j < 2):
                    pe.wait_ge(y_taken, e - 1)
                for c in range(2):
                    for f in range(K2):
                        mm = nc.tensor.matmul(psY[:, b, c * 512:(c + 1) * 512], hT[:, b, f, :], wd[:, j, f, c * 512:(c + 1) * 512],
                                              start=(f == 0), stop=(f == K2 - 1))
                mm.then_inc(y_ready, 1)
            rounds(pe, body)

        @block.scalar
        def _(act):
            def body(it, j):
                e = it * RING + j
                first = isinstance(it, int)
                b = j % 2
                act.wait_ge(g_ready, e + 1)
                if not (first and j < 2):
                    act.wait_ge(h_ready, e - 1)
                nc.scalar.activation(gate[:, b, :, :], psG[:, b, :K2 * CAP].rearrange("p (f c) -> p f c", f=K2), ACT.Silu
                                     ).then_inc(gate_ready, 1)
                act.wait_ge(y_ready, e + 1)
                if not (first and j < 2):
                    act.wait_ge(y_stored[b], (it * (RING // 2) + j // 2) * 16)
                nc.scalar.activation(y[:, b, :], psY[:, b, :], ACT.Copy).then_inc(y_taken, 1)
                act.wait_ge(y_taken, e + 1)
                act.dma_start(S["y"][bass.ds(e * CAP, CAP), :], y[:, b, :]).then_inc(y_stored[b], 16)
            rounds(act, body)
            for b in range(2):
                act.wait_ge(y_stored[b], 16 * NE // 2)

        @block.vector
        def _(dve):
            def body(it, j):
                e = it * RING + j
                first = isinstance(it, int)
                b = j % 2
                if not (first and j < 2):
                    dve.wait_ge(g_ready, e - 1)
                for half in range(2):
                    dve.wait_ge(x_half if half == 0 else x_turned, e + 1)
                    nc.vector.tensor_tensor(xT[:, b, 4 * half:4 * half + 4, :],
                                            psX[:, half, :4 * CAP].rearrange("p (k c) -> p k c", k=4),
                                            A["ln2_gT"][:, 4 * half:4 * half + 4].unsqueeze(2).to_broadcast([P, 4, CAP]),
                                            ALU.mult).then_inc(xT_ready, 1)
                dve.wait_ge(gate_ready, e + 1)
                if not (first and j < 2):
                    dve.wait_ge(y_ready, e - 1)
                nc.vector.tensor_tensor(hT[:, b, :, :], gate[:, b, :, :],
                                        psG[:, b, K2 * CAP:2 * K2 * CAP].rearrange("p (f c) -> p f c", f=K2),
                                        ALU.mult).then_inc(h_ready, 1)
            rounds(dve, body)


def overflow_experts(nc, S, A, M):
    K2 = DE // P
    with ExitStack() as ctx:
        sb = lambda n, s, d=F32: ctx.enter_context(nc.sbuf_tensor("v_" + n, s, d))
        sem = stage_semaphores(nc, ctx, "v_")
        wg = sb("wg", [P, KD, DE])
        wu = sb("wu", [P, KD, DE])
        wd = sb("wd", [P, K2, D])
        xg = sb("xg", [CAP, D])
        ids = sb("ids", [CAP, 1], U32)
        xT = sb("xT", [P, KD, CAP])
        gate = sb("gate", [P, K2, CAP])
        hT = sb("hT", [P, K2, CAP])
        y = sb("y", [CAP, D])
        psX = ctx.enter_context(nc.psum_tensor("v_psX", [P, 2, 512], F32))
        psG = ctx.enter_context(nc.psum_tensor("v_psG", [P, 512], F32))
        psY = ctx.enter_context(nc.psum_tensor("v_psY", [CAP, D], F32))
        gathers = sem("gathers")
        w_loaded, x_loaded, ids_ready, x_turned, xT_ready = sem("w_loaded"), sem("x_loaded"), sem("ids_ready"), sem("x_turned"), sem("xT_ready")
        g_ready, gate_ready, h_ready, y_ready, y_taken, y_stored = sem("g_ready"), sem("gate_ready"), sem("h_ready"), sem("y_ready"), sem("y_taken"), sem("y_stored")
        block = ctx.enter_context(nc.Block())

        def slots(engine):
            return engine.Fori(0, engine.value_load(M["over_count"][0:1, 0:1], min_val=0, max_val=OVER))

        @block.sync
        def _(sp):
            with slots(sp) as s:
                e = sp.value_load(M["over_expert"][0:1, bass.ds(s, 1)], min_val=0, max_val=NE - 1)
                sp.wait_ge(y_ready, s + 1)
                sp.dma_start(wg[:, :, :], S["w_gate"][bass.ds(e, 1)].rearrange("o (k p) f -> p (o k) f", p=P)).then_inc(w_loaded, 16)
                sp.dma_start(wu[:, :, :], S["w_up"][bass.ds(e, 1)].rearrange("o (k p) f -> p (o k) f", p=P)).then_inc(w_loaded, 16)
                sp.dma_start(wd[:, :, :], S["w_down"][bass.ds(e, 1)].rearrange("o (k p) n -> p (o k) n", p=P)).then_inc(w_loaded, 16)

        @block.gpsimd
        def _(pool):
            with slots(pool) as s:
                pool.wait_ge(x_turned, s + 1)
                nc.gpsimd.tensor_copy(ids[:, :], M["token"][:, bass.ds(NE + s, 1)]).then_inc(ids_ready, 1)
                pool.wait_ge(ids_ready, s + 1)
                pool.sem_inc(gathers, 1)
                pool.indirect_dma_start(xg[:, :], None, S["xn"], bass.IndirectOffsetOnAxis(ap=ids[:, :], axis=0)
                                        ).then_inc(x_loaded, 16)

        @block.tensor
        def _(pe):
            pe.sem_inc(x_turned, 1)
            pe.sem_inc(y_ready, 1)
            with slots(pe) as s:
                pe.wait_ge(x_loaded, s * 16 + 16)
                for k in range(KD):
                    mm = nc.tensor.transpose(psX[:, k // 4, k % 4 * CAP:(k % 4 + 1) * CAP], xg[:, k * P:(k + 1) * P],
                                             A["identity"][:CAP, :CAP])
                mm.then_inc(x_turned, 1)
                pe.wait_ge(w_loaded, s * 48 + 48)
                pe.wait_ge(xT_ready, s * 2 + 2)
                for m in range(2 * K2):
                    w, f = wg if m < K2 else wu, m % K2
                    for k in range(KD):
                        mm = nc.tensor.matmul(psG[:, m * CAP:(m + 1) * CAP], w[:, k, f * P:(f + 1) * P], xT[:, k, :],
                                              start=(k == 0), stop=(k == KD - 1), skip_group_check=True)
                mm.then_inc(g_ready, 1)
                pe.wait_ge(h_ready, s + 1)
                pe.wait_ge(y_taken, s + 1)
                for c in range(2):
                    for f in range(K2):
                        mm = nc.tensor.matmul(psY[:, c * 512:(c + 1) * 512], hT[:, f, :], wd[:, f, c * 512:(c + 1) * 512],
                                              start=(f == 0), stop=(f == K2 - 1))
                mm.then_inc(y_ready, 1)

        @block.scalar
        def _(act):
            act.sem_inc(y_taken, 1)
            with slots(act) as s:
                act.wait_ge(g_ready, s + 1)
                nc.scalar.activation(gate[:, :, :], psG[:, :K2 * CAP].rearrange("p (f c) -> p f c", f=K2), ACT.Silu).then_inc(gate_ready, 1)
                act.wait_ge(y_ready, s + 2)
                nc.scalar.activation(y[:, :], psY[:, :], ACT.Copy).then_inc(y_taken, 1)
                act.wait_ge(y_taken, s + 2)
                act.dma_start(S["y"][bass.ds((NE + s) * CAP, CAP), :], y[:, :]).then_inc(y_stored, 16)
                act.wait_ge(y_stored, s * 16 + 16)

        @block.vector
        def _(dve):
            with slots(dve) as s:
                dve.wait_ge(x_turned, s + 2)
                for half in range(2):
                    nc.vector.tensor_tensor(xT[:, 4 * half:4 * half + 4, :], psX[:, half, :4 * CAP].rearrange("p (k c) -> p k c", k=4),
                                            A["ln2_gT"][:, 4 * half:4 * half + 4].unsqueeze(2).to_broadcast([P, 4, CAP]),
                                            ALU.mult).then_inc(xT_ready, 1)
                dve.wait_ge(gate_ready, s + 1)
                nc.vector.tensor_tensor(hT[:, :, :], gate[:, :, :], psG[:, K2 * CAP:2 * K2 * CAP].rearrange("p (f c) -> p f c", f=K2),
                                        ALU.mult).then_inc(h_ready, 1)


def combine(nc, S, M):
    with ExitStack() as ctx:
        sb = lambda n, s, d=F32: ctx.enter_context(nc.sbuf_tensor("c_" + n, s, d))
        sem = stage_semaphores(nc, ctx, "c_")
        h = sb("h", [P, TILES, D])
        ya = sb("ya", [P, 4, D])
        yb = sb("yb", [P, 4, D])
        h_loaded = [sem(f"h_loaded{j}") for j in range(TILES)]
        y_loaded = [[sem(f"y{c}_loaded{j}") for j in range(4)] for c in range(2)]
        half_done, ready, stored = sem("half_done"), sem("ready"), sem("stored")
        block = ctx.enter_context(nc.Block())

        @block.sync
        def _(sp):
            for i in range(TILES):
                sp.dma_start(h[:rows_of(i), i, :], S["h"][cols_of(i), :]).then_inc(h_loaded[i], 16)
            for i in range(TILES):
                sp.wait_ge(ready, i + 1)
                sp.dma_start(S["out_rows"](i), h[:rows_of(i), i, :]).then_inc(stored, 16)
            sp.wait_ge(stored, 16 * TILES)

        @block.gpsimd
        def _(pool):
            for i in range(TILES):
                n = rows_of(i)
                if i >= 4:
                    pool.wait_ge(ready, i - 3)
                for c, y in enumerate((ya, yb)):
                    pool.indirect_dma_start(y[:n, i % 4, :], None, S["y"], bass.IndirectOffsetOnAxis(ap=M["pos"][:n, c, i:i + 1], axis=0)
                                            ).then_inc(y_loaded[c][i % 4], 16)

        @block.vector
        def _(dve):
            for i in range(TILES):
                n = rows_of(i)
                dve.wait_ge(h_loaded[i], 16)
                dve.wait_ge(y_loaded[0][i % 4], 16 * (i // 4 + 1))
                nc.vector.scalar_tensor_tensor(h[:n, i, :], ya[:n, i % 4, :], M["weight"][:n, 0, i:i + 1], h[:n, i, :],
                                               ALU.mult, ALU.add).then_inc(half_done, 1)
                dve.wait_ge(half_done, i + 1)
                dve.wait_ge(y_loaded[1][i % 4], 16 * (i // 4 + 1))
                nc.vector.scalar_tensor_tensor(h[:n, i, :], yb[:n, i % 4, :], M["weight"][:n, 1, i:i + 1], h[:n, i, :],
                                               ALU.mult, ALU.add).then_inc(ready, 1)


def load_constants(nc, name, pairs, casts):
    with ExitStack() as ctx:
        sem = stage_semaphores(nc, ctx, name)
        loaded, loaded_by_act, done = sem("loaded"), sem("loaded_by_act"), sem("done")
        block = ctx.enter_context(nc.Block())
        by_sp, by_act = pairs[0::2], pairs[1::2]

        @block.sync
        def _(sp):
            with nc.allow_non_contiguous_dma(reason="small tables"):
                for dst, src in by_sp:
                    sp.dma_start(dst, src).then_inc(loaded, 16)
            if by_sp:
                sp.wait_ge(loaded, 16 * len(by_sp))

        @block.scalar
        def _(act):
            with nc.allow_non_contiguous_dma(reason="small tables"):
                for dst, src in by_act:
                    act.dma_start(dst, src).then_inc(loaded_by_act, 16)
            if by_act:
                act.wait_ge(loaded_by_act, 16 * len(by_act))

        @block.vector
        def _(dve):
            if by_sp:
                dve.wait_ge(loaded, 16 * len(by_sp))
            if by_act:
                dve.wait_ge(loaded_by_act, 16 * len(by_act))
            for dst, src, scale, offset in casts:
                nc.vector.tensor_scalar(dst, src, scale, offset, ALU.mult, ALU.add).then_inc(done, 1)
            if casts:
                dve.wait_ge(done, len(casts))


INPUTS = ["x_prompt", "x_sample", "cache_k", "cache_v", "cache_kidx", "state_ret", "page_table", "rel_bias", "ln1_g",
          "w_in", "q_norm_g", "k_norm_g", "ret_gn_g", "ret_gn_b", "w_out", "ln2_g", "w_group", "w_expert", "w_gate",
          "w_up", "w_down"]
OUTPUTS = [(1, SEQ, D), (DB, DS, D), (1, 1, SEQ, H, HD), (1, 1, SEQ, H, HD), (1, 1, SEQ, 64), (1, 1, H, HD, HD),
           (1, DB, DS, H, HD), (1, DB, DS, H, HD), (1, DB, DS, 64), (1, DB, H, HD, HD)]


def shape_constants():
    f = np.float32
    pos = np.concatenate([np.arange(SEQ), np.tile(PAST + np.arange(DS), DB)]).astype(f)
    inv = (10000.0 ** (-np.arange(HD // 2) / (HD // 2))).astype(f)
    ang = (pos[:, None] * inv[None]).astype(f)
    gamma = 1 - 2.0 ** (-5 - np.arange(H))
    j = np.stack([np.arange(P), np.arange(P) % DS]) + 1.0
    step = np.arange(P)
    own = lambda n: (np.arange(NS)[:, None] // DS == np.arange(n)[None] // DS)
    prompt_mask = step[:, None] <= step[None]
    sample_mask = np.zeros((P, P))
    sample_mask[:NS, :NS] = own(NS) & (step[:NS, None] <= step[None, :NS])
    n = np.maximum(PAST + DS - 1 - np.arange(PAST + DS + P), 0)
    nf = np.maximum(n, 16).astype(f)
    large = 16 + (np.log(nf / f(16)) / f(np.log(64.0)) * f(16)).astype(np.int32)
    bucket = np.where(n < 16, n, np.minimum(large, 31))
    pair_gamma = gamma.reshape(PAIRS, 2)[:, step // HD].T
    rows = np.arange(NS)
    return {
        "identity": np.eye(P), "cos": np.cos(ang), "sin": np.sin(ang),
        "decay_q": gamma[None, None] ** j[:, :, None],
        "decay_k": gamma[None, None] ** -j[:, :, None] * HD ** -0.5,
        "ret_mask": np.stack([prompt_mask, sample_mask]),
        "gamma_chunk": np.stack([pair_gamma ** P, pair_gamma ** DS], 1),
        "own_seq": rows[:, None] // DS == np.arange(DB)[None],
        "sum_heads": (step[:, None] // 32 == np.arange(32)[None] // DS) & (step[:, None] % DS == np.arange(32)[None] % DS),
        "causal": np.where(step[None] <= step[:, None], 0, NEG),
        "causal_s": np.where(own(NS) & (rows[None] <= rows[:, None]), 0, NEG),
        "own_rows": (rows[:, None, None] // DS == np.arange(DB)[None, :, None]) 
                    & (step[None, None] % 32 < 2 * DS) & (rows[:, None, None] % DS == step[None, None] % DS),
        "onehot": np.arange(32)[:, None] == bucket[None],
        "above": step[:, None] < step[None],
        "countdown": np.arange(EPG, 0, -1)[None], "cap_multiples": (CAP * np.arange(1, MULTIPLES + 1))[None],
        "expert_id": np.arange(NE)[None], "row_in_page": (step % 8)[:, None],
        "quarter_in_page": 4 * (step % 8)[:, None] + np.arange(4)[None],
    }


def build(nc, a, outs, c):
    dram = lambda n, s, d=F32: nc.dram_tensor(n, s, d, kind="Internal").ap()
    xp, xs = a["x_prompt"][0], a["x_sample"].rearrange("b t d -> (b t) d")
    row = lambda p, s: (lambda i: p[cols_of(i), :] if i < NT else s)
    S = {
        "w_in": a["w_in"][0], "w_out": a["w_out"][0], "ret_gn_g": a["ret_gn_g"], "ret_gn_b": a["ret_gn_b"],
        "state_ret": a["state_ret"][0], "rel_bias": a["rel_bias"], "w_group": a["w_group"][0], "w_expert": a["w_expert"][0],
        "w_gate": a["w_gate"][0], "w_up": a["w_up"][0], "w_down": a["w_down"][0],
        "cache_k": a["cache_k"][0].rearrange("n (g r) h e -> (n g) (r h e)", r=4),
        "cache_v": a["cache_v"][0].rearrange("n (g r) h e -> (n g) (r h e)", r=4),
        "cache_kidx": a["cache_kidx"][0].rearrange("n (g r) e -> (n g) (r e)", r=16),
        "ret_prompt": outs[5][0, 0], "ret_sample": outs[9][0], "c_onehot": c["onehot"],
        "x_rows": row(xp, xs), "out_rows": row(outs[0][0], outs[1].rearrange("b t d -> (b t) d")),
        "h": dram("h_rows", (TOK, D)), "xn": dram("xn_rows", (TOK, D)), "y": dram("y_rows", (SLOTS * CAP, D)),
        "token_list": dram("token_list", (-(-SLOTS * CAP // P) * P, 1), U32),
        "skew": dram("skew", (H, P, SEQ + P)), "skew_s": dram("skew_s", (NS, PAST + 2 * DS)),
    }
    flat = lambda k: row(outs[k][0, 0].rearrange("s h e -> s (h e)"), outs[k + 4][0].rearrange("b t h e -> (b t) (h e)"))
    k_rows, v_rows = flat(2), flat(3)
    i_rows = row(outs[4][0, 0], outs[8][0].rearrange("b t e -> (b t) e"))
    with ExitStack() as top:
        def sb(stack, n, s, d=F32):
            return stack.enter_context(nc.sbuf_tensor(n, s, d))
        A, X, T, M = {}, {}, {}, {}
        for n, s, d in (("identity", [P, P], F32), ("identity_b", [P, P], BF16), ("causal", [P, P], F32),
                        ("causal_b", [P, P], BF16), ("ones_b", [P, P], BF16), ("above_b", [P, P], BF16),
                        ("own_rows", [NS, DB, P], BF16), ("causal_s", [NS, NS], F32), ("own_seq", [NS, DB], F32),
                        ("sum_heads", [P, 32], F32), ("gamma_chunk", [P, 2, PAIRS], F32), ("row_id", [P, DB], U32),
                        ("quarter_id", [P, 4, DB], U32),
                        ("countdown", [P, EPG], F32), ("cap_multiples", [P, MULTIPLES], F32), ("expert_id", [P, NE], F32),
                        ("ln2_gT", [P, KD], F32), ("attT", [P, PAIRS, TOK], F32), ("retT", [P, PAIRS, TOK], F32)):
            A[n] = sb(top, "k_" + n, s, d)
        M["pos"] = sb(top, "m_pos", [P, 2, TILES], U32)
        M["weight"] = sb(top, "m_weight", [P, 2, TILES])
        M["token"] = sb(top, "m_token", [CAP, SLOTS], U32)
        M["over_count"] = sb(top, "m_over_count", [P, 1], I32)
        M["over_expert"] = sb(top, "m_over_expert", [P, OVER], I32)

        bc = lambda ap, n: ap.to_broadcast([P, n])
        with ExitStack() as st:
            above = sb(st, "above", [P, P])
            own = sb(st, "own", [NS, DB, P])
            table = sb(st, "table", [P, DB], I32)
            off = sb(st, "off", [P, 1])
            off_quarter = sb(st, "off_quarter", [P, 4])
            pairs = [(A[n][:, :], c[n]) for n in ("identity", "causal", "causal_s", "own_seq", "sum_heads")]
            pairs += [(A["gamma_chunk"][:, :, :], c["gamma_chunk"]), (above[:, :], c["above"]), (own[:, :, :], c["own_rows"]),
                      (off[:, :], c["row_in_page"]), (off_quarter[:, :], c["quarter_in_page"]),
                      (A["ln2_gT"][:, :], a["ln2_g"].rearrange("o (k p) -> p (o k)", p=P))]
            pairs += [(A[n][:, :], bc(c[n], A[n].shape[1])) for n in ("countdown", "cap_multiples", "expert_id")]
            pages = a["page_table"].rearrange("b g -> g b")
            pairs += [(table[8 * g:8 * g + 8, :], pages[g:g + 1, :].to_broadcast([8, DB])) for g in range(PAGES)]
            casts = [(A["identity_b"][:, :], A["identity"][:, :], 1.0, 0.0), (A["causal_b"][:, :], A["causal"][:, :], 1.0, 0.0),
                     (A["ones_b"][:, :], A["identity"][:, :], 0.0, 1.0), (A["above_b"][:, :], above[:, :], 1.0, 0.0),
                     (A["own_rows"][:, :, :], own[:, :, :], 1.0, 0.0), (A["row_id"][:, :], table[:, :], 8.0, off[:, 0:1])]
            casts += [(A["quarter_id"][:, j, :], table[:, :], 32.0, off_quarter[:, j:j + 1]) for j in range(4)]
            load_constants(nc, "l0_", pairs, casts)

        A["mask_s"] = X["mask_s"] = sb(top, "mask_s", [NS, NK], BF16)
        A["qaT_s"], A["kaT_s"] = sb(top, "qaT_s", [P, PAIRS, NS]), sb(top, "kaT_s", [P, PAIRS, NS])
        A["va_s"] = sb(top, "va_s", [NS, W])

        with ExitStack() as early:
            buf = [sb(early, f"buf{j}", [P, TILES, W]) for j in range(3)]
            flat_buf = lambda t: t[:, :, :].rearrange("p i w -> p (i w)")[:, :PAIRS * TOK].rearrange("p (a t) -> p a t", a=PAIRS)
            A["kp"], A["vr"], A["sg"] = buf
            A["qpT"], A["kpT"] = A["attT"], A["retT"]
            A["qaT"], A["kaT"], A["va"] = flat_buf(buf[0]), flat_buf(buf[2]), buf[1]
            A["qiT"] = sb(early, "qiT", [P, 2, TOK])
            A["kiT2"] = sb(early, "kiT", [P, 1, TOK])
            A["kiT"] = A["kiT2"][:, 0, :]
            A["wi"] = sb(early, "wi", [P, TILES, IH])
            gq, gk = sb(early, "gq", [P, HD]), sb(early, "gk", [P, HD])
            load_constants(nc, "l1_", [(gq[:, :], bc(a["q_norm_g"], HD)), (gk[:, :], bc(a["k_norm_g"], HD))],
                           [(gq[:, :], gq[:, :], HD ** -0.5, 0.0)])
            with ExitStack() as st:
                A["uT"] = sb(st, "uT", [P, KD, TOK])
                norm_and_transpose(nc, "n1_", S["x_rows"], a["ln1_g"], A["identity"], A["uT"])
                with ExitStack() as tb:
                    cos, sin = sb(tb, "cos", [P, TILES, HD // 2]), sb(tb, "sin", [P, TILES, HD // 2])
                    dq, dk = sb(tb, "dq", [P, 2, H]), sb(tb, "dk", [P, 2, H])
                    pairs = []
                    for dst, n in ((cos, "cos"), (sin, "sin")):
                        pairs += [(dst[:, :NT, :], c[n][:SEQ].rearrange("(i p) r -> p i r", p=P)), (dst[:NS, NT, :], c[n][SEQ:])]
                    pairs += [(dst[:, :, :], c[n].rearrange("s p h -> p s h")) for dst, n in ((dq, "decay_q"), (dk, "decay_k"))]
                    load_constants(nc, "l2_", pairs, [])
                    A["cos"], A["sin"] = cos, sin
                    project(nc, "pr_", [
                        dict(kind="rotary", col=QR, n=W, decay=dq, blocks=PAIRS, to=[(A["qpT"], 0, PAIRS)]),
                        dict(kind="rotary", col=KR, n=W, decay=dk, blocks=PAIRS, nat=A["kp"], to=[(A["kpT"], 0, PAIRS)]),
                        dict(kind="copy", col=VR, n=W, keep=A["vr"]),
                        dict(kind="silu", col=GR, n=W, keep=A["sg"])], S, A)
                with ExitStack() as tb:
                    A["ret_mask"] = sb(tb, "ret_mask", [P, 2, P])
                    load_constants(nc, "l3_", [(A["ret_mask"][:, :, :], c["ret_mask"].rearrange("s p q -> p s q"))], [])
                    retention(nc, S, A)
                project(nc, "pa_", [
                    dict(kind="index", col=QI, n=N_QI, blocks=3, to=[(A["qiT"], 0, 2), (A["kiT2"], 2, 3)],
                         out=i_rows, out_cols=slice(256, 320)),
                    dict(kind="norm", col=QA, n=W, gain=gq, blocks=PAIRS, to=[(A["qaT"], 0, PAIRS)]),
                    dict(kind="norm", col=KA, n=W, gain=gk, blocks=PAIRS, to=[(A["kaT"], 0, PAIRS)], out=k_rows, out_cols=slice(0, W)),
                    dict(kind="copy", col=VA, n=W, keep=A["va"], out=v_rows)], S, A)
            first = TOPK // P
            at = {}
            for i in range(first, NT):
                at[i] = sum((q + 1) * P for q in range(first, i))
            total = at[NT - 1] + NT * P
            mask = sb(early, "mask", [P, total], BF16)
            X["mask"] = lambda i: mask[:, at[i]:at[i] + (i + 1) * P]
            with ExitStack() as st:
                sc = sb(st, "sc", [P, total])
                X["sc"] = lambda i: sc[:, at[i]:at[i] + (i + 1) * P]
                X["sc_s"] = sb(st, "sc_s", [NS, NK])
                X["lo"], X["hi"] = sb(st, "lo", [P, TILES]), sb(st, "hi", [P, TILES])
                index_scores(nc, S, A, X)
                select_keys(nc, A, X)
            with ExitStack() as st:
                T["bias"] = sb(st, "bias", [P, H, SEQ])
                make_bias(nc, S, T)
                prompt_attention(nc, A, X, T)
            load_constants(nc, "l4_", [], [(A["qaT_s"][:, :, :], A["qaT"][:, :, SEQ:], 1.0, 0.0),
                                    (A["kaT_s"][:, :, :], A["kaT"][:, :, SEQ:], 1.0, 0.0),
                                    (A["va_s"][:, :], A["va"][:NS, NT, :], 1.0, 0.0)])
        sample_attention(nc, S, A, X)
        output_projection(nc, S, A)
        with ExitStack() as st:
            A["uT"] = sb(st, "uT2", [P, KD, TOK])
            norm_and_transpose(nc, "n2_", lambda i: S["h"][cols_of(i), :], a["ln2_g"], A["identity"], A["uT"], S["xn"])
            route(nc, S, A, M)
        experts(nc, S, A, M)
        overflow_experts(nc, S, A, M)
        combine(nc, S, M)


def kernel(**inputs):
    import numpy as _np
    import concourse.bacc as _bacc
    from concourse import mybir as _mybir
    from concourse.bass_utils import run_bass_kernel_spmd as _run

    nc = _bacc.Bacc("TRN2", target_bir_lowering=False, num_devices=1)
    arrays, args, consts = {}, {}, {}
    for name in INPUTS:
        arrays[f"in_{name}"] = _np.ascontiguousarray(inputs[name])
    for name, table in shape_constants().items():
        arrays[f"const_{name}"] = _np.ascontiguousarray(table.astype(_np.float32))
    for name, array in arrays.items():
        ap = nc.dram_tensor(name, array.shape, _mybir.dt.from_np(array.dtype), kind="ExternalInput").ap()
        kind, key = name.split("_", 1)
        (args if kind == "in" else consts)[key] = ap
    outs = [nc.dram_tensor(f"out_{i}", shape, _mybir.dt.float32, kind="ExternalOutput").ap() for i, shape in enumerate(OUTPUTS)]
    build(nc, args, outs, consts)
    r = _run(nc, [arrays], core_ids=[0])
    return tuple(r.results[0][f"out_{i}"] for i in range(len(OUTPUTS)))
```

```python
from contextlib import ExitStack

import numpy as np
import concourse.bass as bass
from concourse import mybir

ALU = mybir.AluOpType
ACT = mybir.ActivationFunctionType
F32 = mybir.dt.float32
BF16 = mybir.dt.bfloat16
U32 = mybir.dt.uint32
I32 = mybir.dt.int32
AX_X = mybir.AxisListType.X

P = 128
D = 1024
KD = D // P
SEQ = 1024
DB, DS = 8, 8
NS = DB * DS
TOK = SEQ + NS
NT = SEQ // P
TILES = NT + 1
H, HD = 8, 64
W = H * HD
PAIRS = H // 2
IH = 4
PAST, PAGE = 2048, 128
PAGES = PAST // PAGE
NPHYS = DB * PAGES * 5 // 4
NK = PAST + NS
TOPK = 256
NE, NG, EPG, DE = 32, 4, 8, 256
EPS, GN_EPS = 1e-6, 1e-5
NEG = -1e30
CAP = 96
PAGE_RING = 12
OVER = 2 * TOK // CAP
SLOTS = NE + OVER
MULTIPLES = TOK // CAP + 1
RING = 4
BISECT = 32

QA, KA, VA, QI, QR, KR, VR, GR = 0, 512, 1024, 1536, 1860, 2372, 2884, 3396
N_IN = 3908
N_QI = IH * 64 + 64 + IH


def rows_of(i):
    return P if i < NT else NS


def cols_of(i):
    return slice(i * P, i * P + rows_of(i))


def stage_semaphores(nc, ctx, prefix):
    taken = []

    def release():
        nc.clear_and_free_semaphores(taken)
        nc.all_engine_barrier()

    def take(name):
        taken.append(nc.alloc_semaphore(prefix + name))
        return taken[-1]

    ctx.callback(release)
    return take


class Chain:

    def __init__(self, engine, semaphore):
        self.engine, self.semaphore, self.n = engine, semaphore, 0

    def __call__(self, instruction):
        self.n += 1
        instruction.then_inc(self.semaphore, 1)
        self.engine.wait_ge(self.semaphore, self.n)


def norm_and_transpose(nc, name, tile_rows, g_dram, identity, uT, xn_dram=None, tables=(), casts=(), weights=None):
    share = -(-len(tables) // (TILES - 2))
    with ExitStack() as ctx:
        sb = lambda n, s, d=F32: ctx.enter_context(nc.sbuf_tensor(name + n, s, d))
        sem = stage_semaphores(nc, ctx, name)
        x = sb("x", [P, 3, D])
        sq = sb("sq", [P, D])
        xn = sb("xn", [P, 2, D])
        ms = sb("ms", [P, TILES])
        rms = sb("rms", [P, TILES])
        rstd = sb("rstd", [P, TILES])
        g = sb("g", [P, KD])
        psT = ctx.enter_context(nc.psum_tensor(name + "psT", [P, 2, KD, P], F32))
        x_loaded = [sem(f"x_loaded{j}") for j in range(3)]
        xn_stored = [sem(f"xn_stored{j}") for j in range(2)]
        g_loaded, squared, rooted = sem("g_loaded"), sem("squared"), sem("rooted")
        mean_ready, xn_ready = sem("mean_ready"), sem("xn_ready")
        turned, taken, dve_done = sem("turned"), sem("taken"), sem("dve_done")
        tables_loaded, cast = sem("tables_loaded"), sem("cast")
        block = ctx.enter_context(nc.Block())

        @block.sync
        def _(sp):
            with nc.allow_non_contiguous_dma(reason="one gain per partition"):
                sp.dma_start(g[:, :], g_dram.rearrange("o (k p) -> p (o k)", p=P)).then_inc(g_loaded, 16)
            for i in range(TILES):
                if i >= 3:
                    sp.wait_ge(xn_ready, i - 2)
                sp.dma_start(x[:rows_of(i), i % 3, :], tile_rows(i)).then_inc(x_loaded[i % 3], 16)
                if i >= 2:
                    with nc.allow_non_contiguous_dma(reason="small tables"):
                        for dst, src in tables[(i - 2) * share:(i - 1) * share]:
                            sp.dma_start(dst, src).then_inc(tables_loaded, 16)
            if weights is not None:
                sp.dma_start(weights[0], weights[1]).then_inc(weights[2], 16)
            if tables:
                sp.wait_ge(tables_loaded, 16 * len(tables))

        @block.scalar
        def _(act):
            for i in range(TILES):
                n = rows_of(i)
                act.wait_ge(x_loaded[i % 3], 16 * (i // 3 + 1))
                if i:
                    act.wait_ge(squared, i)
                nc.scalar.activation(sq[:n, :], x[:n, i % 3, :], ACT.Square,
                                     accum_out=ms[:n, i:i + 1]).then_inc(squared, 1)
                act.wait_ge(mean_ready, i + 1)
                nc.scalar.activation(rms[:n, i:i + 1], rstd[:n, i:i + 1], ACT.Sqrt).then_inc(rooted, 1)

        @block.vector
        def _(dve):
            link = Chain(dve, dve_done)
            dve.wait_ge(g_loaded, 16)
            for i in range(TILES + 1):
                if i < TILES:
                    n = rows_of(i)
                    dve.wait_ge(squared, i + 1)
                    nc.vector.tensor_scalar(rstd[:n, i:i + 1], ms[:n, i:i + 1], 1.0 / D, EPS,
                                            ALU.mult, ALU.add).then_inc(mean_ready, 1)
                    dve.wait_ge(rooted, i + 1)
                    link(nc.vector.reciprocal(rstd[:n, i:i + 1], rms[:n, i:i + 1]))
                    if i >= 2:
                        dve.wait_ge(turned, i - 1)
                        if xn_dram is not None:
                            dve.wait_ge(xn_stored[i % 2], 16 * (i // 2))
                    nc.vector.tensor_scalar(xn[:n, i % 2, :], x[:n, i % 3, :], rstd[:n, i:i + 1], None,
                                            ALU.mult).then_inc(xn_ready, 1)
                if i:
                    n = rows_of(i - 1)
                    dve.wait_ge(turned, i)
                    nc.vector.tensor_tensor(uT[:, :, cols_of(i - 1)], psT[:, (i - 1) % 2, :, :n],
                                            g[:, :].unsqueeze(2).to_broadcast([P, KD, n]),
                                            ALU.mult).then_inc(taken, 1)
            if casts:
                dve.wait_ge(tables_loaded, 16 * len(tables))
                for dst, src, scale, offset in casts:
                    nc.vector.tensor_scalar(dst, src, scale, offset, ALU.mult, ALU.add).then_inc(cast, 1)
                dve.wait_ge(cast, len(casts))

        @block.tensor
        def _(pe):
            for i in range(TILES):
                n = rows_of(i)
                pe.wait_ge(xn_ready, i + 1)
                if i >= 2:
                    pe.wait_ge(taken, i - 1)
                for k in range(KD):
                    mm = nc.tensor.transpose(psT[:, i % 2, k, :n], xn[:n, i % 2, k * P:(k + 1) * P],
                                             identity[:n, :n])
                mm.then_inc(turned, 1)

        @block.gpsimd
        def _(pool):
            if xn_dram is not None:
                for i in range(TILES):
                    pool.wait_ge(xn_ready, i + 1)
                    pool.dma_start(xn_dram[cols_of(i), :], xn[:rows_of(i), i % 2, :]).then_inc(xn_stored[i % 2], 16)
                pool.wait_ge(xn_stored[0], 16 * ((TILES + 1) // 2))
                pool.wait_ge(xn_stored[1], 16 * (TILES // 2))


def project(nc, name, chunks, S, A, w_first=None, preloaded=None, X=None):
    units = [(c, i) for c in range(len(chunks)) for i in range(TILES)]
    worked = [u for u, (c, i) in enumerate(units) if chunks[c]["kind"] in ("rotary", "norm", "index")]
    stored = [u for u, (c, i) in enumerate(units) if "out" in chunks[c]]
    with ExitStack() as ctx:
        sb = lambda n, s, d=F32: ctx.enter_context(nc.sbuf_tensor(name + n, s, d))
        sem = stage_semaphores(nc, ctx, name)
        kinds = {ch["kind"] for ch in chunks}
        w = [w_first if w_first is not None else sb("w0", [P, KD, W])]
        if len(chunks) > 1:
            w.append(sb("w1", [P, KD, W]))
        z = sb("z", [P, 3, W])
        nat = sb("nat", [P, 2, W])
        t = sb("t", [P, 4, W // 2]) if "rotary" in kinds else None
        ssq = sb("ssq", [P, H])
        rms = sb("rms", [P, H])
        rstd = sb("rstd", [P, H])
        psZ = [ctx.enter_context(nc.psum_tensor(f"{name}psZ{j}", [P, W], F32)) for j in range(3)]
        psT = [ctx.enter_context(nc.psum_tensor(f"{name}psT{j}", [P, 4, P], F32)) for j in range(2)]
        w_loaded = [sem(f"w_loaded{j}") for j in range(2)]
        z_ready, z_taken, z_kept = sem("z_ready"), sem("z_taken"), sem("z_kept")
        mean_ready, rooted, nat_ready = sem("mean_ready"), sem("rooted"), sem("nat_ready")
        turned, t_taken, dve_done = sem("turned"), sem("t_taken"), sem("dve_done")
        out_stored = [sem(f"out_stored{j}") for j in range(2)]
        if X is not None:
            act_halve, begin_halving, dve_halve = bisection(nc, sb, sem, X)
        block = ctx.enter_context(nc.Block())

        def halvings(u):
            return range(BISECT * u // len(units), BISECT * (u + 1) // len(units)) if X is not None else ()

        def store_count(u, j):
            return sum(1 for q, s in enumerate(stored) if s < u and q % 2 == j)

        @block.sync
        def _(sp):
            for c, ch in enumerate(chunks):
                if c == 0 and preloaded is not None:
                    continue
                if c >= 2:
                    sp.wait_ge(z_ready, TILES * (c - 1))
                sp.dma_start(w[c % 2][:, :, :ch["n"]],
                             S["w_in"][:, ch["col"]:ch["col"] + ch["n"]].rearrange("(k p) n -> p k n", p=P)
                             ).then_inc(w_loaded[c % 2], 16)

        @block.tensor
        def _(pe):
            def turn(q):
                c, i = units[worked[q]]
                ch, n = chunks[c], rows_of(i)
                pe.wait_ge(nat_ready, q + 1)
                if q >= 2:
                    pe.wait_ge(t_taken, q - 1)
                src = ch["nat"][:, i, :] if "nat" in ch else nat[:, q % 2, :]
                for b in range(ch["blocks"]):
                    mm = nc.tensor.transpose(psT[q % 2][:, b, :n], src[:n, b * P:(b + 1) * P], A["identity"][:n, :n])
                mm.then_inc(turned, 1)

            done = 0
            for u, (c, i) in enumerate(units):
                n, ch = rows_of(i), chunks[c]
                if i == 0 and c == 0 and preloaded is not None:
                    pe.wait_ge(*preloaded)
                elif i == 0:
                    before = 1 if c % 2 == 0 and preloaded is not None else 0
                    pe.wait_ge(w_loaded[c % 2], 16 * (c // 2 + 1 - before))
                if u >= 3:
                    pe.wait_ge(z_taken, u - 2)
                for k in range(KD):
                    mm = nc.tensor.matmul(psZ[u % 3][:n, :ch["n"]], A["uT"][:, k, cols_of(i)],
                                          w[c % 2][:, k, :ch["n"]], start=(k == 0), stop=(k == KD - 1))
                mm.then_inc(z_ready, 1)
                while done < len(worked) and worked[done] < u:
                    turn(done)
                    done += 1
            while done < len(worked):
                turn(done)
                done += 1

        @block.scalar
        def _(act):
            def take_turned(q):
                c, i = units[worked[q]]
                ch = chunks[c]
                act.wait_ge(turned, q + 1)
                for dst, b0, b1 in ch["to"]:
                    ins = nc.scalar.activation(dst[:, :, cols_of(i)], psT[q % 2][:, b0:b1, :rows_of(i)], ACT.Copy)
                ins.then_inc(t_taken, 1)

            done, roots = 0, 0
            for u, (c, i) in enumerate(units):
                ch, n = chunks[c], rows_of(i)
                act.wait_ge(z_ready, u + 1)
                if u in worked:
                    q = worked.index(u)
                    if q >= 3:
                        act.wait_ge(nat_ready, q - 2)
                    if ch["kind"] == "index" and "out" in ch:
                        q2 = stored.index(u)
                        if q2 >= 3:
                            act.wait_ge(out_stored[(q2 - 3) % 2], 16 * ((q2 - 3) // 2 + 1))
                    nc.scalar.activation(z[:n, q % 3, :ch["n"]], psZ[u % 3][:n, :ch["n"]], ACT.Copy).then_inc(z_taken, 1)
                    for it in halvings(u):
                        act_halve(act, it)
                    if ch["kind"] == "norm":
                        roots += 1
                        act.wait_ge(mean_ready, roots)
                        nc.scalar.activation(rms[:n, :], ssq[:n, :], ACT.Sqrt).then_inc(rooted, 1)
                elif ch["kind"] == "silu":
                    nc.scalar.activation(ch["keep"][:n, i, :], psZ[u % 3][:n, :], ACT.Silu).then_inc(z_taken, 1)
                else:
                    nc.scalar.activation(ch["keep"][:n, i, :], psZ[u % 3][:n, :], ACT.Copy).then_inc(z_taken, 1)
                    for it in halvings(u):
                        act_halve(act, it)
                while done < len(worked) and worked[done] < u:
                    take_turned(done)
                    done += 1
            while done < len(worked):
                take_turned(done)
                done += 1

        @block.vector
        def _(dve):
            link = Chain(dve, dve_done)
            roots = 0
            if X is not None:
                begin_halving(link)
            for u, (c, i) in enumerate(units):
                for it in halvings(u):
                    dve_halve(dve, it)
                if u not in worked:
                    continue
                q = worked.index(u)
                ch, n = chunks[c], rows_of(i)
                dve.wait_ge(z_taken, u + 1)
                zz = z[:n, q % 3, :]
                out = (ch["nat"][:n, i, :] if "nat" in ch else nat[:n, q % 2, :])
                if q >= 2:
                    dve.wait_ge(turned, q - 1)
                    for j in range(2):
                        if "nat" not in ch and store_count(u - 1, j):
                            dve.wait_ge(out_stored[j], 16 * store_count(u - 1, j))
                if ch["kind"] == "rotary":
                    z4 = zz.rearrange("p (h s r) -> p h s r", h=H, s=2)
                    o4 = out.rearrange("p (h s r) -> p h s r", h=H, s=2)
                    r = HD // 2
                    cos = A["cos"][:n, i, :].unsqueeze(1).to_broadcast([n, H, r])
                    sin = A["sin"][:n, i, :].unsqueeze(1).to_broadcast([n, H, r])
                    tv = [t[:n, j, :].rearrange("p (h r) -> p h r", h=H) for j in range(4)]
                    nc.vector.tensor_tensor(tv[0], z4[:, :, 0, :], cos, ALU.mult)
                    nc.vector.tensor_tensor(tv[1], z4[:, :, 1, :], sin, ALU.mult)
                    nc.vector.tensor_tensor(tv[2], z4[:, :, 0, :], sin, ALU.mult)
                    link(nc.vector.tensor_tensor(tv[3], z4[:, :, 1, :], cos, ALU.mult))
                    nc.vector.tensor_tensor(o4[:, :, 0, :], tv[0], tv[1], ALU.subtract)
                    link(nc.vector.tensor_tensor(o4[:, :, 1, :], tv[2], tv[3], ALU.add))
                    o3 = out.rearrange("p (h e) -> p h e", h=H)
                    dec = ch["decay"][:n, 1 if i == NT else 0, :].unsqueeze(2).to_broadcast([n, H, HD])
                    nc.vector.tensor_tensor(o3, o3, dec, ALU.mult).then_inc(nat_ready, 1)
                elif ch["kind"] == "norm":
                    roots += 1
                    z3 = zz.rearrange("p (h e) -> p h e", h=H)
                    o3 = out.rearrange("p (h e) -> p h e", h=H)
                    link(nc.vector.tensor_tensor(out, zz, zz, ALU.mult))
                    link(nc.vector.tensor_reduce(rstd[:n, :], o3, AX_X, ALU.add))
                    nc.vector.tensor_scalar(ssq[:n, :], rstd[:n, :], 1.0 / HD, EPS, ALU.mult, ALU.add).then_inc(mean_ready, 1)
                    dve.wait_ge(rooted, roots)
                    link(nc.vector.reciprocal(rstd[:n, :], rms[:n, :]))
                    link(nc.vector.tensor_tensor(o3, z3, rstd[:n, :].unsqueeze(2).to_broadcast([n, H, HD]), ALU.mult))
                    nc.vector.tensor_tensor(o3, o3, ch["gain"][:n, :].unsqueeze(1).to_broadcast([n, H, HD]),
                                            ALU.mult).then_inc(nat_ready, 1)
                else:
                    nc.vector.tensor_copy(out[:, 0:320], zz[:, 0:320])
                    nc.vector.tensor_copy(out[:, 320:384], zz[:, 256:320])
                    nc.vector.tensor_scalar(A["wi"][:n, i, :], zz[:, 320:324], IH ** -0.5 * 0.125, None,
                                            ALU.mult).then_inc(nat_ready, 1)

        @block.gpsimd
        def _(pool):
            for q, u in enumerate(stored):
                c, i = units[u]
                ch, n = chunks[c], rows_of(i)
                if u in worked:
                    pool.wait_ge(nat_ready, worked.index(u) + 1)
                    src = nat[:n, worked.index(u) % 2, ch["out_cols"]]
                else:
                    pool.wait_ge(z_taken, u + 1)
                    src = ch["keep"][:n, i, :]
                pool.dma_start(ch["out"](i), src).then_inc(out_stored[q % 2], 16)
            for j in range(2):
                if store_count(len(units), j):
                    pool.wait_ge(out_stored[j], 16 * store_count(len(units), j))


def retention(nc, S, A, weights):
    with ExitStack() as ctx:
        sb = lambda n, s, d=F32: ctx.enter_context(nc.sbuf_tensor("r_" + n, s, d))
        sem = stage_semaphores(nc, ctx, "r_")
        ps = lambda n, s: ctx.enter_context(nc.psum_tensor("r_" + n, s, F32))
        intra = sb("intra", [P, H, P])
        state = sb("state", [P, PAIRS, HD])
        s0 = sb("s0", [P, DB, PAIRS, HD])
        vexp = sb("vexp", [NS, 2, DB, HD])
        oT = sb("oT", [HD, W])
        o = sb("o", [P, W])
        o2 = sb("o2", [P, W])
        on = sb("on", [P, 2, W])
        st = sb("st", [P, 4, H])
        gg = sb("gg", [P, W])
        gb = sb("gb", [P, W])
        blank = sb("blank", [CAP, D])
        blank_ready = sem("blank_ready")
        psI = ps("psI", [P, 2, 4, P])
        psO = ps("psO", [P, 2, PAIRS, P])
        psU = ps("psU", [P, PAIRS, P])
        psN = ps("psN", [P, W])
        psT = ps("psT", [P, PAIRS, P])
        loaded, intra_used = sem("loaded"), sem("intra_used")
        scores_ready, intra_ready, o_ready, o_taken = sem("scores_ready"), sem("intra_ready"), sem("o_ready"), sem("o_taken")
        update_ready, state_ready, on_ready = sem("update_ready"), sem("state_ready"), sem("on_ready")
        turned, t_taken, dve_done, var_ready, rooted = sem("turned"), sem("t_taken"), sem("dve_done"), sem("var_ready"), sem("rooted")
        oT_ready, v_spread, su_ready, su_taken, stored = sem("oT_ready"), sem("v_spread"), sem("su_ready"), sem("su_taken"), sem("stored")
        block = ctx.enter_context(nc.Block())
        qpT, kpT, kp, vr = A["qpT"], A["kpT"], A["kp"], A["vr"]

        @block.sync
        def _(sp):
            sp.dma_start(weights[0], weights[1]).then_inc(weights[2], 16)
            sp.dma_start(gg[:, :], S["ret_gn_g"].to_broadcast([P, W])).then_inc(loaded, 16)
            sp.dma_start(gb[:, :], S["ret_gn_b"].to_broadcast([P, W])).then_inc(loaded, 16)
            for half in range(2):
                for b in range(DB):
                    sp.dma_start(s0[half * HD:(half + 1) * HD, b, :, :],
                                 S["state_ret"][b].rearrange("(pr hh) d e -> hh d pr e", hh=2)[half]).then_inc(loaded, 16)
            sp.wait_ge(blank_ready, 1)
            for v in range(NE, SLOTS):
                sp.dma_start(S["y"][v * CAP:(v + 1) * CAP, :], blank[:, :]).then_inc(stored, 16)
            sp.wait_ge(state_ready, NT)
            for half in range(2):
                sp.dma_start(S["ret_prompt"].rearrange("(pr hh) d e -> hh d pr e", hh=2)[half],
                             state[half * HD:(half + 1) * HD, :, :]).then_inc(stored, 16)
            sp.wait_ge(su_taken, PAIRS)
            for half in range(2):
                for b in range(DB):
                    sp.dma_start(S["ret_sample"][b].rearrange("(pr hh) d e -> hh d pr e", hh=2)[half],
                                 s0[half * HD:(half + 1) * HD, b, :, :]).then_inc(stored, 16)
            sp.wait_ge(stored, 16 * (2 + 2 * DB + OVER))

        @block.tensor
        def _(pe):
            def scores(i):
                n = rows_of(i)
                if i:
                    pe.wait_ge(intra_ready, i)
                for h in range(H):
                    half = slice(h % 2 * HD, h % 2 * HD + HD)
                    mm = nc.tensor.matmul(psI[:n, h % 2, h // 2, :n], kpT[half, h // 2, cols_of(i)],
                                          qpT[half, h // 2, cols_of(i)], start=True, stop=True)
                mm.then_inc(scores_ready, 1)

            def turn(i):
                n = rows_of(i)
                pe.wait_ge(on_ready, i + 1)
                if i:
                    pe.wait_ge(t_taken, i)
                for b in range(PAIRS):
                    mm = nc.tensor.transpose(psT[:, b, :n], on[:n, i % 2, b * P:(b + 1) * P], A["identity"][:n, :n])
                mm.then_inc(turned, 1)

            scores(0)
            for i in range(NT):
                scores_next = i + 1
                pe.wait_ge(intra_ready, i + 1)
                if i:
                    pe.wait_ge(state_ready, i)
                    pe.wait_ge(o_taken, i)
                for h in range(H):
                    half = slice(h % 2 * HD, h % 2 * HD + HD)
                    out = psO[:, h % 2, h // 2, :HD]
                    mm = nc.tensor.matmul(out, intra[:, h, :], vr[:, i, h * HD:(h + 1) * HD],
                                          start=True, stop=(i == 0))
                    if i:
                        mm = nc.tensor.matmul(out, qpT[half, h // 2, cols_of(i)], state[half, h // 2, :],
                                              start=False, stop=True)
                mm.then_inc(o_ready, 1)
                for pr in range(PAIRS):
                    mm = nc.tensor.matmul(psU[:, pr, :], kp[:, i, pr * P:(pr + 1) * P], vr[:, i, pr * P:(pr + 1) * P],
                                          start=True, stop=True)
                mm.then_inc(update_ready, 1)
                scores(scores_next)
                if i:
                    turn(i - 1)
            i = NT
            pe.wait_ge(intra_ready, i + 1)
            pe.wait_ge(o_taken, i)
            pe.wait_ge(loaded, 16 * (2 + 2 * DB))
            for h in range(H):
                mm = nc.tensor.matmul(psO[:HD, h % 2, h // 2, :HD], vr[:NS, i, h * HD:(h + 1) * HD], intra[:NS, h, :NS],
                                      start=(h < 2), stop=False, skip_group_check=True)
            mm.then_inc(intra_used, 1)
            pe.wait_ge(intra_used, 1)
            for h in range(H):
                half = slice(h % 2 * HD, h % 2 * HD + HD)
                for b in range(DB):
                    mm = nc.tensor.matmul(psO[:HD, h % 2, h // 2, b * DS:(b + 1) * DS], s0[half, b, h // 2, :],
                                          qpT[half, h // 2, SEQ + b * DS:SEQ + (b + 1) * DS],
                                          start=False, stop=(b == DB - 1), skip_group_check=True)
            mm.then_inc(o_ready, 1)
            turn(NT - 1)
            pe.wait_ge(oT_ready, 1)
            for h in range(H):
                mm = nc.tensor.transpose(psN[:NS, h * HD:(h + 1) * HD], oT[:, h * HD:(h + 1) * HD], A["identity"][:HD, :HD])
            mm.then_inc(o_ready, 1)
            for pr in range(PAIRS):
                pe.wait_ge(v_spread, 2 * (pr + 1))
                pe.wait_ge(state_ready, NT)
                if pr:
                    pe.wait_ge(su_taken, pr)
                for hh in range(2):
                    mm = nc.tensor.matmul(psU[hh * HD:(hh + 1) * HD, :, :].rearrange("p a b -> p (a b)"),
                                          kp[:NS, i, (2 * pr + hh) * HD:(2 * pr + hh + 1) * HD],
                                          vexp[:, hh, :, :].rearrange("p b e -> p (b e)"), start=True, stop=True)
                mm.then_inc(su_ready, 1)
            turn(NT)

        @block.scalar
        def _(act):
            for i in range(TILES):
                n = rows_of(i)
                if i == NT:
                    act.wait_ge(o_ready, NT + 1)
                    nc.scalar.activation(oT[:, :].rearrange("p (pr hh e) -> p hh pr e", hh=2, e=HD), psO[:HD, :, :, :HD], ACT.Copy).then_inc(oT_ready, 1)
                    act.wait_ge(o_ready, NT + 2)
                    act.wait_ge(on_ready, i)
                    nc.scalar.activation(o[:n, :], psN[:n, :], ACT.Copy).then_inc(o_taken, 1)
                else:
                    act.wait_ge(o_ready, i + 1)
                    if i:
                        act.wait_ge(on_ready, i)
                    nc.scalar.activation(o[:n, :].rearrange("p (pr hh e) -> p hh pr e", hh=2, e=HD), psO[:n, :, :, :HD], ACT.Copy).then_inc(o_taken, 1)
                act.wait_ge(var_ready, i + 1)
                nc.scalar.activation(st[:n, 2, :], st[:n, 1, :], ACT.Sqrt).then_inc(rooted, 1)
                act.wait_ge(turned, i + 1)
                nc.scalar.activation(A["retT"][:, :, cols_of(i)], psT[:, :, :n], ACT.Copy).then_inc(t_taken, 1)

        @block.vector
        def _(dve):
            link = Chain(dve, dve_done)
            link(nc.vector.memset(state[:, :, :], 0.0))
            nc.vector.memset(blank[:, :], 0.0).then_inc(blank_ready, 1)
            dve.wait_ge(loaded, 16 * (2 + 2 * DB))

            def mask(i):
                n = rows_of(i)
                dve.wait_ge(scores_ready, i + 1)
                if i:
                    dve.wait_ge(o_ready, i)
                m = A["ret_mask"][:n, 1 if i == NT else 0, :n].unsqueeze(1).to_broadcast([n, 4, n])
                link(nc.vector.tensor_tensor(intra[:n, 0:H:2, :n], psI[:n, 0, :, :n], m, ALU.mult))
                nc.vector.tensor_tensor(intra[:n, 1:H:2, :n], psI[:n, 1, :, :n], m, ALU.mult).then_inc(intra_ready, 1)

            mask(0)
            for i in range(TILES):
                n = rows_of(i)
                if i < NT:
                    dve.wait_ge(update_ready, i + 1)
                    for hh in range(2):
                        half = slice(hh * HD, (hh + 1) * HD)
                        link(nc.vector.tensor_tensor(state[half, :, :], psU[half, :, hh * HD:(hh + 1) * HD],
                                                     state[half, :, :], ALU.add))
                    nc.vector.tensor_tensor(state[:, :, :], state[:, :, :],
                                            A["gamma_chunk"][:, 0, :].unsqueeze(2).to_broadcast([P, PAIRS, HD]),
                                            ALU.mult).then_inc(state_ready, 1)
                    mask(i + 1)
                else:
                    for pr in range(PAIRS):
                        if pr:
                            dve.wait_ge(su_ready, pr)
                        for hh in range(2):
                            h = 2 * pr + hh
                            nc.vector.tensor_tensor(
                                vexp[:, hh, :, :], A["own_seq"][:NS, :].unsqueeze(2).to_broadcast([NS, DB, HD]),
                                vr[:NS, i, h * HD:(h + 1) * HD].unsqueeze(1).to_broadcast([NS, DB, HD]),
                                ALU.mult).then_inc(v_spread, 1)
                        dve.wait_ge(su_ready, pr + 1)
                        link(nc.vector.tensor_tensor(s0[:, :, pr, :], psU[:, :, :].rearrange("p a (b e) -> p (a b) e", e=HD),
                                                     s0[:, :, pr, :], ALU.add))
                        nc.vector.tensor_scalar(s0[:, :, pr, :], s0[:, :, pr, :], A["gamma_chunk"][:, 1, pr:pr + 1], None,
                                                ALU.mult).then_inc(su_taken, 1)
                dve.wait_ge(o_taken, i + 1)
                o3 = o[:n, :].rearrange("p (h e) -> p h e", h=H)
                q3 = o2[:n, :].rearrange("p (h e) -> p h e", h=H)
                bc = lambda a: a.unsqueeze(2).to_broadcast([n, H, HD])
                link(nc.vector.tensor_reduce(st[:n, 0, :], o3, AX_X, ALU.add))
                link(nc.vector.tensor_scalar(st[:n, 0, :], st[:n, 0, :], 1.0 / HD, None, ALU.mult))
                link(nc.vector.tensor_tensor(o3, o3, bc(st[:n, 0, :]), ALU.subtract))
                link(nc.vector.tensor_tensor(q3, o3, o3, ALU.mult))
                link(nc.vector.tensor_reduce(st[:n, 3, :], q3, AX_X, ALU.add))
                nc.vector.tensor_scalar(st[:n, 1, :], st[:n, 3, :], 1.0 / HD, GN_EPS, ALU.mult, ALU.add).then_inc(var_ready, 1)
                dve.wait_ge(rooted, i + 1)
                link(nc.vector.reciprocal(st[:n, 3, :], st[:n, 2, :]))
                link(nc.vector.tensor_tensor(q3, o3, bc(st[:n, 3, :]), ALU.mult))
                link(nc.vector.tensor_tensor(o2[:n, :], o2[:n, :], gg[:n, :], ALU.mult))
                link(nc.vector.tensor_tensor(o2[:n, :], o2[:n, :], gb[:n, :], ALU.add))
                if i >= 2:
                    dve.wait_ge(turned, i - 1)
                nc.vector.tensor_tensor(on[:n, i % 2, :], o2[:n, :], A["sg"][:n, i, :], ALU.mult).then_inc(on_ready, 1)


def index_scores(nc, S, A, X):
    blocks = list(range(TOPK // P, NT))
    chunks = [(i, k0, min(512, (i + 1) * P - k0)) for i in blocks for k0 in range(0, (i + 1) * P, 512)]
    units = [(i, k0, n, h) for i, k0, n in chunks for h in range(IH)]
    U = len(units)
    with ExitStack() as ctx:
        sb = lambda n, s, d=F32: ctx.enter_context(nc.sbuf_tensor("x_" + n, s, d))
        sem = stage_semaphores(nc, ctx, "x_")
        r = sb("r", [P, 3, 512])
        qs = sb("qs", [P, DB, IH, DS])
        ws = sb("ws", [P, 2])
        kx = sb("kx", [P, 2, 16, 64])
        kxT = sb("kxT", [P, 4, 8, P])
        wsum = sb("wsum", [P, 2, 512])
        psS = ctx.enter_context(nc.psum_tensor("x_psS", [P, 3, 512], F32))
        psK = ctx.enter_context(nc.psum_tensor("x_psK", [P, 2, 4, P], F32))
        psQ = ctx.enter_context(nc.psum_tensor("x_psQ", [P, 2, 512], F32))
        psR = ctx.enter_context(nc.psum_tensor("x_psR", [NS, 512], F32))
        s_ready, s_taken, r_used, dve_done = sem("s_ready"), sem("s_taken"), sem("r_used"), sem("dve_done")
        q_loaded, w_loaded = sem("q_loaded"), sem("w_loaded")
        kx_loaded = [sem(f"kx_loaded{j}") for j in range(2)]
        kx_turned, kxT_ready = sem("kx_turned"), sem("kxT_ready")
        heads_ready, heads_weighed, row_ready, row_taken = sem("heads_ready"), sem("heads_weighed"), sem("row_ready"), sem("row_taken")
        block = ctx.enter_context(nc.Block())
        parts = [(half, rr) for half in range(2) for rr in (0, 4)] + [None]

        @block.sync
        def _(sp):
            with nc.allow_non_contiguous_dma(reason="small pieces of the sample queries"):
                for half in range(2):
                    for h in range(IH):
                        sp.dma_start(qs[half * 64:half * 64 + 64, :, h, :],
                                     A["qiT"][h % 2 * 64:h % 2 * 64 + 64, h // 2, SEQ:].rearrange("p (b t) -> p b t", b=DB)
                                     ).then_inc(q_loaded, 16)
                for b in range(DB):
                    for h in range(IH):
                        row = b % 4 * 32 + h * DS
                        sp.dma_start(ws[row:row + DS, b // 4:b // 4 + 1], A["wi"][b * DS:(b + 1) * DS, NT, h:h + 1]
                                     ).then_inc(w_loaded, 16)

        @block.gpsimd
        def _(pool):
            for b in range(DB):
                if b >= 2:
                    pool.wait_ge(kx_turned, 2 * (b - 1))
                pool.indirect_dma_start(kx[:, b % 2, :, :].rearrange("p r e -> p (r e)"), None, S["cache_kidx"],
                                        bass.IndirectOffsetOnAxis(ap=A["row_id"][:, b:b + 1], axis=0)
                                        ).then_inc(kx_loaded[b % 2], 16)

        @block.tensor
        def _(pe):
            for u, (i, k0, n, h) in enumerate(units):
                if u >= 3:
                    pe.wait_ge(s_taken, u - 2)
                half = slice(h % 2 * 64, h % 2 * 64 + 64)
                nc.tensor.matmul(psS[:, u % 3, :n], A["qiT"][half, h // 2, cols_of(i)],
                                 A["kiT"][half, k0:k0 + n], start=True, stop=True).then_inc(s_ready, 1)
            pe.wait_ge(q_loaded, 16 * 2 * IH)

            def sum_heads(m, g, part):
                pe.wait_ge(heads_weighed, m + 1)
                if m:
                    pe.wait_ge(row_taken, m)
                n = 512 if part else NS
                nc.tensor.matmul(psR[32 * g:32 * g + 32, :n], A["sum_heads"][:, :], wsum[:, m % 2, :n],
                                 start=True, stop=True).then_inc(row_ready, 1)

            m = 0
            for g in range(2):
                for bb in range(4):
                    b = 4 * g + bb
                    pe.wait_ge(kx_loaded[b % 2], 16 * (b // 2 + 1))
                    for j in range(2):
                        q = 2 * b + j
                        if q >= 2:
                            pe.wait_ge(kxT_ready, q - 1)
                        for rr in range(4):
                            e0 = (4 * j + rr) * 2
                            mm = nc.tensor.transpose(psK[:, j, rr, :], kx[:, b % 2, e0:e0 + 2, :].rearrange("p r e -> p (r e)"),
                                                     A["identity"][:, :])
                        mm.then_inc(kx_turned, 1)
                pe.wait_ge(kxT_ready, 8 * (g + 1))
                for k, part in enumerate(parts):
                    if m >= 2:
                        pe.wait_ge(heads_weighed, m - 1)
                    for bb in range(4):
                        half = slice((part[0] if part else 0) * 64, (part[0] if part else 0) * 64 + 64)
                        rhs = (kxT[half, bb, part[1]:part[1] + 4, :].rearrange("p r k -> p (r k)") if part
                               else A["kiT"][half, SEQ:])
                        mm = nc.tensor.matmul(psQ[bb * 32:bb * 32 + 32, m % 2, :rhs.shape[1]],
                                              qs[half, 4 * g + bb, :, :].rearrange("p h t -> p (h t)"), rhs,
                                              start=True, stop=True)
                    mm.then_inc(heads_ready, 1)
                    if k:
                        sum_heads(m - 1, g, parts[k - 1])
                    m += 1
                sum_heads(m - 1, g, parts[-1])

        @block.scalar
        def _(act):
            for u, (i, k0, n, h) in enumerate(units):
                act.wait_ge(s_ready, u + 1)
                if u >= 3:
                    act.wait_ge(r_used, u - 2)
                nc.scalar.activation(r[:, u % 3, :n], psS[:, u % 3, :n], ACT.Relu).then_inc(s_taken, 1)
            m = 0
            for g in range(2):
                for q in range(8 * g, 8 * g + 8):
                    act.wait_ge(kx_turned, q + 1)
                    if g:
                        act.wait_ge(heads_ready, 5)
                    nc.scalar.activation(kxT[:, (q // 2) % 4, 4 * (q % 2):4 * (q % 2) + 4, :], psK[:, q % 2, :, :],
                                         ACT.Copy).then_inc(kxT_ready, 1)
                for part in parts:
                    act.wait_ge(row_ready, m + 1)
                    rows = slice(32 * g, 32 * g + 32)
                    if part:
                        dst = X["sc_s"][rows, :PAST].rearrange("q (k rr hf) -> q hf rr k", hf=2, rr=8)[:, part[0], part[1]:part[1] + 4, :]
                        src = psR[rows, :].rearrange("q (rr k) -> q rr k", rr=4)
                    else:
                        dst, src = X["sc_s"][rows, PAST:], psR[rows, :NS]
                    nc.scalar.activation(dst, src, ACT.Copy).then_inc(row_taken, 1)
                    m += 1

        @block.vector
        def _(dve):
            link = Chain(dve, dve_done)
            link(nc.vector.memset(X["lo"][:, :], 0.0))
            link(nc.vector.memset(X["hi"][:, :], 0.0))
            for u, (i, k0, n, h) in enumerate(units):
                dve.wait_ge(s_taken, u + 1)
                acc = X["sc"](i)[:, k0:k0 + n]
                if h == 0:
                    ins = nc.vector.tensor_scalar(acc, r[:, u % 3, :n], A["wi"][:, i, h:h + 1], None, ALU.mult)
                else:
                    ins = nc.vector.scalar_tensor_tensor(acc, r[:, u % 3, :n], A["wi"][:, i, h:h + 1], acc, ALU.mult, ALU.add)
                ins.then_inc(r_used, 1)
                dve.wait_ge(r_used, u + 1)
            for i in blocks:
                sc = X["sc"](i)
                nc.vector.tensor_reduce(X["lo"][:, i:i + 1], sc, AX_X, ALU.min)
                link(nc.vector.tensor_reduce(X["hi"][:, i:i + 1], sc, AX_X, ALU.max))
                d = sc[:, i * P:]
                link(nc.vector.tensor_tensor(d, d, A["causal"][:, :], ALU.add))
            dve.wait_ge(w_loaded, 16 * DB * IH)
            m = 0
            for g in range(2):
                for part in parts:
                    n = 512 if part else NS
                    dve.wait_ge(heads_ready, m + 1)
                    if m >= 2:
                        dve.wait_ge(row_ready, m - 1)
                    nc.vector.tensor_scalar(wsum[:, m % 2, :n], psQ[:, m % 2, :n], 0.0, ws[:, g:g + 1], ALU.max, ALU.mult
                                            ).then_inc(heads_weighed, 1)
                    m += 1
            dve.wait_ge(row_taken, m)
            link(nc.vector.tensor_reduce(X["lo"][:NS, NT:NT + 1], X["sc_s"][:, :], AX_X, ALU.min))
            link(nc.vector.tensor_reduce(X["hi"][:NS, NT:NT + 1], X["sc_s"][:, :], AX_X, ALU.max))
            d = X["sc_s"][:, PAST:]
            link(nc.vector.tensor_tensor(d, d, A["causal_s"][:NS, :], ALU.add))


def bisection(nc, sb, sem, X):
    def view(i):
        return X["sc"](i) if i < NT else X["sc_s"][:, :]

    blocks = list(range(TOPK // P, NT))
    on_act = [NT, NT - 1, blocks[1]]
    on_dve = [i for i in blocks if i not in on_act]
    c0 = blocks[0]
    two, mid, nmid, count = sb("two", [P, TILES]), sb("mid", [P, TILES]), sb("nmid", [P, TILES]), sb("count", [P, TILES])
    want, up, down = sb("want", [P, TILES]), sb("up", [P, TILES]), sb("down", [P, TILES])
    junk = sb("junk", [P, sum(view(i).shape[1] for i in on_dve)], BF16)
    junk_at = [sum(view(i).shape[1] for i in on_dve[:j]) for j in range(len(on_dve) + 1)]
    junk_act = sb("junk_act", [P, NK], BF16)
    mid_ready, act_counted, dve_step = sem("mid_ready"), sem("act_counted"), sem("dve_step")
    lo, hi = X["lo"], X["hi"]
    STEPS = 2 + len(on_dve) + 6

    def act_step(act, it):
        act.wait_ge(mid_ready, it + 1)
        for j, i in enumerate(on_act):
            n = rows_of(i)
            if it or j:
                act.wait_ge(act_counted, it * len(on_act) + j)
            nc.scalar.activation(junk_act[:n, :view(i).shape[1]], view(i), ACT.Sign, bias=nmid[:n, i:i + 1],
                                 accum_out=count[:n, i:i + 1]).then_inc(act_counted, 1)

    def dve_begin(link):
        for i in blocks + [NT]:
            n = view(i).shape[1]
            link(nc.vector.memset(want[:, i:i + 1], float(2 * TOPK - n if i in on_act else TOPK)))
        link(nc.vector.memset(count[:, :], 0.0))

    def dve_step_of(dve, it):
        base = it * STEPS
        nc.vector.tensor_tensor(two[:, c0:], lo[:, c0:], hi[:, c0:], ALU.add).then_inc(dve_step, 1)
        dve.wait_ge(dve_step, base + 1)
        nc.vector.tensor_scalar(nmid[:, c0:], two[:, c0:], -0.5, None, ALU.mult).then_inc(mid_ready, 1)
        nc.vector.tensor_scalar(mid[:, c0:], two[:, c0:], 0.5, None, ALU.mult).then_inc(dve_step, 1)
        dve.wait_ge(dve_step, base + 2)
        for j, i in enumerate(on_dve):
            nc.vector.tensor_scalar(junk[:, junk_at[j]:junk_at[j + 1]], view(i), mid[:, i:i + 1], None, ALU.is_ge, ALU.add,
                                    accum_out=count[:, i:i + 1]).then_inc(dve_step, 1)
        dve.wait_ge(dve_step, base + (2 + len(on_dve)))
        dve.wait_ge(act_counted, it * len(on_act) + len(on_act))
        nc.vector.tensor_tensor(up[:, c0:], count[:, c0:], want[:, c0:], ALU.is_ge).then_inc(dve_step, 1)
        nc.vector.tensor_tensor(down[:, c0:], count[:, c0:], want[:, c0:], ALU.is_lt).then_inc(dve_step, 1)
        dve.wait_ge(dve_step, base + (4 + len(on_dve)))
        nc.vector.scalar_tensor_tensor(down[:, c0:], down[:, c0:], NEG, mid[:, c0:], ALU.mult, ALU.add).then_inc(dve_step, 1)
        nc.vector.scalar_tensor_tensor(up[:, c0:], up[:, c0:], -NEG, mid[:, c0:], ALU.mult, ALU.add).then_inc(dve_step, 1)
        dve.wait_ge(dve_step, base + (6 + len(on_dve)))
        nc.vector.tensor_tensor(lo[:, c0:], lo[:, c0:], down[:, c0:], ALU.max).then_inc(dve_step, 1)
        nc.vector.tensor_tensor(hi[:, c0:], hi[:, c0:], up[:, c0:], ALU.min).then_inc(dve_step, 1)
        dve.wait_ge(dve_step, base + STEPS)

    return act_step, dve_begin, dve_step_of


def select_keys(nc, sb, link, A, X):
    blocks = list(range(TOPK // P, NT))
    count, want, above, band, before = sb
    lo, hi = X["lo"], X["hi"]

    def view(i):
        return X["sc"](i) if i < NT else X["sc_s"][:, :]

    for i in blocks + [NT]:
        s = view(i)
        r, n = s.shape[0], s.shape[1]
        a, bd, be = above[:r, :n], band[:r, :n], before[:r, :n]
        link(nc.vector.tensor_scalar(a, s, hi[:r, i:i + 1], None, ALU.is_gt, ALU.add, accum_out=count[:r, i:i + 1]))
        link(nc.vector.scalar_tensor_tensor(bd, s, lo[:r, i:i + 1], a, ALU.is_ge, ALU.subtract))
        link(nc.vector.tensor_tensor_scan(be, bd, bd, 0.0, ALU.add, ALU.max))
        link(nc.vector.tensor_scalar(want[:r, i:i + 1], count[:r, i:i + 1], -1.0, float(TOPK), ALU.mult, ALU.add))
        link(nc.vector.scalar_tensor_tensor(bd, be, want[:r, i:i + 1], bd, ALU.is_le, ALU.mult))
        link(nc.vector.tensor_tensor(a, a, bd, ALU.add))
        if i < NT:
            link(nc.vector.tensor_scalar(X["mask"](i), a, -1.0, -NEG, ALU.add, ALU.mult))
        else:
            link(nc.vector.tensor_scalar(X["mask_s"][:, :PAST].rearrange("q (r k) -> q k r", r=16),
                                         a[:, :PAST].rearrange("q (k r) -> q k r", r=16), -1.0, -NEG, ALU.add, ALU.mult))
            link(nc.vector.tensor_scalar(X["mask_s"][:, PAST:], a[:, PAST:], -1.0, -NEG, ALU.add, ALU.mult))


def make_bias(nc, S, A, X, T):
    LP, LS = SEQ + P, PAST + 2 * DS
    HOT = PAST + DS + P
    with ExitStack() as ctx:
        sb = lambda n, s, d=F32: ctx.enter_context(nc.sbuf_tensor("b_" + n, s, d))
        sem = stage_semaphores(nc, ctx, "b_")
        rb = sb("rb", [32, H])
        rep = sb("rep", [32, H, P])
        rep_s = sb("rep_s", [32, H, DS])
        hot = sb("hot", [32, HOT])
        row = sb("row", [P, 2, LP])
        row_s = sb("row_s", [NS, LS])
        chosen = [sb(n, [P, w]) for n, w in (("count", TILES), ("want", TILES), ("above", NK), ("band", NK), ("before", NK))]
        ps = ctx.enter_context(nc.psum_tensor("b_ps", [P, 2, 512], F32))
        loaded, spread, ready, taken = sem("loaded"), sem("spread"), sem("ready"), sem("taken")
        wrote = [sem(f"wrote{j}") for j in range(2)]
        read, wrote_s, dve_done = sem("read"), sem("wrote_s"), sem("dve_done")
        block = ctx.enter_context(nc.Block())
        first = PAST + DS - SEQ
        jobs = [(h, a, min(512, LP - a)) for h in range(H) for a in range(0, LP, 512)]
        jobs_s = [(a, min(512, LS - a)) for a in range(0, LS, 512)]

        @block.sync
        def _(sp):
            sp.dma_start(rb[:, :], S["rel_bias"]).then_inc(loaded, 16)
            sp.dma_start(hot[:, :], S["c_onehot"]).then_inc(loaded, 16)
            per = len(jobs) // H

            def read_skewed(h):
                sp.wait_ge(wrote[h % 2], 16 * (h // 2 + 1))
                src = S["skew"][h].rearrange("p l -> (p l)")
                src = src[P - 1:P - 1 + P * (LP - 1)].rearrange("(p l) -> p l", l=LP - 1)[:, :SEQ]
                sp.dma_start(T["bias"][:, h, :], src).then_inc(read, 16)

            for h in range(H):
                sp.wait_ge(taken, per * (h + 1))
                sp.dma_start(S["skew"][h], row[:, h % 2, :]).then_inc(wrote[h % 2], 16)
                if h:
                    read_skewed(h - 1)
            sp.wait_ge(taken, len(jobs) + len(jobs_s))
            sp.dma_start(S["skew_s"], row_s[:, :]).then_inc(wrote_s, 16)
            read_skewed(H - 1)
            sp.wait_ge(wrote_s, 16)
            sp.wait_ge(read, 16 * H)

        @block.tensor
        def _(pe):
            pe.wait_ge(spread, 2)
            for j, (h, a, n) in enumerate(jobs):
                if j >= 2:
                    pe.wait_ge(taken, j - 1)
                nc.tensor.matmul(ps[:, j % 2, :n], rep[:, h, :], hot[:, first + a:first + a + n],
                                 start=True, stop=True).then_inc(ready, 1)
            for q, (a, n) in enumerate(jobs_s):
                j = len(jobs) + q
                pe.wait_ge(taken, j - 1)
                nc.tensor.matmul(ps[:NS, j % 2, :n], rep_s[:, :, :].rearrange("k h t -> k (h t)"), hot[:, a:a + n],
                                 start=True, stop=True).then_inc(ready, 1)

        @block.scalar
        def _(act):
            for j, (h, a, n) in enumerate(jobs):
                act.wait_ge(ready, j + 1)
                if a == 0 and h >= 2:
                    act.wait_ge(wrote[h % 2], 16 * (h // 2))
                nc.scalar.activation(row[:, h % 2, a:a + n], ps[:, j % 2, :n], ACT.Copy).then_inc(taken, 1)
            for q, (a, n) in enumerate(jobs_s):
                j = len(jobs) + q
                act.wait_ge(ready, j + 1)
                nc.scalar.activation(row_s[:, a:a + n], ps[:NS, j % 2, :n], ACT.Copy).then_inc(taken, 1)

        @block.vector
        def _(dve):
            dve.wait_ge(loaded, 32)
            nc.vector.tensor_copy(rep[:, :, :], rb[:, :].unsqueeze(2).to_broadcast([32, H, P])).then_inc(spread, 1)
            nc.vector.tensor_copy(rep_s[:, :, :], rb[:, :].unsqueeze(2).to_broadcast([32, H, DS])).then_inc(spread, 1)
            select_keys(nc, chosen, Chain(dve, dve_done), A, X)


def prompt_attention(nc, A, X, T):
    units = [(i, h) for i in reversed(range(NT)) for h in range(H)]
    place = lambda i: NT - 1 - i
    turns = [(u, b0, min(4, units[u][0] + 1 - b0)) for u in range(len(units)) for b0 in range(0, units[u][0] + 1, 4)]
    turns_before = [sum(1 for t in turns if t[0] < u) for u in range(len(units) + 1)]
    with ExitStack() as ctx:
        sb = lambda n, s, d=F32: ctx.enter_context(nc.sbuf_tensor("a_" + n, s, d))
        sem = stage_semaphores(nc, ctx, "a_")
        logit = sb("logit", [P, 2, SEQ])
        prob = sb("prob", [P, 2, SEQ])
        probT = sb("probT", [P, 2, NT, P])
        peak = sb("peak", [P, 2])
        neg = sb("neg", [P, 2])
        total = sb("total", [P, 2, H])
        inv = sb("inv", [P, H])
        o = sb("o", [P, 2, W])
        psS = [ctx.enter_context(nc.psum_tensor(f"a_psS{j}", [P, SEQ], F32)) for j in range(2)]
        psT = ctx.enter_context(nc.psum_tensor("a_psT", [P, 2, 4, P], F32))
        psO = ctx.enter_context(nc.psum_tensor("a_psO", [P, W], F32))
        psA = ctx.enter_context(nc.psum_tensor("a_psA", [P, PAIRS, P], F32))
        s_ready, l_ready, neg_ready, p_ready = sem("s_ready"), sem("l_ready"), sem("neg_ready"), sem("p_ready")
        turned, t_taken, o_ready, o_scaled = sem("turned"), sem("t_taken"), sem("o_ready"), sem("o_scaled")
        a_ready, a_taken, dve_done = sem("a_ready"), sem("a_taken"), sem("dve_done")
        block = ctx.enter_context(nc.Block())

        @block.tensor
        def _(pe):
            def scores(u):
                i, h = units[u]
                half = slice(h % 2 * HD, h % 2 * HD + HD)
                if u >= 2:
                    pe.wait_ge(l_ready, u - 1)
                for k0 in range(0, (i + 1) * P, 512):
                    n = min(512, (i + 1) * P - k0)
                    diagonal = i < TOPK // P and k0 + n == (i + 1) * P
                    masked = i >= TOPK // P or diagonal
                    mm = nc.tensor.matmul(psS[u % 2][:, k0:k0 + n], A["qaT"][half, h // 2, cols_of(i)],
                                          A["kaT"][half, h // 2, k0:k0 + n], start=True, stop=not masked,
                                          skip_group_check=True)
                    if diagonal:
                        mm = nc.tensor.matmul(psS[u % 2][:, i * P:(i + 1) * P], A["identity_b"][:, :], A["causal_b"][:, :],
                                              start=False, stop=True, skip_group_check=True)
                    elif masked:
                        mm = nc.tensor.matmul(psS[u % 2][:, k0:k0 + n], A["identity_b"][:, :], X["mask"](i)[:, k0:k0 + n],
                                              start=False, stop=True, skip_group_check=True)
                mm.then_inc(s_ready, 1)

            def turn(u):
                pe.wait_ge(p_ready, u + 1)
                for t in range(turns_before[u], turns_before[u + 1]):
                    _, b0, nb = turns[t]
                    if t >= 2:
                        pe.wait_ge(t_taken, t - 1)
                    for b in range(nb):
                        mm = nc.tensor.transpose(psT[:, t % 2, b, :], prob[:, u % 2, (b0 + b) * P:(b0 + b + 1) * P],
                                                 A["identity"][:, :])
                    mm.then_inc(turned, 1)

            def values(u):
                i, h = units[u]
                pe.wait_ge(t_taken, turns_before[u + 1])
                if h == 0 and place(i):
                    pe.wait_ge(o_scaled, place(i))
                for b in range(i + 1):
                    mm = nc.tensor.matmul(psO[:, h * HD:(h + 1) * HD], probT[:, u % 2, b, :], A["va"][:, b, h * HD:(h + 1) * HD],
                                          start=(b == 0), stop=(b == i))
                if h == H - 1:
                    mm.then_inc(o_ready, 1)

            def turn_out(i):
                pe.wait_ge(o_scaled, place(i) + 1)
                if place(i):
                    pe.wait_ge(a_taken, place(i))
                for b in range(PAIRS):
                    mm = nc.tensor.transpose(psA[:, b, :], o[:, place(i) % 2, b * P:(b + 1) * P], A["identity"][:, :])
                mm.then_inc(a_ready, 1)

            scores(0)
            for u in range(len(units)):
                if u + 1 < len(units):
                    scores(u + 1)
                turn(u)
                if u:
                    values(u - 1)
                i, h = units[u]
                if h == 2 and place(i):
                    turn_out(i + 1)
            values(len(units) - 1)
            turn_out(0)

        def take(act, u):
            for t in range(turns_before[u], turns_before[u + 1]):
                _, b0, nb = turns[t]
                act.wait_ge(turned, t + 1)
                nc.scalar.activation(probT[:, u % 2, b0:b0 + nb, :], psT[:, t % 2, :nb, :], ACT.Copy).then_inc(t_taken, 1)

        def take_out(act, i):
            act.wait_ge(a_ready, place(i) + 1)
            nc.scalar.activation(A["attT"][:, :, cols_of(i)], psA[:, :, :], ACT.Copy).then_inc(a_taken, 1)

        @block.scalar
        def _(act):
            for u, (i, h) in enumerate(units):
                n = (i + 1) * P
                act.wait_ge(neg_ready, u + 1)
                if u >= 2:
                    act.wait_ge(turned, turns_before[u - 1])
                if h == 0 and place(i) >= 2:
                    act.wait_ge(o_scaled, place(i) - 1)
                nc.scalar.activation(prob[:, u % 2, :n], logit[:, u % 2, :n], ACT.Exp, bias=neg[:, u % 2:u % 2 + 1],
                                     accum_out=total[:, place(i) % 2, h:h + 1]).then_inc(p_ready, 1)
                if u:
                    take(act, u - 1)
                if h == 3 and place(i):
                    take_out(act, i + 1)
            take(act, len(units) - 1)
            take_out(act, 0)

        @block.vector
        def _(dve):
            link = Chain(dve, dve_done)

            def scale_out(i):
                dve.wait_ge(o_ready, place(i) + 1)
                link(nc.vector.reciprocal(inv[:, :], total[:, place(i) % 2, :]))
                if place(i) >= 2:
                    dve.wait_ge(a_ready, place(i) - 1)
                nc.vector.tensor_tensor(o[:, place(i) % 2, :].rearrange("p (h e) -> p h e", h=H),
                                        psO[:, :].rearrange("p (h e) -> p h e", h=H),
                                        inv[:, :].unsqueeze(2).to_broadcast([P, H, HD]), ALU.mult).then_inc(o_scaled, 1)

            for u, (i, h) in enumerate(units):
                n, off = (i + 1) * P, SEQ - (i + 1) * P
                dve.wait_ge(s_ready, u + 1)
                if u >= 2:
                    dve.wait_ge(p_ready, u - 1)
                nc.vector.tensor_tensor_reduce(logit[:, u % 2, :n], psS[u % 2][:, :n], T["bias"][:, h, off:off + n],
                                               1.0, NEG, ALU.add, ALU.max, peak[:, u % 2:u % 2 + 1]).then_inc(l_ready, 1)
                dve.wait_ge(l_ready, u + 1)
                nc.vector.tensor_scalar(neg[:, u % 2:u % 2 + 1], peak[:, u % 2:u % 2 + 1], -1.0, None, ALU.mult).then_inc(neg_ready, 1)
                if h == 1 and place(i):
                    scale_out(i + 1)
            scale_out(0)


def sample_attention(nc, S, A, X):
    R = 16
    loads = [(kind, b - (kind == "v"), c) for b in range(DB + 1) for kind in "kv" for c in range(4)]
    loads = [(kind, b, c) for kind, b, c in loads if 0 <= b < DB]
    index = {load: n for n, load in enumerate(loads)}
    strip = lambda pr: slice(32 * pr, 32 * pr + 32)
    pair = lambda pr: slice(pr * P, (pr + 1) * P)
    with ExitStack() as ctx:
        sb = lambda n, s, d=F32: ctx.enter_context(nc.sbuf_tensor("s_" + n, s, d))
        sem = stage_semaphores(nc, ctx, "s_")
        ring = sb("ring", [P, PAGE_RING, 4, W])
        kcT = sb("kcT", [P, 2, PAIRS, 512])
        logit = sb("logit", [P, NK])
        probT = sb("probT", [P, R + 1, P])
        qd = sb("qd", [P, 2, PAIRS, 32])
        st = sb("st", [P, 2, 4])
        bias = sb("bias", [P, NK])
        o_rows = sb("o_rows", [P, P])
        psK = ctx.enter_context(nc.psum_tensor("s_psK", [P, 2, 512], F32))
        psS = ctx.enter_context(nc.psum_tensor("s_psS", [P, 5 * 512], F32))
        psV = ctx.enter_context(nc.psum_tensor("s_psV", [P, 512], F32))
        slot_loaded = [sem(f"slot{j}_loaded") for j in range(PAGE_RING)]
        zeroed, q_spread = sem("zeroed"), sem("q_spread")
        k_turned, k_scored, s_ready, l_ready = sem("k_turned"), sem("k_scored"), sem("s_ready"), sem("l_ready")
        k_taken = [sem("k_taken_by_act"), sem("k_taken_by_dve")]
        neg_ready, e_ready, p_turned, p_taken = sem("neg_ready"), sem("e_ready"), sem("p_turned"), sem("p_taken")
        o_ready, o_normed, o_turned, o_taken = sem("o_ready"), sem("o_normed"), sem("o_turned"), sem("o_taken")
        dve_done, bias_loaded = sem("dve_done"), sem("bias_loaded")
        block = ctx.enter_context(nc.Block())

        @block.sync
        def _(sp):
            L = PAST + 2 * DS
            sp.wait_ge(zeroed, 3)
            for h in range(H):
                src = S["skew_s"][h * DS:(h + 1) * DS, :].rearrange("p l -> (p l)")
                src = src[DS - 1:DS - 1 + DS * (L - 1)].rearrange("(p l) -> p l", l=L - 1)
                row = 32 * (h // 2) + DS * (h % 2)
                sp.dma_start(logit[row:row + DS, :PAST + DS], src[:, :PAST + DS]).then_inc(bias_loaded, 16)

        @block.gpsimd
        def _(pool):
            for n, (kind, b, c) in enumerate(loads):
                if n >= PAGE_RING:
                    was, wb, wc = loads[n - PAGE_RING]
                    if was == "k":
                        pool.wait_ge(k_turned, 16 * wb + 4 * wc + 4)
                    else:
                        pool.wait_ge(o_ready, wb + 1)
                pool.indirect_dma_start(ring[:, n % PAGE_RING, :, :].rearrange("p r e -> p (r e)"), None, S["cache_" + kind],
                                        bass.IndirectOffsetOnAxis(ap=A["quarter_id"][:, c, b:b + 1], axis=0)
                                        ).then_inc(slot_loaded[n % PAGE_RING], 16)

        @block.tensor
        def _(pe):
            def slot_of(kind, b, c):
                n = index[kind, b, c]
                pe.wait_ge(slot_loaded[n % PAGE_RING], 16 * (n // PAGE_RING + 1))
                return n % PAGE_RING

            def turn_keys(b, c):
                slot = slot_of("k", b, c)
                for pr in range(PAIRS):
                    q = 16 * b + 4 * c + pr
                    if q >= 2:
                        pe.wait_ge(k_taken[q % 2], q // 2)
                    for r in range(4):
                        mm = nc.tensor.transpose(psK[:, q % 2, r * P:(r + 1) * P], ring[:, slot, r, pair(pr)], A["identity"][:, :])
                    mm.then_inc(k_turned, 1)

            def score(b, c):
                cols = slice(c * 512, (c + 1) * 512) if c < 4 else slice(PAST, NK)
                if c == 0 and b:
                    pe.wait_ge(l_ready, b)
                if c < 4:
                    for j in range(2):
                        pe.wait_ge(k_taken[j], 2 * (4 * b + c) + 2)
                nc.tensor.matmul(psS[:, cols], A["own_rows"][:, b, :], X["mask_s"][:, cols],
                                 start=True, stop=False, skip_group_check=True)
                for pr in range(PAIRS):
                    keys = kcT[:, c % 2, pr, :] if c < 4 else A["kaT_s"][:, pr, :]
                    mm = nc.tensor.matmul(psS[strip(pr), cols], qd[:, b % 2, pr, :], keys, start=False, stop=(pr == PAIRS - 1),
                                          tile_position=(0, 32 * pr), skip_group_check=True)
                mm.then_inc(k_scored if c < 4 else s_ready, 1)

            def turn_probs(b, t):
                pe.wait_ge(e_ready, b + 1)
                if b or t:
                    pe.wait_ge(p_taken, 5 * b + t)
                if t == 0 and b:
                    pe.wait_ge(o_taken, b)
                for r in range(4 if t < 4 else 1):
                    k = 4 * t + r
                    rows = P if k < R else NS
                    mm = nc.tensor.transpose(psV[:rows, r * P:(r + 1) * P], logit[:, k * P:k * P + rows], A["identity"][:, :])
                mm.then_inc(p_turned, 1)

            def sum_values(b):
                slot = [slot_of("v", b, c) for c in range(4)]
                pe.wait_ge(p_taken, 5 * b + 5)
                for r in range(R + 1):
                    for pr in range(PAIRS):
                        rows = P if r < R else NS
                        value = ring[:, slot[r // 4], r % 4, pair(pr)] if r < R else A["va_s"][:NS, pair(pr)]
                        mm = nc.tensor.matmul(psV[strip(pr), :P], probT[:rows, r, strip(pr)], value,
                                              start=(r == 0), stop=(r == R), tile_position=(0, 32 * pr), skip_group_check=True)
                mm.then_inc(o_ready, 1)

            def turn_output(b):
                pe.wait_ge(o_normed, b + 1)
                nc.tensor.transpose(psV[:, P:2 * P], o_rows[:, :], A["identity"][:, :]).then_inc(o_turned, 1)

            for b in range(DB + 1):
                if b < DB:
                    turn_keys(b, 0)
                if b >= 2:
                    turn_output(b - 2)
                if b < DB:
                    pe.wait_ge(q_spread, b + 1)
                for c in range(4):
                    if b < DB and c < 3:
                        turn_keys(b, c + 1)
                    if b:
                        turn_probs(b - 1, c)
                    if b < DB:
                        score(b, c)
                if b:
                    turn_probs(b - 1, 4)
                if b < DB:
                    score(b, 4)
                if b:
                    sum_values(b - 1)
            turn_output(DB - 1)

        @block.scalar
        def _(act):
            for b in range(DB):
                for c in range(4):
                    n = 4 * b + c
                    for pr in (0, 2):
                        act.wait_ge(k_turned, 16 * b + 4 * c + pr + 1)
                        if n >= 2:
                            act.wait_ge(k_scored, n - 1)
                        nc.scalar.activation(kcT[:, c % 2, pr, :], psK[:, 0, :], ACT.Copy).then_inc(k_taken[0], 1)
                act.wait_ge(neg_ready, b + 1)
                nc.scalar.activation(logit[:, :], logit[:, :], ACT.Exp, bias=st[:, b % 2, 1:2], accum_out=st[:, b % 2, 2:3]
                                     ).then_inc(e_ready, 1)

        @block.vector
        def _(dve):
            link = Chain(dve, dve_done)
            for j in range(2):
                nc.vector.memset(qd[:, j, :, :], 0.0).then_inc(zeroed, 1)
            nc.vector.memset(logit[:, :], 0.0).then_inc(zeroed, 1)
            dve.wait_ge(zeroed, 3)

            def spread_q(b):
                for hh in range(2):
                    half = slice(hh * HD, (hh + 1) * HD)
                    ins = nc.vector.tensor_copy(qd[half, b % 2, :, hh * DS:(hh + 1) * DS],
                                                A["qaT_s"][half, :, b * DS:(b + 1) * DS])
                ins.then_inc(q_spread, 1)

            def take_keys(b, c):
                n = 4 * b + c
                for pr in (1, 3):
                    dve.wait_ge(k_turned, 16 * b + 4 * c + pr + 1)
                    if n >= 2:
                        dve.wait_ge(k_scored, n - 1)
                    nc.vector.tensor_copy(kcT[:, c % 2, pr, :], psK[:, 1, :]).then_inc(k_taken[1], 1)

            def take_probs(b, t):
                n, rows = (4, P) if t < 4 else (1, NS)
                dve.wait_ge(p_turned, 5 * b + t + 1)
                if t == 0 and b:
                    dve.wait_ge(o_ready, b)
                nc.vector.tensor_copy(probT[:rows, 4 * t:4 * t + n, :],
                                      psV[:rows, :n * P].rearrange("p (r q) -> p r q", r=n)).then_inc(p_taken, 1)

            def norm_output(b):
                dve.wait_ge(o_ready, b + 1)
                if b:
                    dve.wait_ge(o_turned, b)
                nc.vector.tensor_scalar(o_rows[:, :], psV[:, :P], st[:, b % 2, 3:4], None, ALU.mult).then_inc(o_normed, 1)

            def take_output(b):
                dve.wait_ge(o_turned, b + 1)
                for hh in range(2):
                    half = slice(hh * HD, (hh + 1) * HD)
                    ins = nc.vector.tensor_copy(
                        A["attT"][half, :, SEQ + b * DS:SEQ + (b + 1) * DS],
                        psV[half, P:2 * P].rearrange("p (pr x) -> p pr x", pr=PAIRS)[:, :, hh * DS:(hh + 1) * DS])
                ins.then_inc(o_taken, 1)

            spread_q(0)
            for b in range(DB + 1):
                if b >= 2:
                    norm_output(b - 2)
                if b < DB:
                    take_keys(b, 0)
                if b == 0:
                    dve.wait_ge(bias_loaded, 16 * H)
                    link(nc.vector.tensor_copy(bias[:, :PAST].rearrange("q (r k) -> q k r", r=R),
                                               logit[:, :PAST].rearrange("q (k r) -> q k r", r=R)))
                    link(nc.vector.tensor_copy(bias[:, PAST:].rearrange("q (b t) -> q b t", b=DB),
                                               logit[:, PAST:PAST + DS].unsqueeze(1).to_broadcast([P, DB, DS])))
                if b >= 2:
                    take_output(b - 2)
                for c in range(4):
                    if b < DB and c < 3:
                        take_keys(b, c + 1)
                    if b and c == 0:
                        dve.wait_ge(e_ready, b)
                        link(nc.vector.reciprocal(st[:, (b - 1) % 2, 3:4], st[:, (b - 1) % 2, 2:3]))
                    if b:
                        take_probs(b - 1, c)
                if b:
                    take_probs(b - 1, 4)
                if b + 1 < DB:
                    if b:
                        dve.wait_ge(s_ready, b)
                    spread_q(b + 1)
                if b < DB:
                    dve.wait_ge(s_ready, b + 1)
                    nc.vector.tensor_tensor_reduce(logit[:, :], psS[:, :NK], bias[:, :], 1.0, NEG, ALU.add, ALU.max,
                                                   st[:, b % 2, 0:1]).then_inc(l_ready, 1)
                    dve.wait_ge(l_ready, b + 1)
                    nc.vector.tensor_scalar(st[:, b % 2, 1:2], st[:, b % 2, 0:1], -1.0, None, ALU.mult).then_inc(neg_ready, 1)
            norm_output(DB - 1)
            take_output(DB - 1)


def load_expert(sp, S, E, e, j):
    sp.dma_start(E["wg"][:, j, :, :], S["w_gate"][bass.ds(e, 1)].rearrange("o (k p) f -> p (o k) f", p=P)).then_inc(E["w_loaded"][j], 16)
    sp.dma_start(E["wu"][:, j, :, :], S["w_up"][bass.ds(e, 1)].rearrange("o (k p) f -> p (o k) f", p=P)).then_inc(E["w_loaded"][j], 16)
    sp.dma_start(E["wd"][:, j, :, :], S["w_down"][bass.ds(e, 1)].rearrange("o (k p) n -> p (o k) n", p=P)).then_inc(E["w_loaded"][j], 16)


def output_projection(nc, S, A, E):
    with ExitStack() as ctx:
        sb = lambda n, s, d=F32: ctx.enter_context(nc.sbuf_tensor("o_" + n, s, d))
        sem = stage_semaphores(nc, ctx, "o_")
        w = sb("w", [P, KD, D])
        x = sb("x", [P, 3, D])
        h = sb("h", [P, 2, D])
        ps = ctx.enter_context(nc.psum_tensor("o_ps", [P, 2, D], F32))
        w_loaded = [sem(f"w{q}_loaded") for q in range(KD // 2)]
        y_ready, h_ready = sem("y_ready"), sem("h_ready")
        x_loaded = [sem(f"x_loaded{j}") for j in range(3)]
        h_stored = [sem(f"h_stored{j}") for j in range(2)]
        block = ctx.enter_context(nc.Block())

        @block.sync
        def _(sp):
            for q in range(KD // 2):
                sp.dma_start(w[:, 2 * q:2 * q + 2, :], S["w_out"][2 * q * P:(2 * q + 2) * P, :].rearrange("(k p) n -> p k n", p=P)
                             ).then_inc(w_loaded[q], 16)
            for i in range(TILES):
                if i >= 3:
                    sp.wait_ge(h_ready, i - 2)
                sp.dma_start(x[:rows_of(i), i % 3, :], S["x_rows"](i)).then_inc(x_loaded[i % 3], 16)
                if i in range(2, 2 + RING):
                    load_expert(sp, S, E, i - 2, i - 2)

        @block.tensor
        def _(pe):
            for i in range(TILES):
                n = rows_of(i)
                if i >= 2:
                    pe.wait_ge(h_ready, i - 1)
                for half in range(2):
                    for k in range(KD):
                        if i == 0 and half == 0 and k % 2 == 0:
                            pe.wait_ge(w_loaded[k // 2], 16)
                        src = A["attT"][:, k, cols_of(i)] if k < PAIRS else A["retT"][:, k - PAIRS, cols_of(i)]
                        mm = nc.tensor.matmul(ps[:n, i % 2, half * 512:(half + 1) * 512], src, w[:, k, half * 512:(half + 1) * 512],
                                              start=(k == 0), stop=(k == KD - 1))
                mm.then_inc(y_ready, 1)

        @block.vector
        def _(dve):
            for i in range(TILES):
                n = rows_of(i)
                dve.wait_ge(y_ready, i + 1)
                dve.wait_ge(x_loaded[i % 3], 16 * (i // 3 + 1))
                if i >= 2:
                    dve.wait_ge(h_stored[i % 2], 16 * (i // 2))
                nc.vector.tensor_tensor(h[:n, i % 2, :], ps[:n, i % 2, :], x[:n, i % 3, :], ALU.add).then_inc(h_ready, 1)

        @block.gpsimd
        def _(pool):
            for i in range(TILES):
                pool.wait_ge(h_ready, i + 1)
                pool.dma_start(S["h"][cols_of(i), :], h[:rows_of(i), i % 2, :]).then_inc(h_stored[i % 2], 16)
            pool.wait_ge(h_stored[0], 16 * ((TILES + 1) // 2))
            pool.wait_ge(h_stored[1], 16 * (TILES // 2))


def route(nc, S, A, M):
    NR = NG + NE
    with ExitStack() as ctx:
        sb = lambda n, s, d=F32: ctx.enter_context(nc.sbuf_tensor("g_" + n, s, d))
        sem = stage_semaphores(nc, ctx, "g_")
        wr = sb("wr", [P, KD, NR])
        lg = sb("lg", [P, TILES, NR])
        a4 = sb("a4", [P, TILES, NG])
        g_hot = sb("g_hot", [P, TILES, NG])
        prod = sb("prod", [P, TILES, NE])
        el = sb("el", [P, TILES, EPG])
        a8 = sb("a8", [P, TILES, EPG])
        hot = sb("hot", [P, 2, TILES, EPG])
        s9 = sb("s9", [P, 12, TILES])
        pick = sb("pick", [P, 2, TILES, NE])
        both = sb("both", [P, TILES, NE], BF16)
        rank = sb("rank", [P, TILES + 1, NE])
        over = sb("over", [P, 4, NE])
        cmp_t = sb("cmp_t", [P, NE, MULTIPLES])
        ovx = sb("ovx", [P, OVER])
        zeros = sb("zeros", [P, -(-SLOTS * CAP // P)], U32)
        tok = sb("tok", [P, TILES], U32)
        ps = ctx.enter_context(nc.psum_tensor("g_ps", [P, TILES * NR], F32))
        psR = ctx.enter_context(nc.psum_tensor("g_psR", [P, (TILES + 1) * NE], F32))
        loaded, lg_ready, both_ready, rank_ready = sem("loaded"), sem("lg_ready"), sem("both_ready"), sem("rank_ready")
        dve_done, act_in, act_out, pos_ready = sem("dve_done"), sem("act_in"), sem("act_out"), sem("pos_ready")
        zeroed, tok_ready, cleared, read = sem("zeroed"), sem("tok_ready"), sem("cleared"), sem("read")
        listed = [sem(f"listed{j}") for j in range(6)]
        block = ctx.enter_context(nc.Block())

        @block.sync
        def _(sp):
            with nc.allow_non_contiguous_dma(reason="narrow router weights"):
                sp.dma_start(wr[:, :, :NG], S["w_group"].rearrange("(k p) n -> p k n", p=P)).then_inc(loaded, 16)
                sp.dma_start(wr[:, :, NG:], S["w_expert"].rearrange("(k p) n -> p k n", p=P)).then_inc(loaded, 16)
            sp.wait_ge(cleared, 16)
            for j in range(6):
                sp.wait_ge(listed[j], 16 * (2 * TILES // 6))
            with nc.allow_non_contiguous_dma(reason="one token id per partition"):
                sp.dma_start(M["token"][:, :], S["token_list"][:SLOTS * CAP, :].rearrange("(s c) o -> c (s o)", c=CAP)
                             ).then_inc(read, 16)
            sp.wait_ge(read, 16)

        @block.tensor
        def _(pe):
            pe.wait_ge(loaded, 32)
            for i in range(TILES):
                n = rows_of(i)
                for k in range(KD):
                    mm = nc.tensor.matmul(ps[:n, i * NR:(i + 1) * NR], A["uT"][:, k, cols_of(i)], wr[:, k, :],
                                          start=(k == 0), stop=(k == KD - 1), skip_group_check=True)
            mm.then_inc(lg_ready, 1)
            pe.wait_ge(both_ready, 1)
            for i in range(TILES + 1):
                n = rows_of(i) if i < TILES else P
                out = psR[:n, i * NE:(i + 1) * NE]
                last = i == TILES
                for j in range(i):
                    m = rows_of(j)
                    mm = nc.tensor.matmul(out, A["ones_b"][:m, :n], both[:m, j, :], start=(j == 0), stop=(last and j == i - 1),
                                          skip_group_check=True)
                if not last:
                    mm = nc.tensor.matmul(out, A["above_b"][:n, :n], both[:n, i, :], start=(i == 0), stop=True,
                                          skip_group_check=True)
            mm.then_inc(rank_ready, 1)

        @block.scalar
        def _(act):
            act.wait_ge(act_in, 1)
            nc.scalar.activation(a4[:, :, :], a4[:, :, :], ACT.Exp).then_inc(act_out, 1)
            act.wait_ge(act_in, 2)
            nc.scalar.activation(s9[:, 4, :], s9[:, 3, :], ACT.Exp).then_inc(act_out, 1)

        @block.gpsimd
        def _(pool):
            nc.gpsimd.memset(zeros[:, :], 0).then_inc(zeroed, 1)
            nc.gpsimd.iota(tok[:, :], [[P, TILES]], base=0, channel_multiplier=1).then_inc(tok_ready, 1)
            pool.wait_ge(zeroed, 1)
            pool.dma_start(S["token_list"].rearrange("(p n) o -> p (n o)", p=P), zeros[:, :]).then_inc(cleared, 16)
            pool.wait_ge(cleared, 16)
            pool.wait_ge(tok_ready, 1)
            for c in range(2):
                pool.wait_ge(pos_ready, c + 1)
                for i in range(TILES):
                    n, q = rows_of(i), c * TILES + i
                    if q >= 6:
                        pool.wait_ge(listed[q % 6], 16 * (q // 6))
                    pool.indirect_dma_start(S["token_list"], bass.IndirectOffsetOnAxis(ap=M["pos"][:n, c, i:i + 1], axis=0),
                                            tok[:n, i:i + 1], None).then_inc(listed[q % 6], 16)
            for j in range(6):
                pool.wait_ge(listed[j], 16 * (2 * TILES // 6))

        @block.vector
        def _(dve):
            link = Chain(dve, dve_done)
            V = nc.vector
            link(V.memset(lg[:, :, :], 0.0))
            link(V.memset(rank[:, :, :], 0.0))
            dve.wait_ge(lg_ready, 1)
            lp = ps[:, :].rearrange("p (i n) -> p i n", i=TILES)
            link(V.tensor_copy(lg[:, :NT, :], lp[:, :NT, :]))
            link(V.tensor_copy(lg[:NS, NT, :], lp[:NS, NT, :]))
            wide = lambda a, n: a.unsqueeze(2).to_broadcast([P, TILES, n])
            tiles = lambda a, n: a.unsqueeze(1).to_broadcast([P, TILES, n])

            def first_of_max(hot_out, values, peak, scratch, n):
                link(V.tensor_reduce(peak, values, AX_X, ALU.max))
                link(V.tensor_tensor(scratch, values, wide(peak, n), ALU.is_ge))
                link(V.tensor_tensor(scratch, scratch, tiles(A["countdown"][:, EPG - n:], n), ALU.mult))
                link(V.tensor_reduce(s9[:, 11, :], scratch, AX_X, ALU.max))
                link(V.tensor_tensor(hot_out, tiles(A["countdown"][:, EPG - n:], n), wide(s9[:, 11, :], n), ALU.is_equal))

            first_of_max(g_hot[:, :, :], lg[:, :, :NG], s9[:, 0, :], a4[:, :, :], NG)
            V.tensor_tensor(a4[:, :, :], lg[:, :, :NG], wide(s9[:, 0, :], NG), ALU.subtract).then_inc(act_in, 1)
            g3 = g_hot[:, :, :].unsqueeze(3).to_broadcast([P, TILES, NG, EPG])
            link(V.tensor_tensor(prod[:, :, :].rearrange("p i (g e) -> p i g e", g=NG),
                                 lg[:, :, NG:].rearrange("p i (g e) -> p i g e", g=NG), g3, ALU.mult))
            link(V.tensor_reduce(el[:, :, :], prod[:, :, :].rearrange("p i (g e) -> p i e g", g=NG), AX_X, ALU.add))
            first_of_max(hot[:, 0, :, :], el[:, :, :], s9[:, 1, :], a8[:, :, :], EPG)
            link(V.tensor_scalar(a8[:, :, :], hot[:, 0, :, :], NEG, None, ALU.mult))
            link(V.tensor_tensor(el[:, :, :], el[:, :, :], a8[:, :, :], ALU.add))
            first_of_max(hot[:, 1, :, :], el[:, :, :], s9[:, 2, :], a8[:, :, :], EPG)
            V.tensor_tensor(s9[:, 3, :], s9[:, 2, :], s9[:, 1, :], ALU.subtract).then_inc(act_in, 1)
            for c in range(2):
                link(V.tensor_tensor(pick[:, c, :, :].rearrange("p i (g e) -> p i g e", g=NG), g3,
                                     hot[:, c, :, :].unsqueeze(2).to_broadcast([P, TILES, NG, EPG]), ALU.mult))
            V.tensor_tensor(both[:, :, :], pick[:, 0, :, :], pick[:, 1, :, :], ALU.add).then_inc(both_ready, 1)
            dve.wait_ge(act_out, 2)
            link(V.tensor_reduce(s9[:, 5, :], a4[:, :, :], AX_X, ALU.add))
            link(V.tensor_scalar(s9[:, 6, :], s9[:, 4, :], 1.0, None, ALU.add))
            link(V.tensor_tensor(s9[:, 5, :], s9[:, 5, :], s9[:, 6, :], ALU.mult))
            link(V.reciprocal(M["weight"][:, 0, :], s9[:, 5, :]))
            link(V.tensor_tensor(M["weight"][:, 1, :], M["weight"][:, 0, :], s9[:, 4, :], ALU.mult))
            dve.wait_ge(rank_ready, 1)
            rp = psR[:, :].rearrange("p (i e) -> p i e", e=NE)
            link(V.tensor_copy(rank[:, :NT, :], rp[:, :NT, :]))
            link(V.tensor_copy(rank[:NS, NT, :], rp[:NS, NT, :]))
            link(V.tensor_copy(rank[:, TILES, :], rp[:, TILES, :]))
            link(V.tensor_tensor(cmp_t[:, :, :], rank[:, TILES, :].unsqueeze(2).to_broadcast([P, NE, MULTIPLES]),
                                 A["cap_multiples"][:, :].unsqueeze(1).to_broadcast([P, NE, MULTIPLES]), ALU.is_gt))
            link(V.tensor_reduce(over[:, 0, :], cmp_t[:, :, :], AX_X, ALU.add))
            link(V.tensor_tensor_scan(over[:, 1, :], over[:, 0, :], over[:, 0, :], 0.0, ALU.add, ALU.max))
            link(V.tensor_tensor(over[:, 2, :], over[:, 1, :], over[:, 0, :], ALU.subtract))
            link(V.tensor_scalar(over[:, 3, :], over[:, 2, :], float(NE - 1), None, ALU.add))
            link(V.tensor_tensor(over[:, 3, :], over[:, 3, :], A["expert_id"][:, :], ALU.subtract))
            for c in range(2):
                def chosen(out, table):
                    link(V.tensor_tensor(prod[:, :, :], pick[:, c, :, :], table, ALU.mult))
                    link(V.tensor_reduce(out, prod[:, :, :], AX_X, ALU.add))
                chosen(s9[:, 7, :], rank[:, :TILES, :])
                chosen(s9[:, 8, :], A["expert_id"][:, :].unsqueeze(1).to_broadcast([P, TILES, NE]))
                chosen(s9[:, 9, :], over[:, 3, :].unsqueeze(1).to_broadcast([P, TILES, NE]))
                link(V.tensor_scalar(s9[:, 10, :], s9[:, 7, :], float(CAP), None, ALU.is_ge))
                link(V.tensor_tensor(s9[:, 9, :], s9[:, 9, :], s9[:, 10, :], ALU.mult))
                link(V.tensor_tensor(s9[:, 8, :], s9[:, 8, :], s9[:, 9, :], ALU.add))
                link(V.tensor_scalar(s9[:, 8, :], s9[:, 8, :], float(CAP), None, ALU.mult))
                link(V.tensor_tensor(s9[:, 8, :], s9[:, 8, :], s9[:, 7, :], ALU.add))
                V.tensor_copy(M["pos"][:, c, :], s9[:, 8, :]).then_inc(pos_ready, 1)
                dve.wait_ge(pos_ready, c + 1)
            link(V.tensor_copy(M["over_count"][:, :], over[:, 1, NE - 1:NE]))
            for v in range(OVER):
                link(V.tensor_scalar(prod[:, 0, :], over[:, 1, :], float(v), None, ALU.is_le, ALU.add, accum_out=ovx[:, v:v + 1]))
            link(V.tensor_scalar(ovx[:, :], ovx[:, :], float(NE - 1), None, ALU.min))
            V.tensor_copy(M["over_expert"][:, :], ovx[:, :])


def experts(nc, S, A, M, E):
    K2 = DE // P
    with ExitStack() as ctx:
        sb = lambda n, s, d=F32: ctx.enter_context(nc.sbuf_tensor("e_" + n, s, d))
        sem = stage_semaphores(nc, ctx, "e_")
        wg, wu, wd, w_loaded = E["wg"], E["wu"], E["wd"], E["w_loaded"]
        xg = sb("xg", [CAP, RING, D])
        ids = sb("ids", [CAP, RING], U32)
        xT = sb("xT", [P, 2, KD, CAP])
        gate = sb("gate", [P, 2, K2, CAP])
        hT = sb("hT", [P, 2, K2, CAP])
        y = sb("y", [CAP, 2, D])
        psX = ctx.enter_context(nc.psum_tensor("e_psX", [P, 2, 512], F32))
        psG = ctx.enter_context(nc.psum_tensor("e_psG", [P, 2, 512], F32))
        psY = ctx.enter_context(nc.psum_tensor("e_psY", [CAP, 2, D], F32))
        x_loaded = [sem(f"x_loaded{j}") for j in range(RING)]
        gathers = sem("gathers")
        ids_ready, x_half, x_turned, xT_ready = sem("ids_ready"), sem("x_half"), sem("x_turned"), sem("xT_ready")
        g_ready, gate_ready, h_ready, y_ready, y_taken = sem("g_ready"), sem("gate_ready"), sem("h_ready"), sem("y_ready"), sem("y_taken")
        y_stored = [sem(f"y_stored{j}") for j in range(2)]
        block = ctx.enter_context(nc.Block())

        def rounds(engine, body):
            for j in range(RING):
                body(0, j)
            with engine.Fori(1, NE // RING - 1) as it:
                for j in range(RING):
                    body(it, j)
            for j in range(RING):
                body(NE // RING - 1, j)

        @block.sync
        def _(sp):
            def body(it, j):
                if isinstance(it, int) and it == 0:
                    return
                e = it * RING + j
                sp.wait_ge(y_ready, e - (RING - 1))
                load_expert(sp, S, E, e, j)
            rounds(sp, body)
            for i in range(TILES):
                sp.dma_start(M["h"](i)[:rows_of(i), :], S["h"][cols_of(i), :]).then_inc(M["h_loaded"], 16)
            sp.wait_ge(M["h_loaded"], 16 * TILES)

        @block.gpsimd
        def _(pool):
            def body(it, j):
                e = it * RING + j
                if not (isinstance(it, int) and it == 0):
                    pool.wait_ge(x_turned, e - (RING - 1))
                    pool.wait_ge(x_loaded[j], it * 16)
                nc.gpsimd.tensor_copy(ids[:, j:j + 1], M["token"][:, bass.ds(e, 1)]).then_inc(ids_ready, 1)
                pool.wait_ge(ids_ready, e + 1)
                pool.sem_inc(gathers, 1)
                pool.indirect_dma_start(xg[:, j, :], None, S["xn"], bass.IndirectOffsetOnAxis(ap=ids[:, j:j + 1], axis=0)
                                        ).then_inc(x_loaded[j], 16)
            rounds(pool, body)

        @block.tensor
        def _(pe):
            def turn(it, j):
                e = it * RING + j
                slot = j % RING
                pe.wait_ge(x_loaded[slot], (it + j // RING) * 16 + 16)
                for half in range(2):
                    if not (isinstance(it, int) and e == 0):
                        pe.wait_ge(xT_ready, e * 2 + half - 1)
                    for k in range(4):
                        mm = nc.tensor.transpose(psX[:, half, k * CAP:(k + 1) * CAP],
                                                 xg[:, slot, (4 * half + k) * P:(4 * half + k + 1) * P], A["identity"][:CAP, :CAP])
                    mm.then_inc(x_turned if half else x_half, 1)

            def body(it, j):
                e = it * RING + j
                first = isinstance(it, int) and it == 0
                b = j % 2
                pe.wait_ge(w_loaded[j], it * 48 + 48)
                pe.wait_ge(xT_ready, e * 2 + 2)
                if not (first and j < 2):
                    pe.wait_ge(h_ready, e - 1)
                for m in range(2 * K2):
                    w = wg if m < K2 else wu
                    f = m % K2
                    for k in range(KD):
                        mm = nc.tensor.matmul(psG[:, b, m * CAP:(m + 1) * CAP], w[:, j, k, f * P:(f + 1) * P], xT[:, b, k, :],
                                              start=(k == 0), stop=(k == KD - 1), skip_group_check=True)
                mm.then_inc(g_ready, 1)
                if not (isinstance(it, int) and e == NE - 1):
                    turn(it, j + 1)
                pe.wait_ge(h_ready, e + 1)
                if not (first and j < 2):
                    pe.wait_ge(y_taken, e - 1)
                for c in range(2):
                    for f in range(K2):
                        mm = nc.tensor.matmul(psY[:, b, c * 512:(c + 1) * 512], hT[:, b, f, :], wd[:, j, f, c * 512:(c + 1) * 512],
                                              start=(f == 0), stop=(f == K2 - 1))
                mm.then_inc(y_ready, 1)
            turn(0, 0)
            rounds(pe, body)

        @block.scalar
        def _(act):
            def body(it, j):
                e = it * RING + j
                first = isinstance(it, int) and it == 0
                b = j % 2
                act.wait_ge(g_ready, e + 1)
                if not (first and j < 2):
                    act.wait_ge(h_ready, e - 1)
                nc.scalar.activation(gate[:, b, :, :], psG[:, b, :K2 * CAP].rearrange("p (f c) -> p f c", f=K2), ACT.Silu
                                     ).then_inc(gate_ready, 1)
                act.wait_ge(y_ready, e + 1)
                if not (first and j < 2):
                    act.wait_ge(y_stored[b], (it * (RING // 2) + j // 2) * 16)
                nc.scalar.activation(y[:, b, :], psY[:, b, :], ACT.Copy).then_inc(y_taken, 1)
                act.wait_ge(y_taken, e + 1)
                act.dma_start(S["y"][bass.ds(e * CAP, CAP), :], y[:, b, :]).then_inc(y_stored[b], 16)
            rounds(act, body)
            for b in range(2):
                act.wait_ge(y_stored[b], 16 * NE // 2)

        @block.vector
        def _(dve):
            def take_tokens(it, j):
                e = it * RING + j
                b = j % 2
                if not (isinstance(it, int) and e < 2):
                    dve.wait_ge(g_ready, e - 1)
                for half in range(2):
                    dve.wait_ge(x_half if half == 0 else x_turned, e + 1)
                    nc.vector.tensor_tensor(xT[:, b, 4 * half:4 * half + 4, :],
                                            psX[:, half, :4 * CAP].rearrange("p (k c) -> p k c", k=4),
                                            A["ln2_gT"][:, 4 * half:4 * half + 4].unsqueeze(2).to_broadcast([P, 4, CAP]),
                                            ALU.mult).then_inc(xT_ready, 1)

            def body(it, j):
                e = it * RING + j
                b = j % 2
                dve.wait_ge(gate_ready, e + 1)
                if not (isinstance(it, int) and it == 0 and j < 2):
                    dve.wait_ge(y_ready, e - 1)
                nc.vector.tensor_tensor(hT[:, b, :, :], gate[:, b, :, :],
                                        psG[:, b, K2 * CAP:2 * K2 * CAP].rearrange("p (f c) -> p f c", f=K2),
                                        ALU.mult).then_inc(h_ready, 1)
                if not (isinstance(it, int) and e == NE - 1):
                    take_tokens(it, j + 1)
            take_tokens(0, 0)
            rounds(dve, body)


def overflow_experts(nc, S, A, M):
    K2 = DE // P
    with ExitStack() as ctx:
        sb = lambda n, s, d=F32: ctx.enter_context(nc.sbuf_tensor("v_" + n, s, d))
        sem = stage_semaphores(nc, ctx, "v_")
        wg = sb("wg", [P, KD, DE])
        wu = sb("wu", [P, KD, DE])
        wd = sb("wd", [P, K2, D])
        xg = sb("xg", [CAP, D])
        ids = sb("ids", [CAP, 1], U32)
        xT = sb("xT", [P, KD, CAP])
        gate = sb("gate", [P, K2, CAP])
        hT = sb("hT", [P, K2, CAP])
        y = sb("y", [CAP, D])
        psX = ctx.enter_context(nc.psum_tensor("v_psX", [P, 2, 512], F32))
        psG = ctx.enter_context(nc.psum_tensor("v_psG", [P, 512], F32))
        psY = ctx.enter_context(nc.psum_tensor("v_psY", [CAP, D], F32))
        gathers = sem("gathers")
        w_loaded, x_loaded, ids_ready, x_turned, xT_ready = sem("w_loaded"), sem("x_loaded"), sem("ids_ready"), sem("x_turned"), sem("xT_ready")
        g_ready, gate_ready, h_ready, y_ready, y_taken, y_stored = sem("g_ready"), sem("gate_ready"), sem("h_ready"), sem("y_ready"), sem("y_taken"), sem("y_stored")
        block = ctx.enter_context(nc.Block())

        def slots(engine):
            return engine.Fori(0, engine.value_load(M["over_count"][0:1, 0:1], min_val=0, max_val=OVER))

        @block.sync
        def _(sp):
            with slots(sp) as s:
                e = sp.value_load(M["over_expert"][0:1, bass.ds(s, 1)], min_val=0, max_val=NE - 1)
                sp.wait_ge(y_ready, s + 1)
                sp.dma_start(wg[:, :, :], S["w_gate"][bass.ds(e, 1)].rearrange("o (k p) f -> p (o k) f", p=P)).then_inc(w_loaded, 16)
                sp.dma_start(wu[:, :, :], S["w_up"][bass.ds(e, 1)].rearrange("o (k p) f -> p (o k) f", p=P)).then_inc(w_loaded, 16)
                sp.dma_start(wd[:, :, :], S["w_down"][bass.ds(e, 1)].rearrange("o (k p) n -> p (o k) n", p=P)).then_inc(w_loaded, 16)

        @block.gpsimd
        def _(pool):
            with slots(pool) as s:
                pool.wait_ge(x_turned, s + 1)
                nc.gpsimd.tensor_copy(ids[:, :], M["token"][:, bass.ds(NE + s, 1)]).then_inc(ids_ready, 1)
                pool.wait_ge(ids_ready, s + 1)
                pool.sem_inc(gathers, 1)
                pool.indirect_dma_start(xg[:, :], None, S["xn"], bass.IndirectOffsetOnAxis(ap=ids[:, :], axis=0)
                                        ).then_inc(x_loaded, 16)

        @block.tensor
        def _(pe):
            pe.sem_inc(x_turned, 1)
            pe.sem_inc(y_ready, 1)
            with slots(pe) as s:
                pe.wait_ge(x_loaded, s * 16 + 16)
                for k in range(KD):
                    mm = nc.tensor.transpose(psX[:, k // 4, k % 4 * CAP:(k % 4 + 1) * CAP], xg[:, k * P:(k + 1) * P],
                                             A["identity"][:CAP, :CAP])
                mm.then_inc(x_turned, 1)
                pe.wait_ge(w_loaded, s * 48 + 48)
                pe.wait_ge(xT_ready, s * 2 + 2)
                for m in range(2 * K2):
                    w, f = wg if m < K2 else wu, m % K2
                    for k in range(KD):
                        mm = nc.tensor.matmul(psG[:, m * CAP:(m + 1) * CAP], w[:, k, f * P:(f + 1) * P], xT[:, k, :],
                                              start=(k == 0), stop=(k == KD - 1), skip_group_check=True)
                mm.then_inc(g_ready, 1)
                pe.wait_ge(h_ready, s + 1)
                pe.wait_ge(y_taken, s + 1)
                for c in range(2):
                    for f in range(K2):
                        mm = nc.tensor.matmul(psY[:, c * 512:(c + 1) * 512], hT[:, f, :], wd[:, f, c * 512:(c + 1) * 512],
                                              start=(f == 0), stop=(f == K2 - 1))
                mm.then_inc(y_ready, 1)

        @block.scalar
        def _(act):
            act.sem_inc(y_taken, 1)
            with slots(act) as s:
                act.wait_ge(g_ready, s + 1)
                nc.scalar.activation(gate[:, :, :], psG[:, :K2 * CAP].rearrange("p (f c) -> p f c", f=K2), ACT.Silu).then_inc(gate_ready, 1)
                act.wait_ge(y_ready, s + 2)
                nc.scalar.activation(y[:, :], psY[:, :], ACT.Copy).then_inc(y_taken, 1)
                act.wait_ge(y_taken, s + 2)
                act.dma_start(S["y"][bass.ds((NE + s) * CAP, CAP), :], y[:, :]).then_inc(y_stored, 16)
                act.wait_ge(y_stored, s * 16 + 16)

        @block.vector
        def _(dve):
            with slots(dve) as s:
                dve.wait_ge(x_turned, s + 2)
                for half in range(2):
                    nc.vector.tensor_tensor(xT[:, 4 * half:4 * half + 4, :], psX[:, half, :4 * CAP].rearrange("p (k c) -> p k c", k=4),
                                            A["ln2_gT"][:, 4 * half:4 * half + 4].unsqueeze(2).to_broadcast([P, 4, CAP]),
                                            ALU.mult).then_inc(xT_ready, 1)
                dve.wait_ge(gate_ready, s + 1)
                nc.vector.tensor_tensor(hT[:, :, :], gate[:, :, :], psG[:, K2 * CAP:2 * K2 * CAP].rearrange("p (f c) -> p f c", f=K2),
                                        ALU.mult).then_inc(h_ready, 1)


def combine(nc, S, M):
    with ExitStack() as ctx:
        sb = lambda n, s, d=F32: ctx.enter_context(nc.sbuf_tensor("c_" + n, s, d))
        sem = stage_semaphores(nc, ctx, "c_")
        ya = sb("ya", [P, 4, D])
        yb = sb("yb", [P, 4, D])
        y_loaded = [[sem(f"y{c}_loaded{j}") for j in range(4)] for c in range(2)]
        half_done, ready, stored = sem("half_done"), sem("ready"), sem("stored")
        block = ctx.enter_context(nc.Block())

        @block.sync
        def _(sp):
            for i in range(TILES):
                sp.wait_ge(ready, i + 1)
                sp.dma_start(S["out_rows"](i), M["h"](i)[:rows_of(i), :]).then_inc(stored, 16)
            sp.wait_ge(stored, 16 * TILES)

        @block.gpsimd
        def _(pool):
            for i in range(TILES):
                n = rows_of(i)
                if i >= 4:
                    pool.wait_ge(ready, i - 3)
                for c, y in enumerate((ya, yb)):
                    pool.indirect_dma_start(y[:n, i % 4, :], None, S["y"], bass.IndirectOffsetOnAxis(ap=M["pos"][:n, c, i:i + 1], axis=0)
                                            ).then_inc(y_loaded[c][i % 4], 16)

        @block.vector
        def _(dve):
            for i in range(TILES):
                n = rows_of(i)
                h = M["h"](i)[:n, :]
                dve.wait_ge(y_loaded[0][i % 4], 16 * (i // 4 + 1))
                nc.vector.scalar_tensor_tensor(h, ya[:n, i % 4, :], M["weight"][:n, 0, i:i + 1], h,
                                               ALU.mult, ALU.add).then_inc(half_done, 1)
                dve.wait_ge(half_done, i + 1)
                dve.wait_ge(y_loaded[1][i % 4], 16 * (i // 4 + 1))
                nc.vector.scalar_tensor_tensor(h, yb[:n, i % 4, :], M["weight"][:n, 1, i:i + 1], h,
                                               ALU.mult, ALU.add).then_inc(ready, 1)


def load_constants(nc, name, pairs, casts):
    with ExitStack() as ctx:
        sem = stage_semaphores(nc, ctx, name)
        loaded, loaded_by_act, done = sem("loaded"), sem("loaded_by_act"), sem("done")
        block = ctx.enter_context(nc.Block())
        by_sp, by_act = pairs[0::2], pairs[1::2]

        @block.sync
        def _(sp):
            with nc.allow_non_contiguous_dma(reason="small tables"):
                for dst, src in by_sp:
                    sp.dma_start(dst, src).then_inc(loaded, 16)
            if by_sp:
                sp.wait_ge(loaded, 16 * len(by_sp))

        @block.scalar
        def _(act):
            with nc.allow_non_contiguous_dma(reason="small tables"):
                for dst, src in by_act:
                    act.dma_start(dst, src).then_inc(loaded_by_act, 16)
            if by_act:
                act.wait_ge(loaded_by_act, 16 * len(by_act))

        @block.vector
        def _(dve):
            if by_sp:
                dve.wait_ge(loaded, 16 * len(by_sp))
            if by_act:
                dve.wait_ge(loaded_by_act, 16 * len(by_act))
            for dst, src, scale, offset in casts:
                nc.vector.tensor_scalar(dst, src, scale, offset, ALU.mult, ALU.add).then_inc(done, 1)
            if casts:
                dve.wait_ge(done, len(casts))


INPUTS = ["x_prompt", "x_sample", "cache_k", "cache_v", "cache_kidx", "state_ret", "page_table", "rel_bias", "ln1_g",
          "w_in", "q_norm_g", "k_norm_g", "ret_gn_g", "ret_gn_b", "w_out", "ln2_g", "w_group", "w_expert", "w_gate",
          "w_up", "w_down"]
OUTPUTS = [(1, SEQ, D), (DB, DS, D), (1, 1, SEQ, H, HD), (1, 1, SEQ, H, HD), (1, 1, SEQ, 64), (1, 1, H, HD, HD),
           (1, DB, DS, H, HD), (1, DB, DS, H, HD), (1, DB, DS, 64), (1, DB, H, HD, HD)]


def shape_constants():
    f = np.float32
    pos = np.concatenate([np.arange(SEQ), np.tile(PAST + np.arange(DS), DB)]).astype(f)
    inv = (10000.0 ** (-np.arange(HD // 2) / (HD // 2))).astype(f)
    ang = (pos[:, None] * inv[None]).astype(f)
    gamma = 1 - 2.0 ** (-5 - np.arange(H))
    j = np.stack([np.arange(P), np.arange(P) % DS]) + 1.0
    step = np.arange(P)
    own = lambda n: (np.arange(NS)[:, None] // DS == np.arange(n)[None] // DS)
    prompt_mask = step[:, None] <= step[None]
    sample_mask = np.zeros((P, P))
    sample_mask[:NS, :NS] = own(NS) & (step[:NS, None] <= step[None, :NS])
    n = np.maximum(PAST + DS - 1 - np.arange(PAST + DS + P), 0)
    nf = np.maximum(n, 16).astype(f)
    large = 16 + (np.log(nf / f(16)) / f(np.log(64.0)) * f(16)).astype(np.int32)
    bucket = np.where(n < 16, n, np.minimum(large, 31))
    pair_gamma = gamma.reshape(PAIRS, 2)[:, step // HD].T
    rows = np.arange(NS)
    return {
        "identity": np.eye(P), "cos": np.cos(ang), "sin": np.sin(ang),
        "decay_q": gamma[None, None] ** j[:, :, None],
        "decay_k": gamma[None, None] ** -j[:, :, None] * HD ** -0.5,
        "ret_mask": np.stack([prompt_mask, sample_mask]),
        "gamma_chunk": np.stack([pair_gamma ** P, pair_gamma ** DS], 1),
        "own_seq": rows[:, None] // DS == np.arange(DB)[None],
        "sum_heads": (step[:, None] // 32 == np.arange(32)[None] // DS) & (step[:, None] % DS == np.arange(32)[None] % DS),
        "causal": np.where(step[None] <= step[:, None], 0, NEG),
        "causal_s": np.where(own(NS) & (rows[None] <= rows[:, None]), 0, NEG),
        "own_rows": (rows[:, None, None] // DS == np.arange(DB)[None, :, None]) 
                    & (step[None, None] % 32 < 2 * DS) & (rows[:, None, None] % DS == step[None, None] % DS),
        "onehot": np.arange(32)[:, None] == bucket[None],
        "above": step[:, None] < step[None],
        "countdown": np.arange(EPG, 0, -1)[None], "cap_multiples": (CAP * np.arange(1, MULTIPLES + 1))[None],
        "expert_id": np.arange(NE)[None], "row_in_page": (step % 8)[:, None],
        "quarter_in_page": 4 * (step % 8)[:, None] + np.arange(4)[None],
    }


def build(nc, a, outs, c):
    dram = lambda n, s, d=F32: nc.dram_tensor(n, s, d, kind="Internal").ap()
    xp, xs = a["x_prompt"][0], a["x_sample"].rearrange("b t d -> (b t) d")
    row = lambda p, s: (lambda i: p[cols_of(i), :] if i < NT else s)
    S = {
        "w_in": a["w_in"][0], "w_out": a["w_out"][0], "ret_gn_g": a["ret_gn_g"], "ret_gn_b": a["ret_gn_b"],
        "state_ret": a["state_ret"][0], "rel_bias": a["rel_bias"], "w_group": a["w_group"][0], "w_expert": a["w_expert"][0],
        "w_gate": a["w_gate"][0], "w_up": a["w_up"][0], "w_down": a["w_down"][0],
        "cache_k": a["cache_k"][0].rearrange("n (g r) h e -> (n g) (r h e)", r=4),
        "cache_v": a["cache_v"][0].rearrange("n (g r) h e -> (n g) (r h e)", r=4),
        "cache_kidx": a["cache_kidx"][0].rearrange("n (g r) e -> (n g) (r e)", r=16),
        "ret_prompt": outs[5][0, 0], "ret_sample": outs[9][0], "c_onehot": c["onehot"],
        "x_rows": row(xp, xs), "out_rows": row(outs[0][0], outs[1].rearrange("b t d -> (b t) d")),
        "h": dram("h_rows", (TOK, D)), "xn": dram("xn_rows", (TOK, D)), "y": dram("y_rows", (SLOTS * CAP, D)),
        "token_list": dram("token_list", (-(-SLOTS * CAP // P) * P, 1), U32),
        "skew": dram("skew", (H, P, SEQ + P)), "skew_s": dram("skew_s", (NS, PAST + 2 * DS)),
    }
    flat = lambda k: row(outs[k][0, 0].rearrange("s h e -> s (h e)"), outs[k + 4][0].rearrange("b t h e -> (b t) (h e)"))
    k_rows, v_rows = flat(2), flat(3)
    i_rows = row(outs[4][0, 0], outs[8][0].rearrange("b t e -> (b t) e"))
    with ExitStack() as top:
        def sb(stack, n, s, d=F32):
            return stack.enter_context(nc.sbuf_tensor(n, s, d))
        A, X, T, M = {}, {}, {}, {}
        for n, s, d in (("identity", [P, P], F32), ("identity_b", [P, P], BF16), ("causal", [P, P], F32),
                        ("causal_b", [P, P], BF16), ("ones_b", [P, P], BF16), ("above_b", [P, P], BF16),
                        ("own_rows", [NS, DB, P], BF16), ("causal_s", [NS, NS], F32), ("own_seq", [NS, DB], F32),
                        ("sum_heads", [P, 32], F32), ("gamma_chunk", [P, 2, PAIRS], F32), ("row_id", [P, DB], U32),
                        ("quarter_id", [P, 4, DB], U32),
                        ("countdown", [P, EPG], F32), ("cap_multiples", [P, MULTIPLES], F32), ("expert_id", [P, NE], F32),
                        ("ln2_gT", [P, KD], F32), ("mixT", [P, KD, TOK], F32)):
            A[n] = sb(top, "k_" + n, s, d)
        A["attT"], A["retT"] = A["mixT"][:, :PAIRS, :], A["mixT"][:, PAIRS:, :]
        M["pos"] = sb(top, "m_pos", [P, 2, TILES], U32)
        M["weight"] = sb(top, "m_weight", [P, 2, TILES])
        M["token"] = sb(top, "m_token", [CAP, SLOTS], U32)
        M["over_count"] = sb(top, "m_over_count", [P, 1], I32)
        M["over_expert"] = sb(top, "m_over_expert", [P, OVER], I32)

        bc = lambda ap, n: ap.to_broadcast([P, n])
        A["mask_s"] = X["mask_s"] = sb(top, "mask_s", [NS, NK], BF16)
        A["qaT_s"], A["kaT_s"] = sb(top, "qaT_s", [P, PAIRS, NS]), sb(top, "kaT_s", [P, PAIRS, NS])
        A["va_s"] = sb(top, "va_s", [NS, W])

        with ExitStack() as early:
            buf = [sb(early, f"buf{j}", [P, TILES, W]) for j in range(2)]
            flat_buf = lambda t: t[:, :, :].rearrange("p i w -> p (i w)")[:, :PAIRS * TOK].rearrange("p (a t) -> p a t", a=PAIRS)
            A["kp"], A["vr"] = buf
            A["qpT"], A["kpT"] = A["attT"], A["retT"]
            A["qaT"], A["kaT"], A["va"] = A["attT"], flat_buf(buf[0]), buf[1]
            gq, gk = sb(early, "gq", [P, HD]), sb(early, "gk", [P, HD])
            pre = stage_semaphores(nc, early, "early_")
            w_preloaded = pre("w_preloaded")
            first = TOPK // P
            at = {}
            for i in range(first, NT):
                at[i] = sum((q + 1) * P for q in range(first, i))
            total = at[NT - 1] + NT * P
            sc = sb(early, "sc", [P, total])
            X["sc"] = lambda i: sc[:, at[i]:at[i] + (i + 1) * P]
            X["sc_s"] = sb(early, "sc_s", [NS, NK])
            X["lo"], X["hi"] = sb(early, "lo", [P, TILES]), sb(early, "hi", [P, TILES])
            w_first = sc[:, :KD * W].rearrange("p (k n) -> p k n", k=KD)
            with ExitStack() as st:
                A["uT"] = sb(st, "uT", [P, KD, TOK])
                with ExitStack() as rt:
                    A["sg"] = sb(rt, "sg", [P, TILES, W])
                    A["ret_mask"] = sb(rt, "ret_mask", [P, 2, P])
                    with ExitStack() as tb:
                        cos, sin = sb(tb, "cos", [P, TILES, HD // 2]), sb(tb, "sin", [P, TILES, HD // 2])
                        dq, dk = sb(tb, "dq", [P, 2, H]), sb(tb, "dk", [P, 2, H])
                        weights = lambda col, n: (w_first[:, :, :n], S["w_in"][:, col:col + n].rearrange("(k p) n -> p k n", p=P), w_preloaded)
                        load_constants(nc, "l0_", [(A["identity"][:, :], c["identity"])], [])
                        with ExitStack() as nt:
                            above, own = sb(nt, "above", [P, P]), sb(nt, "own", [NS, DB, P])
                            table, off = sb(nt, "table", [P, DB], I32), sb(nt, "off", [P, 1])
                            off_quarter = sb(nt, "off_quarter", [P, 4])
                            pages = a["page_table"].rearrange("b g -> g b")
                            tables = [(dst[:, :NT, :], c[n][:SEQ].rearrange("(i p) r -> p i r", p=P)) for dst, n in ((cos, "cos"), (sin, "sin"))]
                            tables += [(dst[:NS, NT, :], c[n][SEQ:]) for dst, n in ((cos, "cos"), (sin, "sin"))]
                            tables += [(dst[:, :, :], c[n].rearrange("s p h -> p s h")) for dst, n in ((dq, "decay_q"), (dk, "decay_k"))]
                            tables += [(A["ret_mask"][:, :, :], c["ret_mask"].rearrange("s p q -> p s q"))]
                            tables += [(gq[:, :], bc(a["q_norm_g"], HD)), (gk[:, :], bc(a["k_norm_g"], HD))]
                            tables += [(A[n][:, :], c[n]) for n in ("causal", "causal_s", "own_seq", "sum_heads")]
                            tables += [(A["gamma_chunk"][:, :, :], c["gamma_chunk"]), (above[:, :], c["above"]), (own[:, :, :], c["own_rows"]),
                                       (off[:, :], c["row_in_page"]), (off_quarter[:, :], c["quarter_in_page"]),
                                       (A["ln2_gT"][:, :], a["ln2_g"].rearrange("o (k p) -> p (o k)", p=P))]
                            tables += [(A[n][:, :], bc(c[n], A[n].shape[1])) for n in ("countdown", "cap_multiples", "expert_id")]
                            tables += [(table[8 * g:8 * g + 8, :], pages[g:g + 1, :].to_broadcast([8, DB])) for g in range(PAGES)]
                            casts = [(A["identity_b"][:, :], A["identity"][:, :], 1.0, 0.0), (A["causal_b"][:, :], A["causal"][:, :], 1.0, 0.0),
                                     (A["ones_b"][:, :], A["identity"][:, :], 0.0, 1.0), (A["above_b"][:, :], above[:, :], 1.0, 0.0),
                                     (A["own_rows"][:, :, :], own[:, :, :], 1.0, 0.0), (A["row_id"][:, :], table[:, :], 8.0, off[:, 0:1]),
                                     (gq[:, :], gq[:, :], HD ** -0.5, 0.0)]
                            casts += [(A["quarter_id"][:, j, :], table[:, :], 32.0, off_quarter[:, j:j + 1]) for j in range(4)]
                            norm_and_transpose(nc, "n1_", S["x_rows"], a["ln1_g"], A["identity"], A["uT"], None,
                                               tables, casts, weights(QR, W))
                        A["cos"], A["sin"] = cos, sin
                        project(nc, "pr_", [
                            dict(kind="rotary", col=QR, n=W, decay=dq, blocks=PAIRS, to=[(A["qpT"], 0, PAIRS)]),
                            dict(kind="rotary", col=KR, n=W, decay=dk, blocks=PAIRS, nat=A["kp"], to=[(A["kpT"], 0, PAIRS)]),
                            dict(kind="copy", col=VR, n=W, keep=A["vr"]),
                            dict(kind="silu", col=GR, n=W, keep=A["sg"])], S, A, w_first, (w_preloaded, 16))
                    retention(nc, S, A, weights(QI, N_QI))
                with ExitStack() as xt:
                    A["qiT"] = sb(xt, "qiT", [P, 2, TOK])
                    A["kiT2"] = sb(xt, "kiT", [P, 1, TOK])
                    A["kiT"] = A["kiT2"][:, 0, :]
                    A["wi"] = sb(xt, "wi", [P, TILES, IH])
                    project(nc, "pi_", [dict(kind="index", col=QI, n=N_QI, blocks=3, to=[(A["qiT"], 0, 2), (A["kiT2"], 2, 3)],
                                             out=i_rows, out_cols=slice(256, 320))], S, A, w_first, (w_preloaded, 32))
                    index_scores(nc, S, A, X)
                project(nc, "pa_", [
                    dict(kind="norm", col=QA, n=W, gain=gq, blocks=PAIRS, to=[(A["qaT"], 0, PAIRS)]),
                    dict(kind="norm", col=KA, n=W, gain=gk, blocks=PAIRS, to=[(A["kaT"], 0, PAIRS)], out=k_rows, out_cols=slice(0, W)),
                    dict(kind="copy", col=VA, n=W, keep=A["va"], out=v_rows)], S, A, X=X)
            mask = sb(early, "mask", [P, total], BF16)
            X["mask"] = lambda i: mask[:, at[i]:at[i] + (i + 1) * P]
            with ExitStack() as st:
                T["bias"] = sb(st, "bias", [P, H, SEQ])
                make_bias(nc, S, A, X, T)
                prompt_attention(nc, A, X, T)
            load_constants(nc, "l4_", [], [(A["qaT_s"][:, :, :], A["qaT"][:, :, SEQ:], 1.0, 0.0),
                                    (A["kaT_s"][:, :, :], A["kaT"][:, :, SEQ:], 1.0, 0.0),
                                    (A["va_s"][:, :], A["va"][:NS, NT, :], 1.0, 0.0)])
        sample_attention(nc, S, A, X)
        A["h_s"] = sb(top, "h_s", [NS, D])
        with ExitStack() as et:
            E = {n: sb(et, "e_" + n, [P, RING, k, n_out]) for n, k, n_out in (("wg", KD, DE), ("wu", KD, DE), ("wd", DE // P, D))}
            late = stage_semaphores(nc, et, "late_")
            E["w_loaded"] = [late(f"w_loaded{j}") for j in range(RING)]
            output_projection(nc, S, A, E)
            A["uT"] = A["mixT"]
            norm_and_transpose(nc, "n2_", lambda i: S["h"][cols_of(i), :], a["ln2_g"], A["identity"], A["uT"], S["xn"])
            route(nc, S, A, M)
            M["h"] = lambda i: (A["mixT"][:, :, :].rearrange("p k t -> p (k t)")[:, i * D:(i + 1) * D] if i < NT else A["h_s"][:, :])
            M["h_loaded"] = late("h_loaded")
            experts(nc, S, A, M, E)
        overflow_experts(nc, S, A, M)
        combine(nc, S, M)


def kernel(**inputs):
    import numpy as _np
    import concourse.bacc as _bacc
    from concourse import mybir as _mybir
    from concourse.bass_utils import run_bass_kernel_spmd as _run

    nc = _bacc.Bacc("TRN2", target_bir_lowering=False, num_devices=1)
    arrays, args, consts = {}, {}, {}
    for name in INPUTS:
        arrays[f"in_{name}"] = _np.ascontiguousarray(inputs[name])
    for name, table in shape_constants().items():
        arrays[f"const_{name}"] = _np.ascontiguousarray(table.astype(_np.float32))
    for name, array in arrays.items():
        ap = nc.dram_tensor(name, array.shape, _mybir.dt.from_np(array.dtype), kind="ExternalInput").ap()
        kind, key = name.split("_", 1)
        (args if kind == "in" else consts)[key] = ap
    outs = [nc.dram_tensor(f"out_{i}", shape, _mybir.dt.float32, kind="ExternalOutput").ap() for i, shape in enumerate(OUTPUTS)]
    build(nc, args, outs, consts)
    r = _run(nc, [arrays], core_ids=[0])
    return tuple(r.results[0][f"out_{i}"] for i in range(len(OUTPUTS)))
```
